# Optimizing a Trainium2 kernel written in Bass

```python
import jax
import jax.numpy as jnp
from jax import lax
import numpy as np
import math
import jax, jax.numpy as jnp

D_MODEL = 2048
BATCH = 1
SEQ = 256
DEPTH = 1

HEAD_DIM = 128
SB_HEADS = 8
DSA_HEADS = 8
IDX_HEADS = 16
IDX_DIM = 64
TOPK_MAX = 256
D_FF = 5632
CONV_WIDTH = 3
Q_BLOCK = 128
ROPE_THETA = 10000.0
NORM_EPS = 1e-6
N_MOD = 6
SB_WIDTH = SB_HEADS * HEAD_DIM
DSA_WIDTH = DSA_HEADS * HEAD_DIM
IDX_Q_WIDTH = IDX_HEADS * IDX_DIM
IN_SPLIT_SIZES = (SB_WIDTH, SB_WIDTH, SB_WIDTH, DSA_WIDTH, DSA_WIDTH, DSA_WIDTH,
                  IDX_Q_WIDTH, IDX_DIM, IDX_HEADS, D_MODEL, D_MODEL)
IN_WIDTH = 3 * SB_WIDTH + 3 * DSA_WIDTH + IDX_Q_WIDTH + IDX_DIM + IDX_HEADS + 2 * D_MODEL


def rmsnorm(x, g):
    xf = x.astype(jnp.float32)
    r = xf * lax.rsqrt(jnp.mean(xf * xf, axis=-1, keepdims=True) + NORM_EPS)
    return (r * g.astype(jnp.float32)).astype(x.dtype)

def rope(t, pos):
    d = t.shape[-1]
    inv_freq = 1.0 / (ROPE_THETA ** (jnp.arange(0, d, 2, dtype=jnp.float32) / d))
    ang = pos.astype(jnp.float32)[..., None] * inv_freq
    cos = jnp.cos(ang)[:, :, None, :]
    sin = jnp.sin(ang)[:, :, None, :]
    tf = t.astype(jnp.float32)
    t1, t2 = tf[..., : d // 2], tf[..., d // 2:]
    return jnp.concatenate([t1 * cos - t2 * sin, t2 * cos + t1 * sin], axis=-1).astype(t.dtype)

def stick_breaking_attention(q, k, v):
    B, S, H, dh = q.shape
    nb = S // Q_BLOCK
    scale = dh ** -0.5
    kpos = jnp.arange(S)
    qb = q.reshape(B, nb, Q_BLOCK, H, dh).transpose(1, 0, 2, 3, 4)

    def block(args):
        q_blk, start = args
        z = jnp.einsum('bqhd,bkhd->bhqk', q_blk, k,
                       preferred_element_type=jnp.float32) * scale
        qpos = start + jnp.arange(Q_BLOCK)
        past = (kpos[None, :] < qpos[:, None])[None, None]
        log1m = jnp.where(past, -jax.nn.softplus(z), 0.0)
        after = lax.cumsum(log1m, axis=3, reverse=True) - log1m
        w = jnp.where(past, jnp.exp(jax.nn.log_sigmoid(z) + after), 0.0)
        return jnp.einsum('bhqk,bkhd->bqhd', w.astype(v.dtype), v)

    starts = jnp.arange(nb, dtype=jnp.int32) * Q_BLOCK
    out = lax.map(block, (qb, starts))
    return out.transpose(1, 0, 2, 3, 4).reshape(B, S, H, dh)

def dsa_attention(q, k, v, qi, ki, wi):
    B, S, H, dh = q.shape
    nb = S // Q_BLOCK
    topk = min(TOPK_MAX, S // 4)
    kpos = jnp.arange(S)
    starts = jnp.arange(nb, dtype=jnp.int32) * Q_BLOCK

    def per_seq(args):
        q_s, k_s, v_s, qi_s, ki_s, wi_s = args
        q_blocks = q_s.reshape(nb, Q_BLOCK, H, dh)
        qi_blocks = qi_s.reshape(nb, Q_BLOCK, IDX_HEADS, IDX_DIM)
        wi_blocks = wi_s.reshape(nb, Q_BLOCK, IDX_HEADS)

        def block(bargs):
            q_b, qi_b, wi_b, start = bargs
            qpos = start + jnp.arange(Q_BLOCK)
            dots = jnp.einsum('qhi,ki->qhk', qi_b, ki_s,
                              preferred_element_type=jnp.float32) * (IDX_DIM ** -0.5)
            score = jnp.einsum('qh,qhk->qk', wi_b.astype(jnp.float32),
                               jax.nn.relu(dots)) * (IDX_HEADS ** -0.5)
            visible = kpos[None, :] <= qpos[:, None]
            score = jnp.where(visible, score, -jnp.inf)
            _, idx = lax.top_k(score, topk)
            k_sel = k_s[idx]
            v_sel = v_s[idx]
            logits = jnp.einsum('qhd,qkhd->qhk', q_b, k_sel,
                                preferred_element_type=jnp.float32) * (dh ** -0.5)
            valid = (idx <= qpos[:, None])[:, None, :]
            p = jax.nn.softmax(jnp.where(valid, logits, -jnp.inf), axis=-1)
            return jnp.einsum('qhk,qkhd->qhd', p.astype(v_s.dtype), v_sel)

        out = lax.map(block, (q_blocks, qi_blocks, wi_blocks, starts))
        return out.reshape(S, H, dh)

    return lax.map(per_seq, (q, k, v, qi, ki, wi))

def mixer(h, pos, w_in, w_a, w_b, w_o):
    B, S, _ = h.shape
    proj = h @ w_in
    offsets = [int(o) for o in np.cumsum(IN_SPLIT_SIZES)[:-1]]
    q_a, k_a, v_a, q_b, k_b, v_b, qi, ki, wi, g_a, g_b = jnp.split(proj, offsets, axis=-1)
    y_a = stick_breaking_attention(q_a.reshape(B, S, SB_HEADS, HEAD_DIM),
                                   k_a.reshape(B, S, SB_HEADS, HEAD_DIM),
                                   v_a.reshape(B, S, SB_HEADS, HEAD_DIM))
    y_a = y_a.reshape(B, S, SB_WIDTH) @ w_a
    y_b = dsa_attention(rope(q_b.reshape(B, S, DSA_HEADS, HEAD_DIM), pos),
                        rope(k_b.reshape(B, S, DSA_HEADS, HEAD_DIM), pos),
                        v_b.reshape(B, S, DSA_HEADS, HEAD_DIM),
                        rope(qi.reshape(B, S, IDX_HEADS, IDX_DIM), pos),
                        rope(ki[:, :, None, :], pos)[:, :, 0, :],
                        wi)
    y_b = y_b.reshape(B, S, DSA_WIDTH) @ w_b
    merged = jax.nn.sigmoid(g_a) * y_a + jax.nn.sigmoid(g_b) * y_b
    return merged @ w_o

def conv_ffn(h, w_up, conv_w, conv_b, w_down):
    u = h @ w_up
    S = u.shape[1]
    up = jnp.pad(u, ((0, 0), (CONV_WIDTH - 1, 0), (0, 0)))
    u = conv_b + sum(conv_w[i] * up[:, i:i + S] for i in range(CONV_WIDTH))
    a, b = jnp.split(u, 2, axis=-1)
    return (jax.nn.silu(a) * b) @ w_down

def first_inputs(seed: int = 0) -> dict:
    key = jax.random.key(seed)
    ks = jax.random.split(key, 16)
    f32 = jnp.float32

    def nrm(k, shape, scale):
        return jax.random.normal(k, shape, f32) * scale

    x = nrm(ks[0], (BATCH, SEQ, D_MODEL), 1.0)
    c = nrm(ks[1], (BATCH, D_MODEL), 1.0)
    offset = jax.random.randint(ks[2], (BATCH, 1), 0, 4096, dtype=jnp.int32)
    positions = offset + jnp.arange(SEQ, dtype=jnp.int32)[None, :]
    w_in = nrm(ks[3], (DEPTH, D_MODEL, IN_WIDTH), D_MODEL ** -0.5)
    w_a = nrm(ks[4], (DEPTH, SB_WIDTH, D_MODEL), SB_WIDTH ** -0.5)
    w_b = nrm(ks[5], (DEPTH, DSA_WIDTH, D_MODEL), DSA_WIDTH ** -0.5)
    w_o = nrm(ks[6], (DEPTH, D_MODEL, D_MODEL), D_MODEL ** -0.5)
    w_ada = nrm(ks[7], (DEPTH, D_MODEL, N_MOD * D_MODEL), 0.1 * D_MODEL ** -0.5)
    b_ada = nrm(ks[8], (DEPTH, N_MOD * D_MODEL), 0.01)
    g_mix = 1.0 + nrm(ks[9], (DEPTH, D_MODEL), 0.02)
    g_ffn = 1.0 + nrm(ks[10], (DEPTH, D_MODEL), 0.02)
    w_up = nrm(ks[11], (DEPTH, D_MODEL, 2 * D_FF), D_MODEL ** -0.5)
    conv_w = nrm(ks[12], (DEPTH, CONV_WIDTH, 2 * D_FF), CONV_WIDTH ** -0.5)
    conv_b = nrm(ks[13], (DEPTH, 2 * D_FF), 0.01)
    w_down = nrm(ks[14], (DEPTH, D_FF, D_MODEL), D_FF ** -0.5)
    g_final = 1.0 + nrm(ks[15], (D_MODEL,), 0.02)
    return {"x": x, "c": c, "positions": positions, "w_in": w_in, "w_a": w_a, "w_b": w_b,
            "w_o": w_o, "w_ada": w_ada, "b_ada": b_ada, "g_mix": g_mix, "g_ffn": g_ffn,
            "w_up": w_up, "conv_w": conv_w, "conv_b": conv_b, "w_down": w_down,
            "g_final": g_final}

def first_block(x, c, positions, w_in, w_a, w_b, w_o, w_ada, b_ada, g_mix, g_ffn,
              w_up, conv_w, conv_b, w_down, g_final):
    c_act = jax.nn.silu(c)
    for layer in range(DEPTH):
        mod = c_act @ w_ada[layer] + b_ada[layer]
        sh1, sc1, gt1, sh2, sc2, gt2 = jnp.split(mod[:, None, :], N_MOD, axis=-1)
        h = rmsnorm(x, g_mix[layer]) * (1 + sc1) + sh1
        x = x + (1 + gt1) * mixer(h, positions, w_in[layer], w_a[layer], w_b[layer], w_o[layer])
        h = rmsnorm(x, g_ffn[layer]) * (1 + sc2) + sh2
        x = x + (1 + gt2) * conv_ffn(h, w_up[layer], conv_w[layer], conv_b[layer], w_down[layer])
    return rmsnorm(x, g_final)


N_META = 16
CONV_W = D_MODEL // 2
N_CONV_GROUPS = 16
CONV_K = 3
RWKV_W = D_MODEL // 2
HEAD_N = 64
N_RWKV_HEADS = RWKV_W // HEAD_N
DECAY_LORA = 96
AAA_LORA = 96
GATE_LORA = 256
FFN_K = 3
RMS_EPS = 1e-6
GN_EPS = 64e-5
DECAY_SCALE = math.exp(-0.5)

CONV_COLS = 3 * CONV_W
RWKV_COLS = 3 * RWKV_W + DECAY_LORA + AAA_LORA + GATE_LORA
IN_COLS = CONV_COLS + RWKV_COLS


def rmsnorm_2(x, g):
    xf = x.astype(jnp.float32)
    y = xf * lax.rsqrt(jnp.mean(xf * xf, axis=-1, keepdims=True) + RMS_EPS)
    return (y * g.astype(jnp.float32)).astype(x.dtype)

def causal_dwconv(x, w):
    k = w.shape[0]
    seq_len = x.shape[1]
    xp = jnp.pad(x, ((0, 0), (k - 1, 0), (0, 0)))
    y = xp[:, 0:seq_len] * w[0]
    for i in range(1, k):
        y = y + xp[:, i:i + seq_len] * w[i]
    return y

def token_shift(z, mu):
    z_prev = jnp.pad(z, ((0, 0), (1, 0), (0, 0)))[:, :-1]
    return z + (z_prev - z) * mu

def rwkv7_scan(r, w, k, v, a_vec, b_vec):
    bsz, _, h, n = r.shape
    xs = tuple(jnp.swapaxes(t, 0, 1) for t in (r, w, k, v, a_vec, b_vec))

    def step(s, inp):
        r_t, w_t, k_t, v_t, a_t, b_t = inp
        sa = jnp.einsum('bhvk,bhk->bhv', s, a_t)
        s = s * w_t[:, :, None, :] + sa[..., None] * b_t[:, :, None, :] + v_t[..., None] * k_t[:, :, None, :]
        y_t = jnp.einsum('bhvk,bhk->bhv', s, r_t)
        return s, y_t

    s0 = jnp.zeros((bsz, h, n, n), jnp.float32)
    _, ys = lax.scan(step, s0, xs)
    return jnp.swapaxes(ys, 0, 1)

def short_conv_group(zc, conv_w):
    gate_b, gate_c, hx = jnp.split(zc, 3, axis=-1)
    return gate_b * causal_dwconv(gate_c * hx, conv_w)

def rwkv7_group(zr, mu_rwkv, w_decay_up, w0, a_up, a0, g_up, k_k, k_a, r_k, ln_x_w, ln_x_b):
    bsz, seq_len, _ = zr.shape
    zr = token_shift(zr, mu_rwkv)
    o1 = RWKV_W; o2 = 2 * RWKV_W; o3 = 3 * RWKV_W
    o4 = o3 + DECAY_LORA; o5 = o4 + AAA_LORA
    r = zr[..., :o1]
    k = zr[..., o1:o2]
    v = zr[..., o2:o3]
    wd = zr[..., o3:o4]
    ad = zr[..., o4:o5]
    gd = zr[..., o5:]

    f32 = jnp.float32
    log_w = -DECAY_SCALE * jax.nn.sigmoid((w0 + jnp.tanh(wd) @ w_decay_up).astype(f32))
    a = jax.nn.sigmoid(a0 + ad @ a_up)
    g = jax.nn.sigmoid(gd) @ g_up

    hs = (bsz, seq_len, N_RWKV_HEADS, HEAD_N)
    kk = (k * k_k).astype(f32).reshape(hs)
    kk = kk / jnp.maximum(jnp.sqrt(jnp.sum(kk * kk, axis=-1, keepdims=True)), 1e-12)
    k = k * (1.0 + (a - 1.0) * k_a)

    r_h = r.astype(f32).reshape(hs)
    k_h = k.astype(f32).reshape(hs)
    v_h = v.astype(f32).reshape(hs)
    a_h = a.astype(f32).reshape(hs)
    y = rwkv7_scan(r_h, jnp.exp(log_w).reshape(hs), k_h, v_h, -kk, kk * a_h)

    mean = jnp.mean(y, axis=-1, keepdims=True)
    var = jnp.mean(jnp.square(y - mean), axis=-1, keepdims=True)
    y = (y - mean) * lax.rsqrt(var + GN_EPS)
    y = y.reshape(bsz, seq_len, RWKV_W) * ln_x_w.astype(f32) + ln_x_b.astype(f32)
    bonus = jnp.sum(r_h * k_h * r_k.astype(f32), axis=-1, keepdims=True) * v_h
    y = y + bonus.reshape(bsz, seq_len, RWKV_W)
    return (y * g.astype(f32)).astype(zr.dtype)

def conv_glu(x, w_gate_up, conv_ffn, w_down):
    gu = x @ w_gate_up
    gate, up = jnp.split(gu, 2, axis=-1)
    gate = causal_dwconv(gate, conv_ffn)
    return (jax.nn.silu(gate) * up) @ w_down

def second_inputs(seed: int = 0) -> dict:
    key = jax.random.key(seed)
    ks = jax.random.split(key, 24)
    f32 = jnp.float32
    nrm = lambda k, shape, s: jax.random.normal(k, shape, f32) * s
    d = D_MODEL
    return {
        "x": nrm(ks[0], (BATCH, SEQ, d), 1.0),
        "meta_tokens": nrm(ks[1], (N_META, d), 1.0),
        "g_pre_mix": 1.0 + nrm(ks[2], (d,), 0.05),
        "w_in": nrm(ks[3], (d, IN_COLS), d ** -0.5),
        "conv_w": nrm(ks[4], (CONV_K, CONV_W), CONV_K ** -0.5),
        "mu_rwkv": jax.random.uniform(ks[5], (RWKV_COLS,), f32, 0.1, 0.9),
        "w_decay_up": nrm(ks[6], (DECAY_LORA, RWKV_W), 0.1 * DECAY_LORA ** -0.5),
        "w0": nrm(ks[7], (RWKV_W,), 0.5) - 0.5,
        "a_up": nrm(ks[8], (AAA_LORA, RWKV_W), 0.1 * AAA_LORA ** -0.5),
        "a0": nrm(ks[9], (RWKV_W,), 0.1),
        "g_up": nrm(ks[10], (GATE_LORA, RWKV_W), GATE_LORA ** -0.5),
        "k_k": 0.85 + nrm(ks[11], (RWKV_W,), 0.05),
        "k_a": 1.0 + nrm(ks[12], (RWKV_W,), 0.05),
        "r_k": nrm(ks[13], (N_RWKV_HEADS, HEAD_N), 0.1),
        "ln_x_w": 1.0 + nrm(ks[14], (RWKV_W,), 0.05),
        "ln_x_b": nrm(ks[15], (RWKV_W,), 0.02),
        "w_out": nrm(ks[16], (CONV_W + RWKV_W, d), (CONV_W + RWKV_W) ** -0.5),
        "g_post_mix": 1.0 + nrm(ks[17], (d,), 0.05),
        "g_pre_ffn": 1.0 + nrm(ks[18], (d,), 0.05),
        "w_gate_up": nrm(ks[19], (d, 2 * D_FF), d ** -0.5),
        "conv_ffn": nrm(ks[20], (FFN_K, D_FF), FFN_K ** -0.5),
        "w_down": nrm(ks[21], (D_FF, d), D_FF ** -0.5),
        "g_post_ffn": 1.0 + nrm(ks[22], (d,), 0.05),
    }

def second_block(x, meta_tokens, g_pre_mix, w_in, conv_w, mu_rwkv, w_decay_up, w0, a_up, a0,
              g_up, k_k, k_a, r_k, ln_x_w, ln_x_b, w_out, g_post_mix, g_pre_ffn,
              w_gate_up, conv_ffn, w_down, g_post_ffn):
    bsz = x.shape[0]
    meta = jnp.broadcast_to(meta_tokens.astype(x.dtype)[None], (bsz, N_META, x.shape[-1]))
    h = jnp.concatenate([meta, x], axis=1)

    for _ in range(DEPTH):
        n = rmsnorm_2(h, g_pre_mix)
        z = n @ w_in
        y_conv = short_conv_group(z[..., :CONV_COLS], conv_w)
        y_rwkv = rwkv7_group(z[..., CONV_COLS:], mu_rwkv, w_decay_up, w0, a_up, a0, g_up,
                             k_k, k_a, r_k, ln_x_w, ln_x_b)
        mix = jnp.concatenate([y_conv, y_rwkv], axis=-1) @ w_out
        h = h + rmsnorm_2(mix, g_post_mix)
        f = conv_glu(rmsnorm_2(h, g_pre_ffn), w_gate_up, conv_ffn, w_down)
        h = h + rmsnorm_2(f, g_post_ffn)

    return h[:, N_META:]


def setup_inputs(seed=0):
    out = dict(first_inputs(seed))
    for name, value in second_inputs(seed + 1).items():
        if name != "x":
            out[name + "_2"] = value
    return out


def reference(
    x, c, positions, w_in, w_a, w_b, w_o, w_ada, b_ada, g_mix, g_ffn, w_up, conv_w, conv_b,
    w_down, g_final, meta_tokens_2, g_pre_mix_2, w_in_2, conv_w_2, mu_rwkv_2, w_decay_up_2,
    w0_2, a_up_2, a0_2, g_up_2, k_k_2, k_a_2, r_k_2, ln_x_w_2, ln_x_b_2, w_out_2, g_post_mix_2,
    g_pre_ffn_2, w_gate_up_2, conv_ffn_2, w_down_2, g_post_ffn_2,
):
    x = first_block(
        x, c, positions, w_in, w_a, w_b, w_o, w_ada, b_ada, g_mix, g_ffn, w_up, conv_w, conv_b,
        w_down, g_final,
    )
    return second_block(
        x, meta_tokens_2, g_pre_mix_2, w_in_2, conv_w_2, mu_rwkv_2, w_decay_up_2, w0_2, a_up_2,
        a0_2, g_up_2, k_k_2, k_a_2, r_k_2, ln_x_w_2, ln_x_b_2, w_out_2, g_post_mix_2,
        g_pre_ffn_2, w_gate_up_2, conv_ffn_2, w_down_2, g_post_ffn_2,
    )


_drawn_inputs = setup_inputs


def setup_inputs(seed=0):
    import zlib

    import numpy as np

    out = dict(_drawn_inputs(seed))
    spreads = {}
    factors = {'conv_b': 4.674,
     'w_decay_up_2': 8.0,
     'a_up_2': 3.4,
     'k_k_2': 8.0,
     'ln_x_w_2': 2.995,
     'ln_x_b_2': 7.735}
    for name, (base, spread) in spreads.items():
        noise = np.random.default_rng([zlib.crc32(name.encode()), seed]).standard_normal(out[name].shape)
        drawn = base * np.exp(spread * noise) if base else spread * noise
        out[name] = jnp.asarray(drawn.astype(out[name].dtype))
    for name, factor in factors.items():
        out[name] = (out[name] * factor).astype(out[name].dtype)
    return out
```

```python
import math
from contextlib import ExitStack

import numpy as np

import concourse.bass as bass
from concourse import mybir

F32 = mybir.dt.float32
I32 = mybir.dt.int32
ACT = mybir.ActivationFunctionType
ALU = mybir.AluOpType
AX = mybir.AxisListType.X

P = 128
D = 2048
WORK = 22500
KD = D // P
T = 256
META = 16
NT = META + T
F = 5632
KF = F // P
HD = 128
IDX_HEADS = 16
IDX_D = 64
TOPK = 64
UNIT = 256
SLOT = KD * UNIT
NSLOT = 4
HALO = 2
EPS = 1e-6
GN_EPS = 64e-5
DECAY_SCALE = math.exp(-0.5)
NEG = -1e30
UNSEEN = -1e38
TAKEN = -3e38
BIG = 1e30

L = 68
NC = NT // L
MID = L // 2
RH = 16
RN = 64
W = 1024
KW = W // P
LORA = 96
SB_OFF = 0
DSA_OFF = 3 * W
QI_OFF = 6 * W
KI_OFF = 7 * W
WI_OFF = KI_OFF + IDX_D
GATE_OFF = WI_OFF + IDX_HEADS
RW_OFF = 3 * W
LORA_OFF = RW_OFF + 3 * W
GD_OFF = LORA_OFF + 2 * LORA

PARAMS = [("c", KD), ("b_ada", 6 * KD), ("g_mix", KD), ("g_ffn", KD), ("g_final", KD),
          ("conv_w", 3 * 2 * KF), ("conv_b", 2 * KF),
          ("g_pre_mix", KD), ("g_post_mix", KD), ("g_pre_ffn", KD), ("g_post_ffn", KD),
          ("conv_w2", 3 * KW), ("mu_rkv", 3 * KW), ("mu_gd", 2), ("mu_wd", 1), ("mu_ad", 1),
          ("w0", KW), ("a0", KW), ("k_k", KW), ("k_a", KW), ("r_k", KW), ("ln_w", KW), ("ln_b", KW),
          ("conv_ffn", 3 * KF)]
LEVELS = [2, 4, 8, 16, 32, 64]
CONSTS = [("ident", P), ("tri", P), ("heads", P), ("past", 384), ("seen", 384), ("invf", 2), ("sign", 2),
          ("strict", L), ("incl", L), ("first", L)] + [(f"level{b}", L) for b in LEVELS]

STREAM = [("ada", 12, {0: 1, 1: 1, 2: 1, 3: 1}), ("sb", 4, {0: 1, 1: 1, 2: 1}), ("ki", 1, {3: 3}),
          ("qi", 1, {0: 1, 1: 1, 2: 1, 3: 1}), ("dsa", 4, {0: 1, 1: 1, 2: 1}),
          ("merge", 8, {0: 1, 1: 1, 2: 1, 3: 1}), ("wo", 2, {0: 1, 1: 1, 2: 1, 3: 1}),
          ("up", 11, {0: 1, 1: 1, 2: 1, 3: 1}), ("down", 8, {0: 1, 1: 1, 2: 1, 3: 1}),
          ("conv2", 4, {0: 1, 1: 1, 2: 1}), ("rkv", 3, {0: 1, 1: 1, 2: 1, 3: 1}), ("lora", 1, {0: 1, 1: 1}),
          ("loraup", 1, {2: 2, 3: 1}),
          ("mix2", 2, {0: 1, 1: 1, 2: 1, 3: 1}), ("up2", 11, {0: 1, 1: 1, 2: 1, 3: 1}),
          ("down2", 8, {0: 1, 1: 1, 2: 1, 3: 1})]


def offsets(table):
    at, where = 0, {}
    for name, width in table:
        where[name] = (at, at + width)
        at += width
    return where, at


def landed_before():
    count, before = [0] * NSLOT, {}
    for name, iters, slots in STREAM:
        before[name] = list(count)
        for s, dmas in slots.items():
            count[s] += 16 * dmas * iters
    return before


def feature_major(w):
    return w.rearrange("(k p) n -> p k n", p=P)


def first(i):
    return isinstance(i, int) and i == 0


class Steps:

    def __init__(self, eng, sem):
        self.eng, self.sem, self.base, self.i, self.per, self.n = eng, sem, 0, 0, 0, 0

    def begin(self, i, per=None):
        if first(i) or (per is not None and self.per == 0):
            self.base, self.n = self.base + self.n, 0
        if first(i) and per is None:
            self.i, self.per = 0, 0
        else:
            self.i, self.per = i, self.n if per is None else per
        self.n = 0

    def end(self):
        assert self.per == 0 or self.n == self.per, (self.n, self.per)

    def leave(self, count):
        self.base, self.i, self.per, self.n = self.base + count * self.per, 0, 0, 0

    def mark(self, ins):
        self.n += 1
        ins.then_inc(self.sem, 1)

    def wait(self):
        self.eng.wait_ge(self.sem, self.base + self.i * self.per + self.n)

    def __call__(self, ins):
        self.mark(ins)
        self.wait()


def repeat(eng, count, body):
    body(0)
    if count > 1:
        with eng.Fori(1, count) as i:
            body(i)


def build(nc, A, out):
    before = landed_before()
    with ExitStack() as ctx:
        def sb(name, shape, dt=F32):
            return ctx.enter_context(nc.sbuf_tensor(name, shape, dt))

        def sem(name):
            return ctx.enter_context(nc.semaphore(name))

        bank = ctx.enter_context(nc.psum_tensor("bank", [P, 8, 512], F32))
        ring = sb("ring", [P, NSLOT, SLOT])
        res = sb("res", [P, KD, NT])
        hT = sb("hT", [P, KD, NT])
        pw, pwidth = offsets(PARAMS)
        cw, cwidth = offsets(CONSTS)
        params = sb("params", [P, pwidth])
        consts = sb("consts", [P, cwidth])
        ones = sb("ones", [P, P])
        cact = sb("cact", [P, KD])
        mod = sb("mod", [P, 6, KD])
        gain = sb("gain", [P, 2, KD])
        rms = sb("rms", [P, NT])
        sq = sb("sq", [P, 2, NT])
        epsc = sb("epsc", [P, 2])
        omu = sb("omu", [P, 28])
        omka = sb("omka", [P, KW])
        work = sb("work", [P, WORK])

        def param(name, a=None, b=None):
            lo, hi = pw[name]
            return params[:, lo:hi] if a is None else params[:, lo + a:lo + (a + 1 if b is None else b)]

        def pcol(name, i):
            lo, _ = pw[name]
            return params[:, bass.ds(i + lo, 1)] if not isinstance(i, int) else params[:, lo + i:lo + i + 1]

        def const(name):
            lo, hi = cw[name]
            return consts[:, lo:hi]

        def carve(*shapes):
            at, views = 0, []
            for shape in shapes:
                n = int(np.prod(shape))
                v = work[:, at:at + n]
                if len(shape) == 2:
                    v = v.rearrange("p (a b) -> p a b", a=shape[0])
                if len(shape) == 3:
                    v = v.rearrange("p (a b c) -> p a b c", a=shape[0], b=shape[1])
                views.append(v)
                at += n
            assert at <= WORK, at
            return views

        def tile(t, i):
            return t[:, i, :] if isinstance(i, int) else t[:, bass.ds(i, 1), :].rearrange("p a n -> p (a n)")

        def weights(slot, k, n):
            return ring[:, slot, 0:k * n].rearrange("p (k n) -> p k n", k=k)

        params_in, consts_in, pos_in = sem("params_in"), sem("consts_in"), sem("pos_in")
        x_loaded = sem("x_loaded")
        landed = [sem(f"landed{s}") for s in range(NSLOT)]
        phase_done = sem("phase_done")
        act_step, dve_step, pool_step = sem("act_step"), sem("dve_step"), sem("pool_step")
        ones_set = sem("ones_set")
        stored = sem("stored")
        squared, summed, rooted, normed, shifted = (sem(n) for n in ("squared", "summed", "rooted", "normed", "shifted"))
        z_done, s_done, o_done, zm_done, sp_done, l_done, d_done, w_done = (
            sem(n) for n in ("z_done", "s_done", "o_done", "zm_done", "sp_done", "l_done", "d_done", "w_done"))
        q_read, k_read, v_read, q2_read, k2_read, v2_read = (
            sem(n) for n in ("q_read", "k_read", "v_read", "q2_read", "k2_read", "v2_read"))
        angle_done, sines, dots_done, relu_done, relu_used = (
            sem(n) for n in ("angle_done", "sines", "dots_done", "relu_done", "relu_used"))
        logits_done, max_done, exp_done, probs_done, turned, turned_read, o2_done = (
            sem(n) for n in ("logits_done", "max_done", "exp_done", "probs_done", "turned", "turned_read", "o2_done"))
        merge_read = [sem(f"merge_read{s}") for s in range(4)]
        merged, tap_done, silu_done, acted = sem("merged"), sem("tap_done"), sem("silu_done"), sem("acted")
        halves = {n: sem(f"{n}_halves") for n in ("down", "down2")}
        cact_ready = sem("cact_ready")
        meta_loaded, result_ready = sem("meta_loaded"), sem("result_ready")
        c_copied, own_done, lora_ready, tap2_done, silu2_done = (
            sem(n) for n in ("c_copied", "own_done", "lora_ready", "tap2_done", "silu2_done"))
        kk_squared, kk_summed, kk_floored, kk_rooted = (sem(n) for n in ("kk_squared", "kk_summed", "kk_floored", "kk_rooted"))
        cum_done, exps_done, feat_done, n_raw, g0_done, t0_raw, t0_ready, nm_ready, w1_raw, w1_ready, tg_raw, tg_ready = (
            sem(n) for n in ("cum_done", "exps_done", "feat_done", "n_raw", "g0_done", "t0_raw", "t0_ready", "nm_ready",
                             "w1_raw", "w1_ready", "tg_raw", "tg_ready"))
        task_done, tok_read, mat_read, x_raw, x_ready, u_raw, u_ready, h_raw, h_ready, y_raw, pair_done = (
            sem(n) for n in ("task_done", "tok_read", "mat_read", "x_raw", "x_ready", "u_raw", "u_ready", "h_raw", "h_ready",
                             "y_raw", "pair_done"))
        mean_raw, centred, y_squared, var_raw, var_read, gate_tiles = (
            sem(n) for n in ("mean_raw", "centred", "y_squared", "var_raw", "var_read", "gate_tiles"))
        tiles = {n: sem(f"{n}_tiles") for n, _, _ in STREAM}
        evac = {n: sem(f"{n}_evac") for n, _, _ in STREAM}

        def arrived(pe, phase, slot, i):
            dmas = next(sl for n, _, sl in STREAM if n == phase)[slot]
            pe.wait_ge(landed[slot], before[phase][slot] + 16 * dmas + i * (16 * dmas))

        def products(out_ap, pairs, **kw):
            last = None
            for n, (a, b) in enumerate(pairs):
                last = nc.tensor.matmul(out_ap, a, b, start=n == 0, stop=n == len(pairs) - 1, **kw)
            return last

        ends = [0]

        (yaT, ybT, mergedT, qT, kT, vS, s_a, s_b, s_c, s_d, s_e, s_f, small, biasM, tabs128, tabs64) = carve(
            (8, T), (8, T), (KD, T), (2, T), (2, T), (2, T),
            (2, 384), (2, 384), (2, 384), (2, 384), (2, 384), (2, 384), (1, 64), (1, 384), (2, 2 * T), (2, T))
        ropeA = mergedT[:, 0:2, :].rearrange("p a t -> p (a t)")
        ropeB = mergedT[:, 2:4, :].rearrange("p a t -> p (a t)")
        angles = mergedT[:, 4:8, :]
        turns = mergedT[:, 8:12, :]
        qiT = mergedT[:, 4:12, :]
        kiT = mergedT[:, 12, :]
        relu = mergedT[:, 13:16, :].rearrange("p a t -> p (a t)")
        posf = mergedT[:, 12, :]
        posi = mergedT[:, 13, :].bitcast(I32)
        small = small[:, 0, :]
        past, seen = const("past"), const("seen")
        gates_at = 3 * 8 * T + 3 * 2 * T + 8 * T
        gates = work[:, gates_at:gates_at + 4 * T].rearrange("p (a t) -> p a t", a=4)
        gated = work[:, gates_at + 4 * T:gates_at + 8 * T].rearrange("p (a t) -> p a t", a=4)
        actT, cv, sa, fT = carve((KF, T), (8, NT), (4, T), (KD, NT))
        (yconv, zr, lw, aa, kk, gd, TT, G, NM, N, W1, lak, lrk, lrb, tokK, tokB, tokV, XU) = carve(
            (KW, NT), (3 * KW, NT), (KW, NT), (KW, NT), (KW, NT), (2, NT), (2, NT), (2, NT), (2, 2 * NT), (2, NT), (2, NT),
            (2, NT), (2, NT), (2, NT), (NC, P), (NC, P), (NC, P), (2, P))
        Xs, Us = XU[:, 0, :], XU[:, 1, :]
        cs, chs, ycs = carve((KW, NT), (3 * KW, NT), (2, NT), (2, NT + HALO), (2, NT))[2:]
        temp8, temp8b, wdad = carve((KW, NT), (3 * KW, NT), (KW, NT), (KW, NT), (KW, NT), (2, NT), (KW, NT), (KW, NT),
                                    (2, NT))[6:]
        cum, cumc, cpm, Ep, Em, Epm, k2, bb, kt, bt, rkr, vt = (hT[:, k, :] for k in range(12))
        hflat = hT[:].rearrange("p k t -> p (k t)")
        AR = hflat[:, 12 * NT:14 * NT].rearrange("p (c a t) -> p c a t", c=NC, a=2)
        Hs = hflat[:, 14 * NT:14 * NT + 2 * RN].rearrange("p (a v) -> p a v", a=2)
        Hsum = hflat[:, 14 * NT + 2 * RN:14 * NT + 3 * RN]
        ecm = hflat[:, 14 * NT + 3 * RN:14 * NT + 3 * RN + NC]
        mids = hflat[:, 14 * NT + 3 * RN + 8:14 * NT + 3 * RN + 8 + NC]
        onesrow = ones[:, 0:L]

        def all8(x):
            return x.rearrange("p a t -> p (a t)")
        SCALE = HD ** -0.5

        block = ctx.enter_context(nc.Block())

        def phase_end(eng, n):
            eng.drain().then_inc(phase_done, 1)
            eng.wait_ge(phase_done, 3 * n)

        @block.sync
        def _(sp):
            sp.dma_start(params[:], A["params"]).then_inc(params_in, 16)
            sp.dma_start(consts[:], A["consts"]).then_inc(consts_in, 16)
            sp.dma_start(res[:, :, META:NT], A["xT"]).then_inc(x_loaded, 16)
            sp.dma_start(posi, A["pos"]).then_inc(pos_in, 16)
            free = [None] * NSLOT

            def load(slot, dst, src):
                sp.dma_start(dst, src).then_inc(landed[slot], 16)

            def phase(name, units, done):
                _, count, slots = next(p for p in STREAM if p[0] == name)

                def body(i):
                    for s in slots:
                        if first(i):
                            if free[s] is not None:
                                sp.wait_ge(*free[s])
                        else:
                            sm, at, per = done(s)
                            sp.wait_ge(sm, i * per + (at - per))
                        for dst, src in units(s, i):
                            load(s, dst, src)
                repeat(sp, count, body)
                for s in slots:
                    sm, at, per = done(s)
                    free[s] = (sm, at + (count - 1) * per)

            def columns(w, k, col):
                return feature_major(w)[:, :, col:col + UNIT] if isinstance(col, int) else \
                    feature_major(w)[:, :, bass.ds(col, UNIT)]

            def units_of(w, col0, step):
                k = w.shape[0] // P
                return lambda s, i: [(weights(s, k, UNIT), columns(w, k, col0(s) + i * step))]

            def pairs_done(name, n=8):
                return lambda s: (tiles[name], 2 * (s + 1), n)

            phase("ada", units_of(A["w_ada"], lambda s: s * UNIT, NSLOT * UNIT), lambda s: (tiles["ada"], s + 1, NSLOT))
            phase("sb", units_of(A["w_in"], lambda s: SB_OFF + s * W, UNIT), lambda s: (tiles["sb"], s + 1, 3))
            w144 = ring[:, 3, 0:KD * 144].rearrange("p (k n) -> p k n", k=KD)
            wv = feature_major(A["w_in"])
            phase("ki", lambda s, i: [(w144[:, :, 0:64], wv[:, :, KI_OFF:KI_OFF + IDX_D]),
                                      (w144[:, :, 64:128], wv[:, :, KI_OFF:KI_OFF + IDX_D]),
                                      (w144[:, :, 128:144], wv[:, :, WI_OFF:WI_OFF + IDX_HEADS])],
                  lambda s: (tiles["ki"], 2, 2))
            phase("qi", units_of(A["w_in"], lambda s: QI_OFF + s * UNIT, 0), pairs_done("qi"))
            phase("dsa", units_of(A["w_in"], lambda s: DSA_OFF + s * W, UNIT), lambda s: (tiles["dsa"], s + 1, 3))

            def merge_units(s, i):
                col = i * UNIT
                if s < 2:
                    return [(weights(s, KW, UNIT), columns(A["w_a"] if s == 0 else A["w_b"], KW, col))]
                return [(weights(s, KD, UNIT), columns(A["w_in"], KD, col + (GATE_OFF + (s - 2) * D)))]
            phase("merge", merge_units, pairs_done("merge"))
            phase("wo", units_of(A["w_o"], lambda s: s * UNIT, NSLOT * UNIT), pairs_done("wo"))

            def up_units(w):
                return units_of(w, lambda s: (s % 2) * F + (s // 2) * UNIT, 2 * UNIT)

            def down_units(w):
                kq = KF // NSLOT

                def units(s, i):
                    v = feature_major(w)[:, s * kq:(s + 1) * kq, :]
                    v = v[:, :, 0:UNIT] if isinstance(i, int) else v[:, :, bass.ds(i * UNIT, UNIT)]
                    return [(weights(s, kq, UNIT), v)]
                return units
            phase("up", up_units(A["w_up"]), pairs_done("up"))

            def down_done(name):
                return lambda s: (tiles[name], s + 1, NSLOT - 1) if s < NSLOT - 1 else (halves[name], 2, 2)
            phase("down", down_units(A["w_down"]), down_done("down"))
            sp.wait_ge(phase_done, 3 * 11)
            sp.dma_start(res[:, :, 0:META], A["metaT"]).then_inc(meta_loaded, 16)
            phase("conv2", units_of(A["w_in_2"], lambda s: s * W, UNIT), lambda s: (tiles["conv2"], 2 * (s + 1), 6))
            phase("rkv", units_of(A["w_in_2"], lambda s: RW_OFF + s * UNIT, W), pairs_done("rkv"))
            w192 = ring[:, 1, 0:KD * 192].rearrange("p (k n) -> p k n", k=KD)
            phase("lora", lambda s, i: [(weights(0, KD, UNIT), columns(A["w_in_2"], KD, GD_OFF))] if s == 0 else
                  [(w192, feature_major(A["w_in_2"])[:, :, LORA_OFF:LORA_OFF + 2 * LORA])],
                  lambda s: (tiles["lora"], 2 * (s + 1), 4))
            phase("loraup", lambda s, i: [(ring[0:LORA, 2, 0:W], A["w_decay_up_2"]), (ring[0:LORA, 2, W:2 * W], A["a_up_2"])]
                  if s == 2 else [(ring[:, 3, 0:2 * W].rearrange("p (k n) -> p k n", k=2), feature_major(A["g_up_2"]))],
                  lambda s: (tiles["loraup"], 2 * KW, 2 * KW) if s == 2 else (gate_tiles, KW, KW))
            phase("mix2", units_of(A["w_out_2"], lambda s: s * UNIT, NSLOT * UNIT), pairs_done("mix2"))
            phase("up2", up_units(A["w_gate_up_2"]), pairs_done("up2"))
            phase("down2", down_units(A["w_down_2"]), down_done("down2"))
            sp.wait_ge(result_ready, 1)
            sp.dma_start(out, res[:, :, META:NT]).then_inc(stored, 16)
            sp.wait_ge(stored, 16)

        norms = {"act": 0, "pe": 0, "dve": 0}

        def norm_act(act, src, n, step):
            m = norms["act"]
            norms["act"] += 1
            for k in range(KD):
                if k >= 2 or m:
                    act.wait_ge(summed, KD * m + k - 1)
                nc.scalar.activation(sq[:, k % 2, 0:n], src[:, k, :], ACT.Square).then_inc(squared, 1)
            act.wait_ge(summed, KD * (m + 1))
            nc.scalar.activation(rms[:, 0:n], bank[:, 0, 0:n], ACT.Sqrt, scale=1.0 / D, bias=epsc[:, 0:1]).then_inc(rooted, 1)

        def norm_pe(pe, n):
            m = norms["pe"]
            norms["pe"] += 1
            for k in range(KD):
                pe.wait_ge(squared, KD * m + k + 1)
                nc.tensor.matmul(bank[:, 0, 0:n], ones[:], sq[:, k % 2, 0:n], start=k == 0, stop=k == KD - 1)\
                    .then_inc(summed, 1)

        def norm_dve(dve, n, step, apply):
            m = norms["dve"]
            norms["dve"] += 1
            dve.wait_ge(rooted, m + 1)
            step(nc.vector.reciprocal(rms[:, 0:n], rms[:, 0:n]))
            for k in range(KD):
                last = apply(k)
            step(last)

        def scaled(dst, src, g, n):
            return lambda k: nc.vector.scalar_tensor_tensor(
                dst[:, k, :], src[:, k, :], g[:, k:k + 1], rms[:, 0:n], ALU.mult, ALU.mult)

        def scaled_shifted(dst, src, g, shift, n, step):
            def apply(k):
                step(nc.vector.scalar_tensor_tensor(dst[:, k, :], src[:, k, :], g[:, k:k + 1], rms[:, 0:n], ALU.mult, ALU.mult))
                return nc.vector.tensor_scalar(dst[:, k, :], dst[:, k, :], shift[:, k:k + 1], None, ALU.add)
            return apply

        x1 = res[:, :, META:NT]
        h1 = hT[:, :, 0:T]

        @block.tensor
        def _(pe):
            pe.wait_ge(cact_ready, 1)

            def ada(i):
                for s in range(NSLOT):
                    arrived(pe, "ada", s, i)
                    w = weights(s, KD, UNIT)
                    for t in range(2):
                        col = 2 * s + t + i * 2 * NSLOT
                        dst = bank[:, 0, col:col + 1] if isinstance(i, int) else bank[:, 0, bass.ds(col, 1)]
                        last = products(dst, [(w[:, k, t * P:(t + 1) * P], cact[:, k:k + 1]) for k in range(KD)])
                    last.then_inc(tiles["ada"], 1)
            repeat(pe, 12, ada)
            phase_end(pe, 1)
            pe.wait_ge(ones_set, 1)
            pe.wait_ge(consts_in, 16)
            norm_pe(pe, T)
            phase_end(pe, 2)

            def project(phase, slot, i, token_major, dst):
                arrived(pe, phase, slot, i)
                w = weights(slot, KD, UNIT)
                for t in range(2):
                    if token_major:
                        pairs = [(h1[:, k, t * P:(t + 1) * P], w[:, k, :]) for k in range(KD)]
                    else:
                        pairs = [(w[:, k, t * P:(t + 1) * P], h1[:, k, :]) for k in range(KD)]
                    last = products(bank[:, dst, t * T:(t + 1) * T], pairs)
                last.then_inc(tiles[phase], 1)

            def attend_values(e, probs):
                o = bank[:, 3, e * T:(e + 1) * T]
                nc.tensor.matmul(o, vS[:, 0, e * HD:(e + 1) * HD], probs[:, e, 0:T], start=True, stop=False)
                return nc.tensor.matmul(o[:, P:T], vS[:, 1, e * HD:(e + 1) * HD], probs[:, e, T:384], start=False, stop=True)

            def sb(i, head=True, tail=True):
                if head:
                    if not first(i):
                        pe.wait_ge(q_read, i)
                    project("sb", 0, i, False, 0)
                if tail:
                    pe.wait_ge(q_read, i)
                    pe.wait_ge(k_read, i)
                    for e in range(2):
                        z = bank[:, 4 + e, :]
                        nc.tensor.matmul(z[:, 0:T], kT[:, e, 0:P], qT[:, e, :], start=True, stop=True)
                        nc.tensor.matmul(z[:, T:384], kT[:, e, P:T], qT[:, e, P:T], start=True, stop=True)\
                            .then_inc(z_done, 1)
                if head:
                    project("sb", 1, i, False, 1)
                if tail:
                    for e in range(2):
                        pe.wait_ge(sp_done, i * 2 + (e - 1))
                        sp_ = s_e[:, e, :]
                        nc.tensor.matmul(bank[:, 6 + e, 0:T], const("tri"), sp_[:, 0:T], start=True, stop=False)
                        nc.tensor.matmul(bank[:, 6 + e, P:T], ones[:], sp_[:, T:384], start=False, stop=True)
                        nc.tensor.matmul(bank[:, 6 + e, T:384], const("tri"), sp_[:, T:384], start=True, stop=True)\
                            .then_inc(s_done, 1)
                if head:
                    if not first(i):
                        pe.wait_ge(v_read, i)
                    project("sb", 2, i, True, 2)
                if tail:
                    pe.wait_ge(v_read, i)
                    for e in range(2):
                        pe.wait_ge(w_done, i * 2 + (e - 1))
                        attend_values(e, s_f).then_inc(o_done, 1)

            def overlapped(body, count):
                body(0, tail=False)
                with pe.Fori(1, count) as i:
                    body(i)
                body(count, head=False)
            overlapped(sb, 4)
            phase_end(pe, 3)

            arrived(pe, "ki", 3, 0)
            w144 = ring[:, 3, 0:KD * 144].rearrange("p (k n) -> p k n", k=KD)
            products(bank[:, 6, 0:T], [(w144[:, k, 0:P], h1[:, k, :]) for k in range(KD)]).then_inc(tiles["ki"], 1)
            for t in range(2):
                last = products(bank[:, 7, t * IDX_HEADS:(t + 1) * IDX_HEADS],
                                [(h1[:, k, t * P:(t + 1) * P], w144[:, k, P:144]) for k in range(KD)])
            last.then_inc(tiles["ki"], 1)
            for s in range(NSLOT):
                arrived(pe, "qi", s, 0)
                w = weights(s, KD, UNIT)
                for t in range(2):
                    q = 2 * s + t
                    if q == 6:
                        pe.wait_ge(evac["ki"], 2)
                    products(bank[:, q, 0:T], [(w[:, k, t * P:(t + 1) * P], h1[:, k, :]) for k in range(KD)])\
                        .then_inc(tiles["qi"], 1)
            for h in range(IDX_HEADS):
                j, e = h // 2, 64 * (h % 2)
                if h < 8:
                    pe.wait_ge(evac["qi"], 8)
                    pe.wait_ge(evac["ki"], 2)
                else:
                    pe.wait_ge(relu_done, h - 7)
                d = bank[:, h % 8, :]
                nc.tensor.matmul(d[:, 0:P], qiT[e:e + 64, j, 0:P], kiT[e:e + 64, 0:P], start=True, stop=True)
                nc.tensor.matmul(d[:, P:384], qiT[e:e + 64, j, P:T], kiT[e:e + 64, :], start=True, stop=True)\
                    .then_inc(dots_done, 1)
            phase_end(pe, 4)

            def dsa(i, head=True, tail=True):
                if head:
                    if not first(i):
                        pe.wait_ge(q2_read, i)
                    project("dsa", 0, i, False, 0)
                if tail:
                    pe.wait_ge(q2_read, i)
                    pe.wait_ge(k2_read, i)
                    for e in range(2):
                        z = bank[:, 4 + e, :]
                        nc.tensor.matmul(z[:, 0:P], qT[:, e, 0:P], kT[:, e, 0:P], start=True, stop=True)
                        nc.tensor.matmul(z[:, P:384], qT[:, e, P:T], kT[:, e, :], start=True, stop=True)\
                            .then_inc(logits_done, 1)
                if head:
                    project("dsa", 1, i, False, 1)
                if tail:
                    for e in range(2):
                        pe.wait_ge(probs_done, i * 2 + (e - 1))
                        for n in range(3):
                            last = nc.tensor.transpose(bank[:, 6 + e, n * P:(n + 1) * P], s_c[:, e, n * P:(n + 1) * P],
                                                       const("ident"))
                        last.then_inc(turned, 1)
                if head:
                    if not first(i):
                        pe.wait_ge(v2_read, i)
                    project("dsa", 2, i, True, 2)
                if tail:
                    pe.wait_ge(v2_read, i)
                    for e in range(2):
                        pe.wait_ge(turned_read, i * 2 + (e - 1))
                        attend_values(e, s_f).then_inc(o2_done, 1)
            overlapped(dsa, 4)
            phase_end(pe, 5)

            def merge(i):
                for s in range(NSLOT):
                    arrived(pe, "merge", s, i)
                    k_tiles, src = (KW, yaT if s == 0 else ybT) if s < 2 else (KD, h1)
                    w = weights(s, k_tiles, UNIT)
                    for t in range(2):
                        if not first(i):
                            pe.wait_ge(merge_read[s], i * 2 + (t - 1))
                        products(bank[:, 2 * s + t, 0:T],
                                 [(w[:, k, t * P:(t + 1) * P], src[:, k, :]) for k in range(k_tiles)])\
                            .then_inc(tiles["merge"], 1)
            repeat(pe, 8, merge)
            phase_end(pe, 6)

            def linear(phase, count, src, per=NSLOT, free=None):
                def body(i):
                    for s in range(per):
                        arrived(pe, phase, s, i)
                        w = weights(s, KD, UNIT)
                        for t in range(2):
                            q = 2 * s + t
                            if not first(i):
                                if free:
                                    free(i, q)
                                else:
                                    pe.wait_ge(evac[phase], i * 2 * per + (q + 1 - 2 * per))
                            rhs, width = src(s)
                            products(bank[:, q, 0:width], [(w[:, k, t * P:(t + 1) * P], rhs[:, k, :]) for k in range(KD)])\
                                .then_inc(tiles[phase], 1)
                repeat(pe, count, body)

            def down(phase):
                kq = KF // NSLOT

                def body(i):
                    for s in range(NSLOT):
                        arrived(pe, phase, s, i)
                        w = weights(s, kq, UNIT)
                        for t in range(2):
                            if s == 0 and not isinstance(i, int):
                                pe.wait_ge(evac[phase], i * 2 + (t - 1))
                            for k in range(kq):
                                last = nc.tensor.matmul(bank[:, t, 0:T], w[:, k, t * P:(t + 1) * P], actT[:, s * kq + k, :],
                                                        start=s == 0 and k == 0, stop=s == NSLOT - 1 and k == kq - 1)
                            if s == NSLOT - 1:
                                last.then_inc(halves[phase], 1)
                            elif t == 1:
                                last.then_inc(tiles[phase], 1)
                repeat(pe, 8, body)

            linear("wo", 2, lambda s: (mergedT, T))
            phase_end(pe, 7)
            norm_pe(pe, T)
            phase_end(pe, 8)
            linear("up", 11, lambda s: (h1, T))
            phase_end(pe, 9)
            down("down")
            phase_end(pe, 10)
            norm_pe(pe, T)
            phase_end(pe, 11)

            norm_pe(pe, NT)
            phase_end(pe, 12)
            linear("conv2", 4, lambda s: (hT, NT), per=3, free=lambda i, q: pe.wait_ge(evac["conv2"], i * 2 + (q % 2 - 1)))
            phase_end(pe, 13)
            linear("rkv", 3, lambda s: (hT, NT))
            phase_end(pe, 14)
            arrived(pe, "lora", 0, 0)
            w = weights(0, KD, UNIT)
            for t in range(2):
                products(bank[:, t, 0:NT], [(w[:, k, t * P:(t + 1) * P], hT[:, k, :]) for k in range(KD)]).then_inc(tiles["lora"], 1)
            arrived(pe, "lora", 1, 0)
            w192 = ring[:, 1, 0:KD * 192].rearrange("p (k n) -> p k n", k=KD)
            for t in range(2):
                products(bank[0:LORA, 2 + t, 0:NT], [(w192[:, k, t * LORA:(t + 1) * LORA], hT[:, k, :]) for k in range(KD)])\
                    .then_inc(tiles["lora"], 1)
            arrived(pe, "loraup", 2, 0)
            pe.wait_ge(lora_ready, 2)
            for u in range(2):
                for j in range(KW):
                    if u == 0:
                        if j == 0:
                            pe.wait_ge(evac["lora"], 4)
                    else:
                        pe.wait_ge(evac["loraup"], j + 1)
                    nc.tensor.matmul(bank[:, j, 0:NT], ring[0:LORA, 2, u * W + j * P:u * W + (j + 1) * P],
                                     wdad[0:LORA, u, :], start=True, stop=True).then_inc(tiles["loraup"], 1)
            for j in range(KW):
                pe.wait_ge(kk_squared, 1)
                pe.wait_ge(evac["loraup"], KW + j + 1)
                nc.tensor.matmul(bank[:, j, 0:NT], const("heads"), temp8[:, j, :], start=True, stop=True).then_inc(kk_summed, 1)
            phase_end(pe, 15)

            def chunk(x, c):
                return x[:, c * L:(c + 1) * L]

            def recur(i):
                rows = [slice(0, RN), slice(RN, P)]

                def task(n):
                    b = 6 + n % 2
                    if n in (2, 3, 4):
                        pe.wait_ge(tok_read, i * 3 + (n - 1))
                    if n > 4:
                        pe.wait_ge(mat_read, i * 7 + (n - 4))
                    if n < 3:
                        src = (kt, bt, vt)[n]
                        for c in range(NC):
                            last = nc.tensor.transpose(bank[0:L, b, c * P:(c + 1) * P], chunk(src, c), const("ident"))
                    elif n < 9:
                        kind, e = (n - 3) // 2, (n - 3) % 2
                        lhs, which = ((kt, 0), (kt, 1), (bt, 1))[kind]
                        for c in range(NC):
                            last = nc.tensor.matmul(bank[0:L, b, c * L:(c + 1) * L], chunk(lhs, c)[rows[e], :],
                                                    AR[rows[e], c, which, :], start=True, stop=True)
                    else:
                        last = nc.tensor.matmul(bank[:, b, 0:NT], const("heads"), rkr, start=True, stop=True)
                    last.then_inc(task_done, 1)

                pe.wait_ge(feat_done, i + 1)
                for e in range(2):
                    for c in range(NC):
                        last = nc.tensor.matmul(bank[0:L, e, c * L:(c + 1) * L], chunk(bt, c)[rows[e], :],
                                                AR[rows[e], c, 0, :], start=True, stop=True)
                    last.then_inc(n_raw, 1)
                for e in range(2):
                    pe.wait_ge(g0_done, i * 2 + (e + 1))
                    for c in range(NC):
                        last = nc.tensor.transpose(bank[0:L, 2 + e, c * L:(c + 1) * L], G[0:L, e, c * L:(c + 1) * L],
                                                   const("ident")[0:L, 0:L])
                    last.then_inc(t0_raw, 1)
                nl = len(LEVELS)
                for l in range(nl):
                    for e in range(2):
                        pe.wait_ge(nm_ready, i * 2 * nl + (2 * l + e + 1))
                        if l == 0:
                            pe.wait_ge(t0_ready, i * 2 + (e + 1))
                        else:
                            pe.wait_ge(tg_ready, i * 2 * nl + (2 * (l - 1) + e + 1))
                        for c in range(NC):
                            cc = slice(c * L, (c + 1) * L)
                            last = nc.tensor.matmul(bank[0:L, e, cc], NM[0:L, l % 2, e * NT + c * L:e * NT + (c + 1) * L],
                                                    TT[0:L, e, cc], start=True, stop=True)
                        last.then_inc(w1_raw, 1)
                        if 2 * l + e < 10:
                            task(2 * l + e)
                    for e in range(2):
                        pe.wait_ge(w1_ready, i * 2 * nl + (2 * l + e + 1))
                        for c in range(NC):
                            cc = slice(c * L, (c + 1) * L)
                            if l < nl - 1:
                                nc.tensor.matmul(bank[0:L, 2 + e, cc], G[0:L, e, cc], W1[0:L, e, cc], start=True, stop=True)
                        for c in range(NC):
                            cc = slice(c * L, (c + 1) * L)
                            last = nc.tensor.matmul(bank[0:L, 4 + e, cc], W1[0:L, e, cc], G[0:L, e, cc], start=True, stop=True)
                        last.then_inc(tg_raw, 1)
                pe.wait_ge(tg_ready, i * 2 * nl + 2 * nl)
                pe.wait_ge(mat_read, i * 7 + 7)
                for c in range(NC):
                    cc = slice(c * L, (c + 1) * L)
                    H = Hs[:, c % 2, :]
                    for e in range(2):
                        v = tokV[0:L, c, e * RN:(e + 1) * RN]
                        last = nc.tensor.matmul(bank[0:L, e, 0:RN], lak[0:L, e, cc], v, start=True, stop=c == 0)
                        if c:
                            if e == 0:
                                pe.wait_ge(h_ready, i * 3 + c)
                            last = nc.tensor.matmul(bank[0:L, e, 0:RN], AR[rows[e], c, 0, :], H[rows[e], :],
                                                    start=False, stop=True)
                    last.then_inc(x_raw, 1)
                    pe.wait_ge(x_ready, i * NC + (c + 1))
                    for e in range(2):
                        last = nc.tensor.matmul(bank[0:L, 2, e * RN:(e + 1) * RN], G[0:L, e, cc], Xs[0:L, e * RN:(e + 1) * RN],
                                                start=True, stop=True)
                    last.then_inc(u_raw, 1)
                    pe.wait_ge(u_ready, i * NC + (c + 1))
                    if c < NC - 1:
                        for e in range(2):
                            ee = slice(e * RN, (e + 1) * RN)
                            nc.tensor.matmul(bank[rows[e], 3, 0:RN], tokK[0:L, c, ee], tokV[0:L, c, ee], start=True, stop=False)
                            last = nc.tensor.matmul(bank[rows[e], 3, 0:RN], tokB[0:L, c, ee], Us[0:L, ee], start=False, stop=True)
                        last.then_inc(h_raw, 1)
                    for e in range(2):
                        ee = slice(e * RN, (e + 1) * RN)
                        nc.tensor.matmul(bank[rows[e], 4 + e, cc], tokV[0:L, c, ee], lrk[0:L, e, cc], start=True, stop=False)
                        if c:
                            nc.tensor.matmul(bank[rows[e], 4 + e, cc], H[rows[e], :], AR[rows[e], c, 1, :], start=False, stop=False)
                        last = nc.tensor.matmul(bank[rows[e], 4 + e, cc], Us[0:L, ee], lrb[0:L, e, cc], start=False, stop=True)
                last.then_inc(y_raw, 1)
            repeat(pe, KW, recur)
            phase_end(pe, 16)

            for j in range(KW):
                nc.tensor.matmul(bank[:, j, 0:NT], const("heads"), zr[:, j, :], start=True, stop=True).then_inc(mean_raw, 1)
            for j in range(KW):
                pe.wait_ge(y_squared, j + 1)
                nc.tensor.matmul(bank[:, j, 0:NT], const("heads"), kk[:, j, :], start=True, stop=True).then_inc(var_raw, 1)
            arrived(pe, "loraup", 3, 0)
            gup = ring[:, 3, 0:2 * W].rearrange("p (k n) -> p k n", k=2)
            for j in range(KW):
                pe.wait_ge(var_read, j + 1)
                products(bank[:, j, 0:NT], [(gup[:, k, j * P:(j + 1) * P], gd[:, k, :]) for k in range(2)]).then_inc(gate_tiles, 1)
            phase_end(pe, 17)

            class Mixed:
                def __getitem__(self, at):
                    k = at[1]
                    return yconv[:, k, :] if k < KW else zr[:, k - KW, :]
            linear("mix2", 2, lambda s: (Mixed(), NT))
            phase_end(pe, 18)
            norm_pe(pe, NT)
            phase_end(pe, 19)
            norm_pe(pe, NT)
            phase_end(pe, 20)
            linear("up2", 11, lambda s: (hT[:, :, META - HALO:NT], T + HALO) if s % 2 == 0 else (hT[:, :, META:NT], T))
            phase_end(pe, 21)
            down("down2")
            phase_end(pe, 22)
            norm_pe(pe, T)
            phase_end(pe, 23)

        @block.scalar
        def _(act):
            step = Steps(act, act_step)
            act.wait_ge(params_in, 16)
            nc.scalar.activation(cact[:], param("c"), ACT.Silu).then_inc(cact_ready, 1)
            phase_end(act, 1)
            act.wait_ge(ones_set, 1)
            act.wait_ge(x_loaded, 16)
            norm_act(act, x1, T, step)
            for n in range(4):
                act.wait_ge(angle_done, n + 1)
                dst = (tabs128[:, n % 2, 0:T], tabs64[:, n % 2, :])[n // 2]
                nc.scalar.activation(dst, turns[:, n, :], ACT.Sin).then_inc(sines, 1)
            phase_end(act, 2)

            def overlapped(body, count, per):
                body(0, tail=False)
                with act.Fori(1, count) as i:
                    step.begin(i - 1, per)
                    body(i)
                    step.end()
                step.leave(count - 1)
                body(count, head=False)

            def attended(i, o_sem, yT):
                act.wait_ge(o_sem, i * 2)
                for e in range(2):
                    if e == 0:
                        nc.scalar.activation(tile(yT, i * 2 - 2), bank[:, 3, 0:T], ACT.Copy)
                    else:
                        nc.scalar.activation(tile(yT, i * 2 - 1), bank[:, 3, T:2 * T], ACT.Copy)

            def sb(i, head=True, tail=True):
                if not tail:
                    return
                for e in range(2):
                    act.wait_ge(zm_done, i * 2 + (e - 1))
                    step(nc.scalar.activation(s_b[:, e, :], s_a[:, e, :], ACT.Abs))
                    step(nc.scalar.activation(s_c[:, e, :], s_b[:, e, :], ACT.Exp, scale=-1.0))
                    nc.scalar.activation(s_d[:, e, :], s_c[:, e, :], ACT.Ln, bias=ones[:, 0:1]).then_inc(l_done, 1)
                for e in range(2):
                    act.wait_ge(d_done, i * 2 + (e - 1))
                    nc.scalar.activation(s_f[:, e, :], s_b[:, e, :], ACT.Exp).then_inc(w_done, 1)
                attended(i, o_done, yaT)
            overlapped(sb, 4, 4)
            phase_end(act, 3)

            for h in range(IDX_HEADS):
                act.wait_ge(dots_done, h + 1)
                if h >= 2:
                    act.wait_ge(relu_used, h - 1)
                nc.scalar.activation(relu[:, (h % 2) * 384:(h % 2 + 1) * 384], bank[:, h % 8, 0:384], ACT.Relu,
                                     scale=IDX_D ** -0.5 * IDX_HEADS ** -0.5).then_inc(relu_done, 1)
            phase_end(act, 4)

            def dsa(i, head=True, tail=True):
                if not tail:
                    return
                for e in range(2):
                    act.wait_ge(max_done, i * 2 + (e - 1))
                    nc.scalar.activation(s_b[:, e, 0:P], s_a[:, e, 0:P], ACT.Exp, bias=small[:, 8 * e:8 * e + 1],
                                         accum_out=small[:, 8 * e + 2:8 * e + 3])
                    nc.scalar.activation(s_b[:, e, P:384], s_a[:, e, P:384], ACT.Exp, bias=small[:, 8 * e + 1:8 * e + 2],
                                         accum_out=small[:, 8 * e + 3:8 * e + 4]).then_inc(exp_done, 1)
                for e in range(2):
                    act.wait_ge(turned, i * 2 + (e - 1))
                    nc.scalar.activation(s_f[:, e, :], bank[:, 6 + e, 0:384], ACT.Copy).then_inc(turned_read, 1)
                attended(i, o2_done, ybT)
            overlapped(dsa, 4, 0)
            phase_end(act, 5)

            def merge(i):
                if not first(i):
                    act.wait_ge(merged, i * 2)
                for s in (2, 3):
                    for t in range(2):
                        act.wait_ge(tiles["merge"], i * 8 + (2 * s + t + 1))
                        nc.scalar.activation(gates[:, 2 * s + t - 4, :], bank[:, 2 * s + t, 0:T], ACT.Sigmoid)\
                            .then_inc(merge_read[s], 1)
            repeat(act, 8, merge)
            phase_end(act, 6)
            phase_end(act, 7)
            norm_act(act, x1, T, step)
            phase_end(act, 8)

            def up(i):
                if not first(i):
                    act.wait_ge(acted, i * 4)
                for half in range(2):
                    for u in range(4):
                        q = 4 * half + u
                        f = 4 * i + (2 * half + u % 2 + (KF if u >= 2 else 0))
                        act.wait_ge(tiles["up"], i * 8 + (q + 1))
                        nc.scalar.activation(cv[:, q, 0:T], bank[:, q, 0:T], ACT.Identity, scale=pcol("conv_w", 4 * KF + f),
                                             bias=pcol("conv_b", f)).then_inc(tap_done, 1)
                    for t in range(2):
                        act.wait_ge(evac["up"], i * 8 + (4 * half + t + 1))
                        nc.scalar.activation(sa[:, 2 * half + t, :], cv[:, 4 * half + t, 0:T], ACT.Silu).then_inc(silu_done, 1)
            repeat(act, 11, up)
            phase_end(act, 9)
            phase_end(act, 10)
            norm_act(act, x1, T, step)
            phase_end(act, 11)

            act.wait_ge(meta_loaded, 16)
            norm_act(act, res, NT, step)
            phase_end(act, 12)

            def conv2(i):
                if not first(i):
                    act.wait_ge(evac["conv2"], i * 2)
                for t in range(2):
                    act.wait_ge(tiles["conv2"], i * 6 + (3 + t))
                    nc.scalar.activation(cs[:, t, :], bank[:, 2 + t, 0:NT], ACT.Copy).then_inc(c_copied, 1)
            repeat(act, 4, conv2)
            phase_end(act, 13)

            def rkv(i):
                for q in range(8):
                    act.wait_ge(tiles["rkv"], i * 8 + (q + 1))
                    f = i * 8 + q
                    m = omu[:, f:f + 1] if isinstance(f, int) else omu[:, bass.ds(f, 1)]
                    nc.scalar.activation(tile(zr, f), bank[:, q, 0:NT], ACT.Copy, scale=m).then_inc(own_done, 1)
            repeat(act, 3, rkv)
            phase_end(act, 14)
            lora_parts = [(gd[:, 0, :], bank[:, 0, 0:NT], omu[:, 24:25]), (gd[:, 1, :], bank[:, 1, 0:NT], omu[:, 25:26]),
                          (wdad[0:LORA, 0, :], bank[0:LORA, 2, 0:NT], omu[0:LORA, 26:27]),
                          (wdad[0:LORA, 1, :], bank[0:LORA, 3, 0:NT], omu[0:LORA, 27:28])]
            for n, (dst, src, m) in enumerate(lora_parts):
                act.wait_ge(tiles["lora"], n + 1)
                nc.scalar.activation(dst, src, ACT.Copy, scale=m).then_inc(own_done, 1)
            act.wait_ge(evac["lora"], 4)
            nc.scalar.activation(wdad[0:LORA, 0, :], wdad[0:LORA, 0, :], ACT.Tanh).then_inc(lora_ready, 2)
            for t in range(2):
                nc.scalar.activation(gd[:, t, :], gd[:, t, :], ACT.Sigmoid)
            for u, (dst, shift) in enumerate(((lw, "w0"), (aa, "a0"))):
                for j in range(KW):
                    act.wait_ge(tiles["loraup"], u * KW + j + 1)
                    nc.scalar.activation(dst[:, j, :], bank[:, j, 0:NT], ACT.Sigmoid, bias=param(shift, j)).then_inc(evac["loraup"], 1)
            act.wait_ge(kk_floored, 1)
            nc.scalar.activation(all8(temp8b), all8(temp8b), ACT.Sqrt).then_inc(kk_rooted, 1)
            phase_end(act, 15)

            def recur(i):
                nl = len(LEVELS)
                act.wait_ge(cum_done, i + 1)
                nc.scalar.activation(Ep, cumc, ACT.Exp)
                nc.scalar.activation(Em, cumc, ACT.Exp, scale=-1.0)
                nc.scalar.activation(Epm, cpm, ACT.Exp)
                nc.scalar.activation(ecm, mids, ACT.Exp)
                nc.scalar.activation(vt, tile(zr, i + 2 * KW), ACT.Copy).then_inc(exps_done, 1)
                for e in range(2):
                    act.wait_ge(t0_raw, i * 2 + (e + 1))
                    nc.scalar.activation(TT[0:L, e, :], bank[0:L, 2 + e, 0:NT], ACT.Copy).then_inc(t0_ready, 1)
                for l in range(nl):
                    for e in range(2):
                        n = 2 * l + e
                        act.wait_ge(w1_raw, i * 2 * nl + (n + 1))
                        nc.scalar.activation(W1[0:L, e, :], bank[0:L, e, 0:NT], ACT.Copy).then_inc(w1_ready, 1)
                        if n < 3:
                            act.wait_ge(task_done, i * 10 + (n + 1))
                            dst = (tokK, tokB, tokV)[n]
                            nc.scalar.activation(dst[0:L, :, :].rearrange("p a t -> p (a t)"), bank[0:L, 6 + n % 2, :], ACT.Copy)\
                                .then_inc(tok_read, 1)
                for c in range(NC):
                    act.wait_ge(x_raw, i * NC + (c + 1))
                    nc.scalar.activation(Xs[0:L, :].rearrange("p (a v) -> p a v", a=2), bank[0:L, 0:2, 0:RN], ACT.Copy).then_inc(x_ready, 1)
                act.wait_ge(y_raw, i + 1)
                y = tile(zr, i)
                nc.scalar.activation(y[0:RN, :], bank[0:RN, 4, 0:NT], ACT.Copy)
                nc.scalar.activation(y[RN:P, :], bank[RN:P, 5, 0:NT], ACT.Copy).then_inc(pair_done, 1)
            repeat(act, KW, recur)
            phase_end(act, 16)

            for j in range(KW):
                act.wait_ge(centred, j + 1)
                nc.scalar.activation(kk[:, j, :], zr[:, j, :], ACT.Square).then_inc(y_squared, 1)
            for j in range(KW):
                act.wait_ge(var_raw, j + 1)
                nc.scalar.activation(lw[:, j, :], bank[:, j, 0:NT], ACT.Sqrt, scale=1.0 / RN, bias=epsc[:, 1:2]).then_inc(var_read, 1)
            phase_end(act, 17)

            def read_tiles(phase, n, per, count, ready):
                def body(i):
                    for q in range(per):
                        f = i * per + q
                        act.wait_ge(ready, f + 1)
                        nc.scalar.activation(tile(fT, f)[:, 0:n], bank[:, q, 0:n], ACT.Copy).then_inc(evac[phase], 1)
                repeat(act, count, body)
            read_tiles("mix2", NT, 8, 2, tiles["mix2"])
            phase_end(act, 18)
            norm_act(act, fT, NT, step)
            phase_end(act, 19)
            norm_act(act, res, NT, step)
            phase_end(act, 20)

            def up2(i):
                if not first(i):
                    act.wait_ge(evac["up2"], i * 8)
                for half in range(2):
                    for t in range(2):
                        q = 4 * half + t
                        act.wait_ge(tiles["up2"], i * 8 + (q + 1))
                        nc.scalar.activation(cv[:, q, 0:T], bank[:, q, HALO:T + HALO], ACT.Copy,
                                             scale=pcol("conv_ffn", 4 * i + (2 * half + t + 2 * KF))).then_inc(tap2_done, 1)
                    for t in range(2):
                        act.wait_ge(evac["up2"], i * 8 + (4 * half + t + 1))
                        nc.scalar.activation(sa[:, 2 * half + t, :], cv[:, 4 * half + t, 0:T], ACT.Silu).then_inc(silu2_done, 1)
            repeat(act, 11, up2)
            phase_end(act, 21)
            read_tiles("down2", T, 2, 8, halves["down2"])
            phase_end(act, 22)
            norm_act(act, fT[:, :, 0:T], T, step)
            phase_end(act, 23)

        @block.vector
        def _(dve):
            step = Steps(dve, dve_step)
            nc.vector.memset(epsc[:, 0:1], EPS)
            nc.vector.memset(epsc[:, 1:2], GN_EPS)
            nc.vector.memset(ones[:], 1.0).then_inc(ones_set, 1)
            dve.wait_ge(params_in, 16)
            dve.wait_ge(tiles["ada"], 12 * NSLOT)
            flat = mod[:].rearrange("p a k -> p (a k)")
            step(nc.vector.tensor_tensor(flat, bank[:, 0, 0:6 * KD], param("b_ada"), ALU.add))
            nc.vector.scalar_tensor_tensor(gain[:, 0, :], mod[:, 1, :], 1.0, param("g_mix"), ALU.add, ALU.mult)
            nc.vector.scalar_tensor_tensor(gain[:, 1, :], mod[:, 4, :], 1.0, param("g_ffn"), ALU.add, ALU.mult)
            nc.vector.tensor_scalar(mod[:, 2, :], mod[:, 2, :], 1.0, None, ALU.add)
            step(nc.vector.tensor_scalar(mod[:, 5, :], mod[:, 5, :], 1.0, None, ALU.add))
            phase_end(dve, 1)

            dve.wait_ge(pos_in, 16)
            dve.wait_ge(consts_in, 16)
            dve.wait_ge(x_loaded, 16)
            step(nc.vector.tensor_copy(posf, posi))
            C1, C2 = 6.28125, 0.0019350051879882812
            C3 = 2 * math.pi - C1 - C2
            ROUND = 1.5 * 2.0 ** 23
            EDGE = 3.1415925
            for n in range(4):
                f = n // 2
                cosine = n % 2 == 1
                if n:
                    dve.wait_ge(angle_done, n)
                step(nc.vector.tensor_scalar(angles[:, 0, :], posf, const("invf")[:, f:f + 1], None, ALU.mult))
                step(nc.vector.tensor_scalar(angles[:, 1, :], angles[:, 0, :], 1 / (2 * math.pi), 0.25 if cosine else 0.0,
                                             ALU.mult, ALU.add))
                step(nc.vector.tensor_scalar(angles[:, 1, :], angles[:, 1, :], ROUND, -ROUND, ALU.add, ALU.add))
                for c in (C1, C2, C3):
                    step(nc.vector.scalar_tensor_tensor(angles[:, 0, :], angles[:, 1, :], -c, angles[:, 0, :], ALU.mult, ALU.add))
                step(nc.vector.tensor_scalar(angles[:, 0, :], angles[:, 0, :], math.pi / 2 if cosine else 0.0, EDGE,
                                             ALU.add, ALU.min))
                nc.vector.tensor_scalar(turns[:, n, :], angles[:, 0, :], -EDGE, None, ALU.max).then_inc(angle_done, 1)
            norm_dve(dve, T, step, scaled_shifted(h1, x1, gain[:, 0, :], mod[:, 0, :], T, step))
            dve.wait_ge(sines, 4)
            step(nc.vector.tensor_scalar(tabs128[:, 0, 0:T], tabs128[:, 0, 0:T], const("sign")[:, 0:1], None, ALU.mult))
            nc.vector.tensor_scalar(tabs64[:, 0, :], tabs64[:, 0, :], const("sign")[:, 1:2], None, ALU.mult)
            for n in range(2):
                nc.vector.tensor_copy(tabs128[:, n, T:2 * T], tabs128[:, n, 0:T])
            phase_end(dve, 2)

            def overlapped(body, count, per):
                body(0, tail=False)
                with dve.Fori(1, count) as i:
                    step.begin(i - 1, per)
                    body(i)
                    step.end()
                step.leave(count - 1)
                body(count, head=False)

            def sb(i, head=True, tail=True):
                if tail:
                    for e in range(2):
                        dve.wait_ge(z_done, i * 2 + (e - 1))
                        nc.vector.scalar_tensor_tensor(s_a[:, e, :], bank[:, 4 + e, 0:384], SCALE, past, ALU.mult, ALU.add)\
                            .then_inc(zm_done, 1)
                if head:
                    dve.wait_ge(tiles["sb"], i * 3 + 1)
                    nc.vector.tensor_copy(qT[:].rearrange("p a t -> p (a t)"), bank[:, 0, :]).then_inc(q_read, 1)
                if tail:
                    for e in range(2):
                        dve.wait_ge(l_done, i * 2 + (e - 1))
                        dve.wait_ge(zm_done, i * 2 + (e - 1))
                        nc.vector.scalar_tensor_tensor(s_e[:, e, :], s_a[:, e, :], 0.0, s_d[:, e, :], ALU.max, ALU.add)\
                            .then_inc(sp_done, 1)
                if head:
                    dve.wait_ge(tiles["sb"], i * 3 + 2)
                    nc.vector.tensor_copy(kT[:].rearrange("p a t -> p (a t)"), bank[:, 1, :]).then_inc(k_read, 1)
                if tail:
                    for e in range(2):
                        dve.wait_ge(s_done, i * 2 + (e - 1))
                        nc.vector.tensor_tensor(s_b[:, e, :], s_a[:, e, :], bank[:, 6 + e, 0:384], ALU.subtract)\
                            .then_inc(d_done, 1)
                    dve.wait_ge(d_done, i * 2)
                if head:
                    dve.wait_ge(tiles["sb"], i * 3 + 3)
                    if tail:
                        dve.wait_ge(o_done, i * 2)
                    nc.vector.tensor_copy(vS[:].rearrange("p a t -> p (a t)"), bank[:, 2, :]).then_inc(v_read, 1)
            overlapped(sb, 4, 0)
            phase_end(dve, 3)

            def rope(dst, src, n, tabs, half, done, count):
                sin, cos = tabs[:, 0, 0:n], tabs[:, 1, 0:n]
                a, b = ropeA[:, 0:n], ropeB[:, 0:n]
                for lo in range(0, P, 2 * half):
                    mid, hi = lo + half, lo + 2 * half
                    nc.vector.tensor_tensor(a[lo:mid, :], src[mid:hi, :], sin[mid:hi, :], ALU.mult)
                    last = nc.vector.tensor_tensor(a[mid:hi, :], src[lo:mid, :], sin[lo:mid, :], ALU.mult)
                step.mark(last)
                step(nc.vector.tensor_tensor(b, src, cos, ALU.mult))
                nc.vector.tensor_tensor(dst, a, b, ALU.add).then_inc(done, 1)
                dve.wait_ge(done, count)

            dve.wait_ge(tiles["ki"], 1)
            rope(kiT, bank[:, 6, 0:T], T, tabs64, 32, evac["ki"], 1)
            dve.wait_ge(tiles["ki"], 2)
            nc.vector.tensor_copy(small[:, 0:2 * IDX_HEADS], bank[:, 7, 0:2 * IDX_HEADS]).then_inc(evac["ki"], 1)
            for q in range(8):
                dve.wait_ge(tiles["qi"], q + 1)
                rope(qiT[:, q, :], bank[:, q, 0:T], T, tabs64, 32, evac["qi"], q + 1)
            score, spare = s_a[:, 0, :], s_a[:, 1, :]
            dve.wait_ge(evac["ki"], 2)
            step(nc.vector.memset(score, 0.0))
            for h in range(IDX_HEADS):
                dve.wait_ge(relu_done, h + 1)
                r = relu[:, (h % 2) * 384:(h % 2 + 1) * 384]
                step.mark(nc.vector.scalar_tensor_tensor(score[:, 0:P], r[:, 0:P], small[:, h:h + 1], score[:, 0:P],
                                                         ALU.mult, ALU.add))
                nc.vector.scalar_tensor_tensor(score[:, P:384], r[:, P:384], small[:, IDX_HEADS + h:IDX_HEADS + h + 1],
                                               score[:, P:384], ALU.mult, ALU.add).then_inc(relu_used, 1)
                dve.wait_ge(relu_used, h + 1)
            step(nc.vector.scalar_tensor_tensor(score, seen, UNSEEN / NEG, score, ALU.mult, ALU.add))
            src, dst = score, spare
            for r in range(TOPK // 8):
                for lo, hi, m in ((0, P, 40), (P, 384, 48)):
                    step.mark(nc.vector.max(small[:, m:m + 8], src[:, lo:hi]))
                step.wait()
                for lo, hi, m in ((0, P, 40), (P, 384, 48)):
                    step.mark(nc.vector.match_replace(dst[:, lo:hi], small[:, m:m + 8], src[:, lo:hi], TAKEN))
                step.wait()
                src, dst = dst, src
            taken = biasM[:, 0, :]
            step(nc.vector.tensor_scalar(taken, src, TAKEN, None, ALU.is_equal))
            step(nc.vector.tensor_scalar(taken, taken, -NEG, NEG, ALU.mult, ALU.add))
            step(nc.vector.tensor_tensor(taken, taken, seen, ALU.add))
            phase_end(dve, 4)

            def dsa(i, head=True, tail=True):
                if tail:
                    for e in range(2):
                        dve.wait_ge(logits_done, i * 2 + (e - 1))
                        step(nc.vector.scalar_tensor_tensor(s_a[:, e, :], bank[:, 4 + e, 0:384], SCALE, taken, ALU.mult, ALU.add))
                        nc.vector.tensor_reduce(small[:, 8 * e:8 * e + 1], s_a[:, e, 0:P], AX, ALU.max, negate=True)
                        nc.vector.tensor_reduce(small[:, 8 * e + 1:8 * e + 2], s_a[:, e, P:384], AX, ALU.max, negate=True)\
                            .then_inc(max_done, 1)
                if head:
                    dve.wait_ge(tiles["dsa"], i * 3 + 1)
                    rope(qT[:].rearrange("p a t -> p (a t)"), bank[:, 0, :], 2 * T, tabs128, 64, q2_read, i + 1)
                if tail:
                    for e in range(2):
                        dve.wait_ge(exp_done, i * 2 + (e - 1))
                        step(nc.vector.reciprocal(small[:, 8 * e + 4:8 * e + 6], small[:, 8 * e + 2:8 * e + 4]))
                        step.mark(nc.vector.tensor_scalar(s_c[:, e, 0:P], s_b[:, e, 0:P], small[:, 8 * e + 4:8 * e + 5], None, ALU.mult))
                        nc.vector.tensor_scalar(s_c[:, e, P:384], s_b[:, e, P:384], small[:, 8 * e + 5:8 * e + 6], None, ALU.mult)\
                            .then_inc(probs_done, 1)
                if head:
                    dve.wait_ge(tiles["dsa"], i * 3 + 2)
                    rope(kT[:].rearrange("p a t -> p (a t)"), bank[:, 1, :], 2 * T, tabs128, 64, k2_read, i + 1)
                    dve.wait_ge(tiles["dsa"], i * 3 + 3)
                    if tail:
                        dve.wait_ge(o2_done, i * 2)
                    nc.vector.tensor_copy(vS[:].rearrange("p a t -> p (a t)"), bank[:, 2, :]).then_inc(v2_read, 1)
            overlapped(dsa, 4, 10)
            phase_end(dve, 5)

            def merge(i):
                for s in range(2):
                    for t in range(2):
                        dve.wait_ge(merge_read[2 + s], i * 2 + (t + 1))
                        nc.vector.tensor_tensor(gated[:, 2 * s + t, :], gates[:, 2 * s + t, :],
                                                bank[:, 2 * s + t, 0:T], ALU.mult).then_inc(merge_read[s], 1)
                for t in range(2):
                    dve.wait_ge(merge_read[1], i * 2 + (t + 1))
                    nc.vector.tensor_tensor(tile(mergedT, i * 2 + t), gated[:, t, :], gated[:, 2 + t, :],
                                            ALU.add).then_inc(merged, 1)
            repeat(dve, 8, merge)
            phase_end(dve, 6)

            def add_gated(phase, n, per, count, gate, ready=None):
                def body(i):
                    for q in range(per):
                        f = i * per + q
                        dve.wait_ge(ready or tiles[phase], f + 1)
                        g = gate[:, f:f + 1] if isinstance(f, int) else gate[:, bass.ds(f, 1)]
                        nc.vector.scalar_tensor_tensor(tile(x1, f), bank[:, q, 0:n], g, tile(x1, f), ALU.mult, ALU.add)\
                            .then_inc(evac[phase], 1)
                repeat(dve, count, body)
            add_gated("wo", T, 8, 2, mod[:, 2, :])
            phase_end(dve, 7)
            norm_dve(dve, T, step, scaled_shifted(h1, x1, gain[:, 1, :], mod[:, 3, :], T, step))
            phase_end(dve, 8)

            def up(i):
                def taps(q, f):
                    dve.wait_ge(tap_done, i * 8 + (q + 1))
                    c, b = cv[:, q, 0:T], bank[:, q, 0:T]
                    step(nc.vector.scalar_tensor_tensor(c[:, 1:T], b[:, 0:T - 1], pcol("conv_w", 2 * KF + f), c[:, 1:T],
                                                        ALU.mult, ALU.add))
                    nc.vector.scalar_tensor_tensor(c[:, 2:T], b[:, 0:T - 2], pcol("conv_w", f), c[:, 2:T],
                                                   ALU.mult, ALU.add).then_inc(evac["up"], 1)
                step.begin(i)
                for half in range(2):
                    for u in range(4):
                        taps(4 * half + u, 4 * i + (2 * half + u % 2 + (KF if u >= 2 else 0)))
                    for t in range(2):
                        dve.wait_ge(silu_done, i * 4 + (2 * half + t + 1))
                        dve.wait_ge(evac["up"], i * 8 + (4 * half + 2 + t + 1))
                        nc.vector.tensor_tensor(tile(actT, i * 4 + (2 * half + t)), sa[:, 2 * half + t, :],
                                                cv[:, 4 * half + 2 + t, 0:T], ALU.mult).then_inc(acted, 1)
                step.end()
            repeat(dve, 11, up)
            step.leave(11)
            phase_end(dve, 9)
            add_gated("down", T, 2, 8, mod[:, 5, :], ready=halves["down"])
            phase_end(dve, 10)
            norm_dve(dve, T, step, scaled(x1, x1, param("g_final"), T))
            phase_end(dve, 11)

            norm_dve(dve, NT, step, scaled(hT, res, param("g_pre_mix"), NT))
            lo = pw["mu_rkv"][0]
            nc.vector.tensor_scalar(omu[:], params[:, lo:lo + 28], -1.0, 1.0, ALU.mult, ALU.add)
            nc.vector.tensor_scalar(omka[:], param("k_a"), -1.0, 1.0, ALU.mult, ALU.add)
            nc.vector.memset(chs[:, :, 0:HALO], 0.0)
            phase_end(dve, 12)

            def conv2(i):
                step.begin(i)
                for t in range(2):
                    f = i * 2 + t
                    dve.wait_ge(c_copied, i * 2 + (t + 1))
                    dve.wait_ge(tiles["conv2"], i * 6 + (5 + t))
                    step(nc.vector.tensor_tensor(chs[:, t, HALO:HALO + NT], cs[:, t, :], bank[:, 4 + t, 0:NT], ALU.mult))
                    step(nc.vector.tensor_scalar(ycs[:, t, :], chs[:, t, 0:NT], pcol("conv_w2", f), None, ALU.mult))
                    for tap in (1, 2):
                        step(nc.vector.scalar_tensor_tensor(ycs[:, t, :], chs[:, t, tap:tap + NT], pcol("conv_w2", f + tap * KW),
                                                            ycs[:, t, :], ALU.mult, ALU.add))
                    nc.vector.tensor_tensor(tile(yconv, f), ycs[:, t, :], bank[:, t, 0:NT], ALU.mult).then_inc(evac["conv2"], 1)
                step.end()
            repeat(dve, 4, conv2)
            step.leave(4)
            phase_end(dve, 13)

            def shift(dst, src, mu, f, done):
                dve.wait_ge(own_done, f + 1)
                nc.vector.scalar_tensor_tensor(dst[:, 1:NT], src[:, 0:NT - 1], mu, dst[:, 1:NT], ALU.mult, ALU.add).then_inc(done, 1)

            def rkv(i):
                for q in range(8):
                    f = i * 8 + q
                    shift(tile(zr, f), bank[:, q, 0:NT], pcol("mu_rkv", f), f, evac["rkv"])
            repeat(dve, 3, rkv)
            phase_end(dve, 14)
            for t in range(2):
                shift(gd[:, t, :], bank[:, t, 0:NT], param("mu_gd", t), 24 + t, evac["lora"])
            for t, name in enumerate(("mu_wd", "mu_ad")):
                shift(wdad[0:LORA, t, :], bank[0:LORA, 2 + t, 0:NT], param(name, 0)[0:LORA, :], 26 + t, evac["lora"])
            for j in range(KW):
                last = nc.vector.tensor_scalar(kk[:, j, :], zr[:, KW + j, :], param("k_k", j), None, ALU.mult)
            step(last)
            nc.vector.tensor_tensor(all8(temp8), all8(kk), all8(kk), ALU.mult).then_inc(kk_squared, 1)
            dve.wait_ge(evac["loraup"], KW)
            nc.vector.tensor_scalar(all8(lw), all8(lw), -DECAY_SCALE, None, ALU.mult)
            for j in range(KW):
                dve.wait_ge(kk_summed, j + 1)
                last = nc.vector.tensor_scalar(temp8b[:, j, :], bank[:, j, 0:NT], 1e-24, None, ALU.max)
            last.then_inc(kk_floored, 1)
            dve.wait_ge(kk_rooted, 1)
            step(nc.vector.reciprocal(all8(temp8b), all8(temp8b)))
            nc.vector.tensor_tensor(all8(kk), all8(kk), all8(temp8b), ALU.mult)
            phase_end(dve, 15)

            def by_chunk(x):
                return x.rearrange("p (c t) -> p c t", c=NC)

            def mask(name):
                return const(name)[0:L, :].unsqueeze(1).to_broadcast([L, NC, L])

            def recur(i):
                nl = len(LEVELS)
                step.begin(i)
                if not first(i):
                    dve.wait_ge(pair_done, i)
                lwi = tile(lw, i)
                for c in range(NC):
                    last = nc.vector.tensor_tensor_scan(cum[:, c * L:(c + 1) * L], onesrow, lwi[:, c * L:(c + 1) * L], 0.0,
                                                        ALU.mult, ALU.add)
                step(last)
                for c in range(NC):
                    m = cum[:, c * L + MID:c * L + MID + 1]
                    step.mark(nc.vector.tensor_scalar(cumc[:, c * L:(c + 1) * L], cum[:, c * L:(c + 1) * L], m, None, ALU.subtract))
                step(nc.vector.tensor_copy(mids, by_chunk(cum)[:, :, MID]))
                nc.vector.tensor_tensor(cpm, cumc, lwi, ALU.subtract).then_inc(cum_done, 1)
                ki = tile(zr, i + KW)
                step(nc.vector.tensor_scalar(k2, tile(aa, i), pcol("k_a", i), omka[:, i:i + 1] if isinstance(i, int)
                                             else omka[:, bass.ds(i, 1)], ALU.mult, ALU.add))
                step(nc.vector.tensor_tensor(k2, k2, ki, ALU.mult))
                step(nc.vector.tensor_tensor(bb, tile(kk, i), tile(aa, i), ALU.mult))
                step.mark(nc.vector.scalar_tensor_tensor(rkr, tile(zr, i), pcol("r_k", i), k2, ALU.mult, ALU.mult))
                dve.wait_ge(exps_done, i + 1)
                nc.vector.scalar_tensor_tensor(AR[:, :, 0, :], by_chunk(Epm), -1.0, by_chunk(tile(kk, i)), ALU.mult, ALU.mult)
                nc.vector.tensor_tensor(AR[:, :, 1, :], by_chunk(Ep), by_chunk(tile(zr, i)), ALU.mult)
                nc.vector.tensor_tensor(kt, k2, Em, ALU.mult)
                nc.vector.tensor_tensor(bt, bb, Em, ALU.mult).then_inc(feat_done, 1)
                for e in range(2):
                    dve.wait_ge(n_raw, i * 2 + (e + 1))
                    step(nc.vector.scalar_tensor_tensor(by_chunk(N[0:L, e, :]), by_chunk(bank[0:L, e, 0:NT]), BIG, mask("strict"),
                                                        ALU.min, ALU.mult))
                    step(nc.vector.tensor_tensor(by_chunk(G[0:L, e, :]), by_chunk(N[0:L, e, :]), mask("first"), ALU.mult))
                    nc.vector.tensor_tensor(by_chunk(G[0:L, e, :]), by_chunk(G[0:L, e, :]),
                                            const("ident")[0:L, 0:L].unsqueeze(1).to_broadcast([L, NC, L]), ALU.add)\
                        .then_inc(g0_done, 1)
                for l in range(nl):
                    for e in range(2):
                        n = 2 * l + e
                        if 3 <= n < 10:
                            dve.wait_ge(task_done, i * 10 + (n + 1))
                            b = bank[:, 6 + n % 2, 0:NT]
                            if n < 9:
                                kind, h = (n - 3) // 2, (n - 3) % 2
                                dst = (lak, lrk, lrb)[kind]
                                ins = nc.vector.scalar_tensor_tensor(by_chunk(dst[0:L, h, :]), by_chunk(b[0:L, :]), BIG,
                                                                     mask("strict" if kind == 0 else "incl"), ALU.min, ALU.mult)
                            else:
                                ins = nc.vector.tensor_tensor(ki, tile(zr, i + 2 * KW), b, ALU.mult)
                            ins.then_inc(mat_read, 1)
                    for e in range(2):
                        dve.wait_ge(tg_raw, i * 2 * nl + (2 * l + e + 1))
                        if l < nl - 1:
                            nc.vector.tensor_tensor(TT[0:L, e, :], TT[0:L, e, :], bank[0:L, 2 + e, 0:NT], ALU.add)
                        nc.vector.tensor_tensor(G[0:L, e, :], G[0:L, e, :], bank[0:L, 4 + e, 0:NT], ALU.add).then_inc(tg_ready, 1)
                for c in range(NC):
                    dve.wait_ge(u_raw, i * NC + (c + 1))
                    nc.vector.tensor_copy(Us[0:L, :], bank[0:L, 2, 0:P]).then_inc(u_ready, 1)
                    if c < NC - 1:
                        dve.wait_ge(h_raw, i * 3 + (c + 1))
                        src = bank[:, 3, 0:RN]
                        if c:
                            step(nc.vector.tensor_tensor(Hsum, bank[:, 3, 0:RN], Hs[:, c % 2, :], ALU.add))
                            src = Hsum
                        nc.vector.tensor_scalar(Hs[:, (c + 1) % 2, :], src, Ep[:, (c + 1) * L - 1:(c + 1) * L],
                                                ecm[:, c + 1:c + 2], ALU.mult, ALU.mult).then_inc(h_ready, 1)
                        dve.wait_ge(h_ready, i * 3 + (c + 1))
                step.end()
            repeat(dve, KW, recur)
            step.leave(KW)
            phase_end(dve, 16)

            for j in range(KW):
                dve.wait_ge(mean_raw, j + 1)
                nc.vector.scalar_tensor_tensor(zr[:, j, :], bank[:, j, 0:NT], -1.0 / RN, zr[:, j, :], ALU.mult, ALU.add)\
                    .then_inc(centred, 1)
            dve.wait_ge(var_read, KW)
            dve.wait_ge(centred, KW)
            step(nc.vector.reciprocal(all8(lw), all8(lw)))
            for j in range(KW):
                step(nc.vector.scalar_tensor_tensor(zr[:, j, :], zr[:, j, :], param("ln_w", j), lw[:, j, :], ALU.mult, ALU.mult))
                step(nc.vector.scalar_tensor_tensor(zr[:, j, :], zr[:, j, :], param("ln_b", j), zr[:, KW + j, :], ALU.add, ALU.add))
                dve.wait_ge(gate_tiles, j + 1)
                nc.vector.tensor_tensor(zr[:, j, :], zr[:, j, :], bank[:, j, 0:NT], ALU.mult)
            phase_end(dve, 17)
            phase_end(dve, 18)

            def add_normed(g, n, dst):
                def apply(k):
                    step(nc.vector.scalar_tensor_tensor(fT[:, k, 0:n], fT[:, k, 0:n], param(g, k), rms[:, 0:n], ALU.mult, ALU.mult))
                    return nc.vector.tensor_tensor(dst[:, k, :], dst[:, k, :], fT[:, k, 0:n], ALU.add)
                return apply
            norm_dve(dve, NT, step, add_normed("g_post_mix", NT, res))
            phase_end(dve, 19)
            norm_dve(dve, NT, step, scaled(hT, res, param("g_pre_ffn"), NT))
            phase_end(dve, 20)

            def up2(i):
                step.begin(i)
                for half in range(2):
                    for t in range(2):
                        q = 4 * half + t
                        f = 4 * i + (2 * half + t)
                        dve.wait_ge(tap2_done, i * 4 + (2 * half + t + 1))
                        step(nc.vector.scalar_tensor_tensor(cv[:, q, 0:T], bank[:, q, 1:T + 1], pcol("conv_ffn", f + KF),
                                                            cv[:, q, 0:T], ALU.mult, ALU.add))
                        nc.vector.scalar_tensor_tensor(cv[:, q, 0:T], bank[:, q, 0:T], pcol("conv_ffn", f),
                                                       cv[:, q, 0:T], ALU.mult, ALU.add).then_inc(evac["up2"], 1)
                    for t in range(2):
                        q = 4 * half + 2 + t
                        dve.wait_ge(silu2_done, i * 4 + (2 * half + t + 1))
                        dve.wait_ge(tiles["up2"], i * 8 + (q + 1))
                        nc.vector.tensor_tensor(tile(actT, i * 4 + (2 * half + t)), sa[:, 2 * half + t, :],
                                                bank[:, q, 0:T], ALU.mult).then_inc(evac["up2"], 1)
                step.end()
            repeat(dve, 11, up2)
            step.leave(11)
            phase_end(dve, 21)
            phase_end(dve, 22)
            norm_dve(dve, T, step, add_normed("g_post_ffn", T, x1))
            dve.sem_inc(result_ready, 1)
            phase_end(dve, 23)

        @block.gpsimd
        def _(pool):
            pool.wait_ge(consts_in, 16)

            def recur(i):
                nl = len(LEVELS)
                for l, b in enumerate(LEVELS):
                    for e in range(2):
                        if l == 0:
                            pool.wait_ge(g0_done, i * 2 + (e + 1))
                        if l >= 2:
                            pool.wait_ge(w1_raw, i * 2 * nl + (2 * (l - 2) + e + 1))
                        nc.gpsimd.tensor_tensor(
                            NM[0:L, l % 2, e * NT:(e + 1) * NT].rearrange("p (c t) -> p c t", c=NC),
                            N[0:L, e, :].rearrange("p (c t) -> p c t", c=NC),
                            const(f"level{b}")[0:L, :].unsqueeze(1).to_broadcast([L, NC, L]), ALU.mult).then_inc(nm_ready, 1)
            repeat(pool, KW, recur)


def constant_block():
    where, width = offsets(CONSTS)
    c = np.zeros((P, width), np.float32)

    def put(name, a):
        lo = where[name][0]
        c[:a.shape[0], lo:lo + a.shape[1]] = a
    p = np.arange(P)[:, None]
    j = np.arange(P)[None, :]
    put("ident", (p == j).astype(np.float32))
    put("tri", (p >= j).astype(np.float32))
    put("heads", (p // RN == j // RN).astype(np.float32))
    past = np.where(p < j, 0.0, NEG).astype(np.float32)
    put("past", np.concatenate([past, np.zeros((P, P), np.float32), past], 1))
    seen = np.where(j <= p, 0.0, NEG).astype(np.float32)
    put("seen", np.concatenate([seen, np.zeros((P, P), np.float32), seen], 1))
    invf, sign = np.zeros((P, 2), np.float32), np.zeros((P, 2), np.float32)
    for n, d in enumerate((HD, IDX_D)):
        f = (np.float32(1.0) / (np.float32(10000.0) ** (np.arange(0, d, 2, dtype=np.float32) / np.float32(d)))).astype(np.float32)
        at = np.arange(P) % d
        invf[:, n] = f[at % (d // 2)]
        sign[:, n] = np.where(at < d // 2, 1.0, -1.0)
    put("invf", invf)
    put("sign", sign)
    s, t = np.arange(L)[:, None], np.arange(L)[None, :]
    put("strict", (s < t).astype(np.float32))
    put("incl", (s <= t).astype(np.float32))

    def level(b):
        return ((s // (2 * b) == t // (2 * b)) & (s % (2 * b) < b) & (t % (2 * b) >= b)).astype(np.float32)
    put("first", level(1))
    for b in LEVELS:
        put(f"level{b}", level(b))
    return c


def by_feature(a):
    return np.ascontiguousarray(a.reshape(-1, P).T)


def tokens_by_feature(a):
    return np.ascontiguousarray(a.T.reshape(-1, P, a.shape[0]).transpose(1, 0, 2))


def kernel(**inputs):
    import concourse.bacc as bacc
    from concourse.bass_utils import run_bass_kernel_spmd

    x = {k: np.asarray(v) for k, v in inputs.items()}
    mu = x["mu_rwkv_2"]

    def lora_column(a):
        return np.concatenate([a, np.zeros(P - LORA, a.dtype)]).reshape(P, 1)
    pieces = {
        "c": by_feature(x["c"]), "b_ada": by_feature(x["b_ada"]), "g_mix": by_feature(x["g_mix"]),
        "g_ffn": by_feature(x["g_ffn"]), "g_final": by_feature(x["g_final"]), "conv_w": by_feature(x["conv_w"]),
        "conv_b": by_feature(x["conv_b"]), "g_pre_mix": by_feature(x["g_pre_mix_2"]), "g_post_mix": by_feature(x["g_post_mix_2"]),
        "g_pre_ffn": by_feature(x["g_pre_ffn_2"]), "g_post_ffn": by_feature(x["g_post_ffn_2"]),
        "conv_w2": by_feature(x["conv_w_2"]), "mu_rkv": by_feature(mu[:3 * W]), "mu_gd": by_feature(mu[3 * W + 2 * LORA:]),
        "mu_wd": lora_column(mu[3 * W:3 * W + LORA]), "mu_ad": lora_column(mu[3 * W + LORA:3 * W + 2 * LORA]),
        "w0": by_feature(x["w0_2"]), "a0": by_feature(x["a0_2"]), "k_k": by_feature(x["k_k_2"]), "k_a": by_feature(x["k_a_2"]),
        "r_k": by_feature(x["r_k_2"]), "ln_w": by_feature(x["ln_x_w_2"]), "ln_b": by_feature(x["ln_x_b_2"]),
        "conv_ffn": by_feature(x["conv_ffn_2"]),
    }
    arrays = {
        "params": np.ascontiguousarray(np.concatenate([pieces[n] for n, _ in PARAMS], axis=1)),
        "consts": constant_block(),
        "pos": np.ascontiguousarray(np.broadcast_to(x["positions"].reshape(1, T), (P, T))),
        "xT": tokens_by_feature(x["x"][0]), "metaT": tokens_by_feature(x["meta_tokens_2"]),
    }
    for name in ("w_in", "w_a", "w_b", "w_o", "w_ada", "w_up", "w_down"):
        arrays[name] = np.ascontiguousarray(x[name][0])
    for name in ("w_in_2", "w_decay_up_2", "a_up_2", "g_up_2", "w_out_2", "w_gate_up_2", "w_down_2"):
        arrays[name] = np.ascontiguousarray(x[name])
    nc = bacc.Bacc("TRN2", target_bir_lowering=False, num_devices=1)
    aps = {n: nc.dram_tensor(f"{n}_dram", a.shape, mybir.dt.from_np(a.dtype), kind="ExternalInput").ap() for n, a in arrays.items()}
    out = nc.dram_tensor("out_dram", (P, KD, T), F32, kind="ExternalOutput").ap()
    build(nc, aps, out)
    got = run_bass_kernel_spmd(nc, [{f"{n}_dram": a for n, a in arrays.items()}], core_ids=[0]).results[0]["out_dram"]
    return np.ascontiguousarray(got.transpose(2, 1, 0)).reshape(1, T, D)
```

```python
import math
from contextlib import ExitStack

import numpy as np

import concourse.bass as bass
from concourse import mybir

F32 = mybir.dt.float32
F32R = mybir.dt.float32r
I32 = mybir.dt.int32
ACT = mybir.ActivationFunctionType
ALU = mybir.AluOpType
AX = mybir.AxisListType.X

P = 128
D = 2048
WORK = 18432
KD = D // P
T = 256
META = 16
NT = META + T
F = 5632
KF = F // P
HD = 128
IDX_HEADS = 16
IDX_D = 64
TOPK = 64
UNIT = 256
KH = KD // 2
SLOT = KH * UNIT
NSLOT = 4
SBUF_START = 16512
HALO = 2
EPS = 1e-6
GN_EPS = 64e-5
DECAY_SCALE = math.exp(-0.5)
NEG = -1e30
UNSEEN = -1e38
TAKEN = -3e38
BIG = 1e30

L = 68
NC = NT // L
MID = L // 2
RH = 16
RN = 64
W = 1024
KW = W // P
LORA = 96
SB_OFF = 0
DSA_OFF = 3 * W
QI_OFF = 6 * W
KI_OFF = 7 * W
WI_OFF = KI_OFF + IDX_D
GATE_OFF = WI_OFF + IDX_HEADS
RW_OFF = 3 * W
LORA_OFF = RW_OFF + 3 * W
GD_OFF = LORA_OFF + 2 * LORA

PARAMS = [("c", KD), ("b_ada", 6 * KD), ("g_mix", KD), ("g_ffn", KD), ("g_final", KD),
          ("conv_w", 3 * 2 * KF), ("conv_b", 2 * KF),
          ("g_pre_mix", KD), ("g_post_mix", KD), ("g_pre_ffn", KD), ("g_post_ffn", KD),
          ("conv_w2", 3 * KW), ("mu_rkv", 3 * KW), ("mu_gd", 2), ("mu_wd", 1), ("mu_ad", 1),
          ("w0", KW), ("a0", KW), ("k_k", KW), ("k_a", KW), ("r_k", KW), ("ln_w", KW), ("ln_b", KW),
          ("conv_ffn", 3 * KF)]
LEVELS = [2, 4, 8, 16, 32, 64]
CONSTS = [("ident", P), ("tri", P), ("heads", P), ("past", 384), ("seen", 384), ("invf", 2), ("sign", 2),
          ("strict", L), ("incl", L), ("first", L)] + [(f"level{b}", L) for b in LEVELS]

STREAM = [("ada", 3, 32, 4, 1), ("sb", 4, 6, 3, 1), ("ki", 1, 2, 2, 3), ("qi", 1, 8, 4, 1), ("dsa", 4, 6, 3, 1),
          ("merge", 8, 6, 3, 1), ("wo", 4, 4, 4, 1), ("up", 11, 8, 4, 1), ("down", 11, 4, 4, 1),
          ("conv2", 4, 6, 3, 1), ("rkv", 3, 8, 4, 1), ("lora", 1, 4, 4, 2),
          ("mix2", 2, 8, 4, 1), ("up2", 11, 8, 4, 1), ("down2", 11, 4, 4, 1)]
PLAN = {p[0]: p for p in STREAM}
AFTER = {a[0]: b[0] for a, b in zip(STREAM, STREAM[1:])}


def offsets(table):
    at, where = 0, {}
    for name, width in table:
        where[name] = (at, at + width)
        at += width
    return where, at


def landed_before():
    count, before = [0] * NSLOT, {}
    for name, iters, units, slots, dmas in STREAM:
        before[name] = list(count)
        for s in range(slots):
            count[s] += 16 * dmas * iters * (units // slots)
    return before


def units_before():
    count, before = 0, {}
    for name, iters, units, _, _ in STREAM:
        if name != "ada":
            before[name] = count
            count += iters * units
    return before


def feature_major(w):
    return w.rearrange("(k p) n -> p k n", p=P)


def first(i):
    return isinstance(i, int) and i == 0


class Steps:

    def __init__(self, eng, sem):
        self.eng, self.sem, self.base, self.i, self.per, self.n = eng, sem, 0, 0, 0, 0

    def begin(self, i, per=None):
        if first(i) or (per is not None and self.per == 0):
            self.base, self.n = self.base + self.n, 0
        if first(i) and per is None:
            self.i, self.per = 0, 0
        else:
            self.i, self.per = i, self.n if per is None else per
        self.n = 0

    def end(self):
        assert self.per == 0 or self.n == self.per, (self.n, self.per)

    def leave(self, count):
        self.base, self.i, self.per, self.n = self.base + count * self.per, 0, 0, 0

    def mark(self, ins):
        self.n += 1
        ins.then_inc(self.sem, 1)

    def wait(self):
        self.eng.wait_ge(self.sem, self.base + self.i * self.per + self.n)

    def __call__(self, ins):
        self.mark(ins)
        self.wait()


def repeat(eng, count, body):
    body(0)
    if count > 1:
        with eng.Fori(1, count) as i:
            body(i)


def rotated(eng, count, body):
    body(0, count == 1)
    if count > 2:
        with eng.Fori(1, count - 1) as i:
            body(i, False)
    if count > 1:
        body(count - 1, True)


def build(nc, A, out):
    before, unit0 = landed_before(), units_before()
    with ExitStack() as ctx:
        cursor = [SBUF_START]

        def sb(name, shape, dt=F32, at=None):
            where = cursor[0] if at is None else at
            t = nc.alloc_sbuf_tensor_at(name, shape, dt, offset=where, align_bytes=32)
            if at is None:
                cursor[0] += -(-4 * int(np.prod(shape[1:])) // 32) * 32
            return t

        def sem(name):
            return ctx.enter_context(nc.semaphore(name))

        bank = ctx.enter_context(nc.psum_tensor("bank", [P, 8, 512], F32))
        ring = sb("ring", [P, NSLOT, SLOT])
        whi = sb("whi", [P, 2, SLOT], F32R)
        wlo = sb("wlo", [P, 2, SLOT], F32R)
        res = sb("res", [P, KD, NT])
        hhi_at = cursor[0]
        hhi = sb("hhi", [P, KD, NT], F32R)
        hlo_at = cursor[0]
        hlo = sb("hlo", [P, KD, NT], F32R)
        hT = sb("hraw", [P, KD, NT], at=hlo_at)
        fT = sb("fT", [P, KD, NT], at=hhi_at)
        pw, pwidth = offsets(PARAMS)
        cw, cwidth = offsets(CONSTS)
        params = sb("params", [P, pwidth])
        consts = sb("consts", [P, cwidth])
        ones = sb("ones", [P, P])
        cact = sb("cact", [P, KD])
        mod = sb("mod", [P, 6, KD])
        gain = sb("gain", [P, 2, KD])
        xhi_at = cursor[0]
        xhi = sb("xhi", [P, 2, 2 * NT], F32R)
        xlo_at = cursor[0]
        xlo = sb("xlo", [P, 2, 2 * NT], F32R)
        sq = sb("sq", [P, 2, NT], at=xhi_at)
        rms = sb("rms", [P, NT], at=xlo_at)
        epsc = sb("epsc", [P, 2])
        omu = sb("omu", [P, 28])
        omka = sb("omka", [P, KW])
        work_at = cursor[0]
        work = sb("work", [P, WORK])
        yhi_at = work_at + 4 * (2 * 8 + KD) * T
        yhi = sb("yhi", [P, KD, T], F32R, at=yhi_at)
        ylo = sb("ylo", [P, KD, T], F32R, at=yhi_at + 4 * KD * T)
        assert cursor[0] <= 229344, cursor

        def param(name, a=None, b=None):
            lo, hi = pw[name]
            return params[:, lo:hi] if a is None else params[:, lo + a:lo + (a + 1 if b is None else b)]

        def pcol(name, i):
            lo, _ = pw[name]
            return params[:, bass.ds(i + lo, 1)] if not isinstance(i, int) else params[:, lo + i:lo + i + 1]

        def const(name):
            lo, hi = cw[name]
            return consts[:, lo:hi]

        def carve(*shapes):
            at, views = 0, []
            for shape in shapes:
                n = int(np.prod(shape))
                v = work[:, at:at + n]
                if len(shape) == 2:
                    v = v.rearrange("p (a b) -> p a b", a=shape[0])
                if len(shape) == 3:
                    v = v.rearrange("p (a b c) -> p a b c", a=shape[0], b=shape[1])
                views.append(v)
                at += n
            assert at <= WORK, at
            return views

        def tile(t, i):
            return t[:, i, :] if isinstance(i, int) else t[:, bass.ds(i, 1), :].rearrange("p a n -> p (a n)")

        def weights(slot, k, n):
            return ring[:, slot, 0:k * n].rearrange("p (k n) -> p k n", k=k)

        def parts(u, k, n):
            return tuple(w[:, u % 2, 0:k * n].rearrange("p (k n) -> p k n", k=k) for w in (whi, wlo))

        params_in, consts_in, pos_in = sem("params_in"), sem("consts_in"), sem("pos_in")
        x_loaded = sem("x_loaded")
        landed = [sem(f"landed{s}") for s in range(NSLOT)]
        hi_done, lo_done, used = sem("hi_done"), sem("lo_done"), sem("used")
        x_hi, x_lo = sem("x_hi"), sem("x_lo")
        h_scaled, h_hi, h_lo = sem("h_scaled"), sem("h_hi"), sem("h_lo")
        y_hi, y_lo = sem("y_hi"), sem("y_lo")
        ada_used, ada_summed = sem("ada_used"), sem("ada_summed")
        lora_landed, gate_landed = sem("lora_landed"), sem("gate_landed")
        phase_done = sem("phase_done")
        act_step, dve_step, pool_step = sem("act_step"), sem("dve_step"), sem("pool_step")
        ones_set = sem("ones_set")
        stored = sem("stored")
        squared, summed, rooted, normed, shifted = (sem(n) for n in ("squared", "summed", "rooted", "normed", "shifted"))
        z_done, s_done, o_done, zm_done, sp_done, l_done, d_done, w_done = (
            sem(n) for n in ("z_done", "s_done", "o_done", "zm_done", "sp_done", "l_done", "d_done", "w_done"))
        q_read, k_read, v_read, q2_read, k2_read, v2_read = (
            sem(n) for n in ("q_read", "k_read", "v_read", "q2_read", "k2_read", "v2_read"))
        angle_done, sines, dots_done, relu_done, relu_used = (
            sem(n) for n in ("angle_done", "sines", "dots_done", "relu_done", "relu_used"))
        logits_done, max_done, exp_done, probs_done, turned, turned_read, o2_done = (
            sem(n) for n in ("logits_done", "max_done", "exp_done", "probs_done", "turned", "turned_read", "o2_done"))
        merge_read = [sem(f"merge_read{s}") for s in range(4)]
        merged, tap_done, silu_done, acted = sem("merged"), sem("tap_done"), sem("silu_done"), sem("acted")
        cact_ready = sem("cact_ready")
        meta_loaded, result_ready = sem("meta_loaded"), sem("result_ready")
        c_copied, own_done, lora_ready, tap2_done, silu2_done = (
            sem(n) for n in ("c_copied", "own_done", "lora_ready", "tap2_done", "silu2_done"))
        kk_squared, kk_summed, kk_floored, kk_rooted = (sem(n) for n in ("kk_squared", "kk_summed", "kk_floored", "kk_rooted"))
        cum_done, exps_done, feat_done, n_raw, g0_done, t0_raw, t0_ready, nm_ready, w1_raw, w1_ready, tg_raw, tg_ready = (
            sem(n) for n in ("cum_done", "exps_done", "feat_done", "n_raw", "g0_done", "t0_raw", "t0_ready", "nm_ready",
                             "w1_raw", "w1_ready", "tg_raw", "tg_ready"))
        task_done, tok_read, mat_read, x_raw, x_ready, u_raw, u_ready, h_raw, h_ready, y_raw, pair_done = (
            sem(n) for n in ("task_done", "tok_read", "mat_read", "x_raw", "x_ready", "u_raw", "u_ready", "h_raw", "h_ready",
                             "y_raw", "pair_done"))
        mean_raw, centred, y_squared, var_raw, var_read, gate_tiles = (
            sem(n) for n in ("mean_raw", "centred", "y_squared", "var_raw", "var_read", "gate_tiles"))
        loraup_tiles, loraup_evac = sem("loraup_tiles"), sem("loraup_evac")
        evac = {n: sem(f"{n}_evac") for n, *_ in STREAM}

        def arrived(eng, phase, u, i):
            _, _, units, slots, dmas = PLAN[phase]
            n = 16 * dmas
            eng.wait_ge(landed[u % slots], before[phase][u % slots] + n * (u // slots + 1) + i * (n * (units // slots)))

        def number(phase, u, i):
            return i * PLAN[phase][2] + (unit0[phase] + u)

        def multiplied(eng, phase, u, i):
            eng.wait_ge(used, number(phase, u, i) + 1)

        def round_unit(phase, u, i, n=SLOT):
            arrived(nc.scalar, phase, u, i)
            if unit0[phase] or u >= 2 or not isinstance(i, int) or i:
                nc.scalar.wait_ge(used, number(phase, u, i) - 1)
            nc.scalar.activation(whi[:, u % 2, 0:n], ring[:, u % PLAN[phase][3], 0:n], ACT.Copy).then_inc(hi_done, 1)

        def rest_unit(phase, u, i, n=SLOT):
            nc.vector.wait_ge(hi_done, number(phase, u, i) + 1)
            nc.vector.tensor_tensor(wlo[:, u % 2, 0:n], ring[:, u % PLAN[phase][3], 0:n], whi[:, u % 2, 0:n].bitcast(F32),
                                    ALU.subtract).then_inc(lo_done, 1)

        def is_split(pe, phase, u, i):
            pe.wait_ge(lo_done, number(phase, u, i) + 1)

        KI_N = KH * 144

        def ahead(split, phase, i, last):
            for u in range(2):
                if last:
                    if phase in AFTER:
                        split(AFTER[phase], u, 0, *((KI_N,) if AFTER[phase] == "ki" else ()))
                else:
                    split(phase, u, i + 1)

        X_PHASES = ("wo", "down", "mix2", "down2")
        xunit0, n_x = {}, 0
        for name in X_PHASES:
            xunit0[name] = n_x
            n_x += PLAN[name][1] * PLAN[name][2]

        def x_number(phase, u, i):
            return i * PLAN[phase][2] + (xunit0[phase] + u)

        def x_buf(t, u, n):
            return t[:, u % 2, 0:n]

        def round_x(phase, u, i, srcs):
            if isinstance(i, int) and i == 0 and u < 2:
                pass
            else:
                nc.scalar.wait_ge(used, number(phase, u, i) - 1)
            at = 0
            for src in srcs:
                n = src.shape[-1]
                last = nc.scalar.activation(xhi[:, u % 2, at:at + n], src, ACT.Copy)
                at += n
            last.then_inc(x_hi, 1)

        def rest_x(phase, u, i, srcs):
            nc.vector.wait_ge(x_hi, x_number(phase, u, i) + 1)
            at = 0
            for src in srcs:
                n = src.shape[-1]
                last = nc.vector.tensor_tensor(xlo[:, u % 2, at:at + n], src, xhi[:, u % 2, at:at + n].bitcast(F32), ALU.subtract)
                at += n
            last.then_inc(x_lo, 1)

        def threefold(out_ap, a, b, start, stop):
            kw = dict(skip_group_check=True)
            nc.tensor.matmul(out_ap, a[0], b[0], start=start, stop=False, **kw)
            nc.tensor.matmul(out_ap, a[0], b[1], start=False, stop=False, **kw)
            return nc.tensor.matmul(out_ap, a[1], b[0], start=False, stop=stop, **kw)

        def products(out_ap, pairs, **kw):
            last = None
            for n, (a, b) in enumerate(pairs):
                last = nc.tensor.matmul(out_ap, a, b, start=n == 0, stop=n == len(pairs) - 1, **kw)
            return last

        ends = [0]

        (yaT, ybT, mergedT, qT, kT, vS, s_a, s_b, s_c, s_d, s_e, s_f, small, biasM, tabs128, tabs64) = carve(
            (8, T), (8, T), (KD, T), (2, T), (2, T), (2, T),
            (2, 384), (2, 384), (2, 384), (2, 384), (2, 384), (2, 384), (1, 64), (1, 384), (2, 2 * T), (2, T))
        ropeA = mergedT[:, 0:2, :].rearrange("p a t -> p (a t)")
        ropeB = mergedT[:, 2:4, :].rearrange("p a t -> p (a t)")
        angles = mergedT[:, 4:8, :]
        turns = mergedT[:, 8:12, :]
        qiT = mergedT[:, 4:12, :]
        kiT = mergedT[:, 12, :]
        relu = mergedT[:, 13:16, :].rearrange("p a t -> p (a t)")
        posf = mergedT[:, 12, :]
        posi = mergedT[:, 13, :].bitcast(I32)
        small = small[:, 0, :]
        acc = work[:, 0:2 * D].rearrange("p (b n) -> p b n", b=2)
        past, seen = const("past"), const("seen")
        gates_at = 2 * 8 * T + KD * T + 2 * KD * T
        gates = work[:, gates_at:gates_at + 4 * T].rearrange("p (a t) -> p a t", a=4)
        gated = work[:, gates_at + 4 * T:gates_at + 8 * T].rearrange("p (a t) -> p a t", a=4)
        actT, cv, sa = carve((KF, T), (8, NT), (4, T))
        yconv, zr, lw, aa, kk, gd, NM, tokK, tokB, tokV = carve(
            (KW, NT), (3 * KW, NT), (KW, NT), (KW, NT), (KW, NT), (2, NT), (2, 2 * NT), (NC, P), (NC, P), (NC, P))
        low = hT[:].rearrange("p k t -> p (k t)")
        TT, G, N, W1, lak, lrk, lrb = (low[:, n * 2 * NT:(n + 1) * 2 * NT].rearrange("p (a t) -> p a t", a=2) for n in range(7))
        XU = low[:, 14 * NT:14 * NT + 2 * P].rearrange("p (a t) -> p a t", a=2)
        Xs, Us = XU[:, 0, :], XU[:, 1, :]
        cs, chs, ycs = carve((KW, NT), (3 * KW, NT), (2, NT), (2, NT + HALO), (2, NT))[2:]
        wdad = carve((KW, NT), (3 * KW, NT), (KW, NT), (KW, NT), (KW, NT), (2, NT), (2, NT))[6]
        temp8, temp8b = fT[:, 0:KW, :], fT[:, KW:KD, :]
        cum, cumc, cpm, Ep, Em, Epm, k2, bb, kt, bt, rkr, vt = (fT[:, k, :] for k in range(12))
        hflat = fT[:].rearrange("p k t -> p (k t)")
        AR = hflat[:, 12 * NT:14 * NT].rearrange("p (c a t) -> p c a t", c=NC, a=2)
        Hs = hflat[:, 14 * NT:14 * NT + 2 * RN].rearrange("p (a v) -> p a v", a=2)
        Hsum = hflat[:, 14 * NT + 2 * RN:14 * NT + 3 * RN]
        ecm = hflat[:, 14 * NT + 3 * RN:14 * NT + 3 * RN + NC]
        mids = hflat[:, 14 * NT + 3 * RN + 8:14 * NT + 3 * RN + 8 + NC]
        onesrow = ones[:, 0:L]

        def all8(x):
            return x.rearrange("p a t -> p (a t)")
        SCALE = HD ** -0.5

        block = ctx.enter_context(nc.Block())

        def phase_end(eng, n):
            eng.drain().then_inc(phase_done, 1)
            eng.wait_ge(phase_done, 3 * n)

        @block.sync
        def _(sp):
            sp.dma_start(params[:], A["params"]).then_inc(params_in, 16)
            sp.dma_start(consts[:], A["consts"]).then_inc(consts_in, 16)
            sp.dma_start(res[:, :, META:NT], A["xT"]).then_inc(x_loaded, 16)
            sp.dma_start(posi, A["pos"]).then_inc(pos_in, 16)
            free = [None] * NSLOT

            def phase(name, units):
                _, count, per, slots, _ = PLAN[name]

                def read(u, i):
                    return (ada_used, i * per + (u + 1)) if name == "ada" else (lo_done, number(name, u, i) + 1)

                def body(i):
                    for u in range(per):
                        if first(i) and u < slots:
                            if free[u] is not None:
                                sp.wait_ge(*free[u])
                        else:
                            sp.wait_ge(*read(u - slots, i))
                        for dst, src in units(u, i):
                            sp.dma_start(dst, src).then_inc(landed[u % slots], 16)
                repeat(sp, count, body)
                for s in range(slots):
                    free[s] = read(per - slots + s, count - 1)

            def half_unit(w, slot, u, col):
                lo = (u % 2) * KH if w.shape[0] > W else 0
                v = feature_major(w)[:, lo:lo + KH, :]
                v = v[:, :, col:col + UNIT] if isinstance(col, int) else v[:, :, bass.ds(col, UNIT)]
                return [(weights(slot, KH, UNIT), v)]

            def halves_of(name, w, col0, step):
                slots = PLAN[name][3]
                return lambda u, i: half_unit(w, u % slots, u, col0(u // 2) + i * step)

            def row_units(w):
                def units(u, i):
                    row = i * 4 + u
                    v = feature_major(w)
                    v = v[:, row:row + 1, :] if isinstance(row, int) else v[:, bass.ds(row, 1), :]
                    return [(weights(u, 1, D), v)]
                return units

            def ada_units(u, i):
                v = feature_major(A["w_ada"])[:, u % KD:u % KD + 1, :]
                col = i * (2 * D) + (u // KD) * D
                return [(weights(u % NSLOT, 1, D), v[:, :, col:col + D] if isinstance(col, int) else v[:, :, bass.ds(col, D)])]
            phase("ada", ada_units)
            phase("sb", halves_of("sb", A["w_in"], lambda s: SB_OFF + s * W, UNIT))
            wv = feature_major(A["w_in"])

            def ki_units(u, i):
                w144, k = weights(u, KH, 144), slice(u * KH, (u + 1) * KH)
                return [(w144[:, :, 0:64], wv[:, k, KI_OFF:KI_OFF + IDX_D]),
                        (w144[:, :, 64:128], wv[:, k, KI_OFF:KI_OFF + IDX_D]),
                        (w144[:, :, 128:144], wv[:, k, WI_OFF:WI_OFF + IDX_HEADS])]
            phase("ki", ki_units)
            phase("qi", halves_of("qi", A["w_in"], lambda s: QI_OFF + s * UNIT, 0))
            phase("dsa", halves_of("dsa", A["w_in"], lambda s: DSA_OFF + s * W, UNIT))

            def merge_units(u, i):
                if u < 2:
                    return half_unit(A["w_a"] if u == 0 else A["w_b"], u, u, i * UNIT)
                return half_unit(A["w_in"], u % 3, u, i * UNIT + (GATE_OFF + (u // 2 - 1) * D))
            phase("merge", merge_units)
            phase("wo", row_units(A["w_o"]))

            def up_units(name, w):
                return halves_of(name, w, lambda s: (s % 2) * F + (s // 2) * UNIT, 2 * UNIT)
            phase("up", up_units("up", A["w_up"]))
            phase("down", row_units(A["w_down"]))
            w2 = A["w_in_2"]
            phase("conv2", halves_of("conv2", w2, lambda s: s * W, UNIT))
            phase("rkv", halves_of("rkv", w2, lambda s: RW_OFF + s * UNIT, W))

            def lora_units(u, i):
                k = slice((u % 2) * KH, (u % 2 + 1) * KH)
                cols = (GD_OFF, GD_OFF + P) if u < 2 else (LORA_OFF, LORA_OFF + LORA)
                return [(weights(u, KH, UNIT)[:, :, t * P:(t + 1) * P], feature_major(w2)[:, k, c:c + P])
                        for t, c in enumerate(cols)]
            phase("lora", lora_units)
            sp.wait_ge(*free[2])
            sp.dma_start(ring[0:LORA, 2, 0:W], A["w_decay_up_2"]).then_inc(lora_landed, 16)
            sp.dma_start(ring[0:LORA, 2, W:2 * W], A["a_up_2"]).then_inc(lora_landed, 16)
            sp.wait_ge(*free[3])
            sp.dma_start(weights(3, 2, W), feature_major(A["g_up_2"])).then_inc(gate_landed, 16)
            free[2], free[3] = (loraup_tiles, 2 * KW), (gate_tiles, KW)

            def mix_units(u, i):
                v = feature_major(A["w_out_2"])[:, 2 * u:2 * u + 2, :]
                return [(weights(u % NSLOT, 2, W), v[:, :, i * W:(i + 1) * W])]
            phase("mix2", mix_units)
            phase("up2", up_units("up2", A["w_gate_up_2"]))
            phase("down2", row_units(A["w_down_2"]))
            sp.wait_ge(result_ready, 1)
            sp.dma_start(out, res[:, :, META:NT]).then_inc(stored, 16)
            sp.wait_ge(stored, 16)

        norms = {"act": 0, "pe": 0, "dve": 0}

        def norm_act(act, src, n, step):
            m = norms["act"]
            norms["act"] += 1
            for k in range(KD):
                if k >= 2 or m:
                    act.wait_ge(summed, KD * m + k - 1)
                nc.scalar.activation(sq[:, k % 2, 0:n], src[:, k, :], ACT.Square).then_inc(squared, 1)
            act.wait_ge(summed, KD * (m + 1))
            nc.scalar.activation(rms[:, 0:n], bank[:, 0, 0:n], ACT.Sqrt, scale=1.0 / D, bias=epsc[:, 0:1]).then_inc(rooted, 1)

        def norm_pe(pe, n):
            m = norms["pe"]
            norms["pe"] += 1
            for k in range(KD):
                pe.wait_ge(squared, KD * m + k + 1)
                nc.tensor.matmul(bank[:, 0, 0:n], ones[:], sq[:, k % 2, 0:n], start=k == 0, stop=k == KD - 1)\
                    .then_inc(summed, 1)

        def norm_dve(dve, n, step, apply):
            m = norms["dve"]
            norms["dve"] += 1
            dve.wait_ge(rooted, m + 1)
            step(nc.vector.reciprocal(rms[:, 0:n], rms[:, 0:n]))
            for k in range(KD):
                last = apply(k)
            step(last)

        def scaled(dst, src, g, n):
            return lambda k: nc.vector.scalar_tensor_tensor(
                dst[:, k, :], src[:, k, :], g[:, k:k + 1], rms[:, 0:n], ALU.mult, ALU.mult)

        handed = {"act": 0, "dve": 0}

        def hand_act(n, shift=None):
            m = handed["act"]
            handed["act"] += 1
            for k in range(KD):
                nc.scalar.wait_ge(h_scaled, KD * m + k + 1)
                if shift is None:
                    ins = nc.scalar.activation(hhi[:, k, 0:n], hT[:, k, 0:n], ACT.Copy)
                else:
                    ins = nc.scalar.activation(hhi[:, k, 0:n], hT[:, k, 0:n], ACT.Identity, bias=shift[:, k:k + 1])
                ins.then_inc(h_hi, 1)

        def hand_dve(src, g, n, shift=None):
            m = handed["dve"]
            handed["dve"] += 1
            for k in range(KD):
                nc.vector.scalar_tensor_tensor(hT[:, k, 0:n], src[:, k, :], g[:, k:k + 1], rms[:, 0:n], ALU.mult, ALU.mult)\
                    .then_inc(h_scaled, 1)
            for k in range(KD):
                nc.vector.wait_ge(h_hi, KD * m + k + 1)
                nc.vector.scalar_tensor_tensor(hlo[:, k, 0:n], hT[:, k, 0:n], 0.0 if shift is None else shift[:, k:k + 1],
                                               hhi[:, k, 0:n].bitcast(F32), ALU.add, ALU.subtract).then_inc(h_lo, 1)

        def norm_dve_handing(dve, src, g, n, step, shift=None):
            m = norms["dve"]
            norms["dve"] += 1
            dve.wait_ge(rooted, m + 1)
            step(nc.vector.reciprocal(rms[:, 0:n], rms[:, 0:n]))
            hand_dve(src, g, n, shift)

        x1 = res[:, :, META:NT]
        h1 = (hhi[:, :, 0:T], hlo[:, :, 0:T])

        @block.tensor
        def _(pe):
            def ada(i):
                for b in range(2):
                    pe.wait_ge(ada_used, i * 2 * KD + (b + 1) * KD)
                    for m in range(KD):
                        col = i * 2 * KD + (b * KD + m)
                        dst = bank[:, 0, col:col + 1] if isinstance(i, int) else bank[:, 0, bass.ds(col, 1)]
                        last = nc.tensor.matmul(dst, acc[:, b, m * P:(m + 1) * P], ones[:, 0:1], start=True, stop=True)
                    last.then_inc(ada_summed, 1)
            pe.wait_ge(ones_set, 1)
            repeat(pe, 3, ada)
            phase_end(pe, 1)
            pe.wait_ge(consts_in, 16)
            norm_pe(pe, T)
            phase_end(pe, 2)

            def project(phase, n, i, token_major, dst):
                for half in range(2):
                    is_split(pe, phase, 2 * n + half, i)
                    w = parts(half, KH, UNIT)
                    for t in range(2):
                        tt = slice(t * P, (t + 1) * P)
                        for k in range(KH):
                            kk_ = half * KH + k
                            if token_major:
                                a, b = [x[:, kk_, tt] for x in h1], [x[:, k, :] for x in w]
                            else:
                                a, b = [x[:, k, tt] for x in w], [x[:, kk_, :] for x in h1]
                            last = threefold(bank[:, dst, t * T:(t + 1) * T], a, b, half == 0 and t == 0 and k == 0,
                                             half == 1 and k == KH - 1)
                    last.then_inc(used, 1)

            def attend_values(e, probs):
                o = bank[:, 3, e * T:(e + 1) * T]
                nc.tensor.matmul(o, vS[:, 0, e * HD:(e + 1) * HD], probs[:, e, 0:T], start=True, stop=False)
                return nc.tensor.matmul(o[:, P:T], vS[:, 1, e * HD:(e + 1) * HD], probs[:, e, T:384], start=False, stop=True)

            def sb(i, head=True, tail=True):
                if head:
                    if not first(i):
                        pe.wait_ge(q_read, i)
                    project("sb", 0, i, False, 0)
                if tail:
                    pe.wait_ge(q_read, i)
                    pe.wait_ge(k_read, i)
                    for e in range(2):
                        z = bank[:, 4 + e, :]
                        nc.tensor.matmul(z[:, 0:T], kT[:, e, 0:P], qT[:, e, :], start=True, stop=True)
                        nc.tensor.matmul(z[:, T:384], kT[:, e, P:T], qT[:, e, P:T], start=True, stop=True)\
                            .then_inc(z_done, 1)
                if head:
                    project("sb", 1, i, False, 1)
                if tail:
                    for e in range(2):
                        pe.wait_ge(sp_done, i * 2 + (e - 1))
                        sp_ = s_e[:, e, :]
                        nc.tensor.matmul(bank[:, 6 + e, 0:T], const("tri"), sp_[:, 0:T], start=True, stop=False)
                        nc.tensor.matmul(bank[:, 6 + e, P:T], ones[:], sp_[:, T:384], start=False, stop=True)
                        nc.tensor.matmul(bank[:, 6 + e, T:384], const("tri"), sp_[:, T:384], start=True, stop=True)\
                            .then_inc(s_done, 1)
                if head:
                    if not first(i):
                        pe.wait_ge(v_read, i)
                    project("sb", 2, i, True, 2)
                if tail:
                    pe.wait_ge(v_read, i)
                    for e in range(2):
                        pe.wait_ge(w_done, i * 2 + (e - 1))
                        attend_values(e, s_f).then_inc(o_done, 1)

            def overlapped(body, count):
                body(0, tail=False)
                with pe.Fori(1, count) as i:
                    body(i)
                body(count, head=False)
            overlapped(sb, 4)
            phase_end(pe, 3)

            for half in range(2):
                is_split(pe, "ki", half, 0)
                w = parts(half, KH, 144)
                for k in range(KH):
                    threefold(bank[:, 6, 0:T], [x[:, k, 0:P] for x in w], [x[:, half * KH + k, :] for x in h1],
                              half == 0 and k == 0, half == 1 and k == KH - 1)
                for t in range(2):
                    for k in range(KH):
                        last = threefold(bank[:, 7, t * IDX_HEADS:(t + 1) * IDX_HEADS],
                                         [x[:, half * KH + k, t * P:(t + 1) * P] for x in h1], [x[:, k, P:144] for x in w],
                                         half == 0 and t == 0 and k == 0, half == 1 and k == KH - 1)
                last.then_inc(used, 1)

            def pair_of_tiles(phase, s, i, rhs, width, free):
                for half in range(2):
                    is_split(pe, phase, 2 * s + half, i)
                    w = parts(half, KH, UNIT)
                    for t in range(2):
                        q = 2 * s + t
                        if half == 0:
                            free(q)
                        for k in range(KH):
                            last = threefold(bank[:, q, 0:width], [x[:, k, t * P:(t + 1) * P] for x in w],
                                             [x[:, half * KH + k, :] for x in rhs], half == 0 and k == 0,
                                             half == 1 and k == KH - 1)
                    last.then_inc(used, 1)

            for s in range(4):
                pair_of_tiles("qi", s, 0, h1, T, lambda q: pe.wait_ge(evac["ki"], 2) if q == 6 else None)
            for h in range(IDX_HEADS):
                j, e = h // 2, 64 * (h % 2)
                if h < 8:
                    pe.wait_ge(evac["qi"], 8)
                    pe.wait_ge(evac["ki"], 2)
                else:
                    pe.wait_ge(relu_done, h - 7)
                d = bank[:, h % 8, :]
                nc.tensor.matmul(d[:, 0:P], qiT[e:e + 64, j, 0:P], kiT[e:e + 64, 0:P], start=True, stop=True)
                nc.tensor.matmul(d[:, P:384], qiT[e:e + 64, j, P:T], kiT[e:e + 64, :], start=True, stop=True)\
                    .then_inc(dots_done, 1)
            phase_end(pe, 4)

            def dsa(i, head=True, tail=True):
                if head:
                    if not first(i):
                        pe.wait_ge(q2_read, i)
                    project("dsa", 0, i, False, 0)
                if tail:
                    pe.wait_ge(q2_read, i)
                    pe.wait_ge(k2_read, i)
                    for e in range(2):
                        z = bank[:, 4 + e, :]
                        nc.tensor.matmul(z[:, 0:P], qT[:, e, 0:P], kT[:, e, 0:P], start=True, stop=True)
                        nc.tensor.matmul(z[:, P:384], qT[:, e, P:T], kT[:, e, :], start=True, stop=True)\
                            .then_inc(logits_done, 1)
                if head:
                    project("dsa", 1, i, False, 1)
                if tail:
                    for e in range(2):
                        pe.wait_ge(probs_done, i * 2 + (e - 1))
                        for n in range(3):
                            last = nc.tensor.transpose(bank[:, 6 + e, n * P:(n + 1) * P], s_c[:, e, n * P:(n + 1) * P],
                                                       const("ident"))
                        last.then_inc(turned, 1)
                if head:
                    if not first(i):
                        pe.wait_ge(v2_read, i)
                    project("dsa", 2, i, True, 2)
                if tail:
                    pe.wait_ge(v2_read, i)
                    for e in range(2):
                        pe.wait_ge(turned_read, i * 2 + (e - 1))
                        attend_values(e, s_f).then_inc(o2_done, 1)
            overlapped(dsa, 4)
            phase_end(pe, 5)

            pe.wait_ge(y_lo, 1)

            def merge(i):
                def free(q):
                    if not first(i):
                        pe.wait_ge(merge_read[q // 2], i * 2 + (q % 2 - 1))
                for s in range(2):
                    is_split(pe, "merge", s, i)
                    w = parts(s, KW, UNIT)
                    for t in range(2):
                        free(2 * s + t)
                        for k in range(KW):
                            last = threefold(bank[:, 2 * s + t, 0:T], [x[:, k, t * P:(t + 1) * P] for x in w],
                                             [x[:, s * KW + k, :] for x in (yhi, ylo)], k == 0, k == KW - 1)
                    last.then_inc(used, 1)
                for s in (2, 3):
                    for half in range(2):
                        is_split(pe, "merge", 2 * s - 2 + half, i)
                        w = parts(half, KH, UNIT)
                        for t in range(2):
                            if half == 0:
                                free(2 * s + t)
                            for k in range(KH):
                                last = threefold(bank[:, 2 * s + t, 0:T], [x[:, k, t * P:(t + 1) * P] for x in w],
                                                 [x[:, half * KH + k, :] for x in h1], half == 0 and k == 0,
                                                 half == 1 and k == KH - 1)
                        last.then_inc(used, 1)
            repeat(pe, 8, merge)
            phase_end(pe, 6)

            def linear(phase, src, free=None):
                _, count, per, _, _ = PLAN[phase]

                def body(i):
                    def bank_free(q):
                        if not first(i):
                            if free:
                                free(i, q)
                            else:
                                pe.wait_ge(evac[phase], i * per + (q + 1 - per))
                    for s in range(per // 2):
                        pair_of_tiles(phase, s, i, *src(s), bank_free)
                repeat(pe, count, body)

            def by_rows(phase):
                _, count, per, _, _ = PLAN[phase]

                def body(i):
                    for u in range(per):
                        is_split(pe, phase, u, i)
                        pe.wait_ge(x_lo, x_number(phase, u, i) + 1)
                        b = [x_buf(x, u, T) for x in (xhi, xlo)]
                        for m in range(KD):
                            last = threefold(bank[:, m // 2, (m % 2) * T:(m % 2 + 1) * T],
                                             [x[:, u % 2, m * P:(m + 1) * P] for x in (whi, wlo)], b,
                                             first(i) and u == 0 and m % 2 == 0, False)
                        last.then_inc(used, 1)
                repeat(pe, count, body)

            by_rows("wo")
            phase_end(pe, 7)
            norm_pe(pe, T)
            phase_end(pe, 8)
            linear("up", lambda s: (h1, T))
            phase_end(pe, 9)
            by_rows("down")
            phase_end(pe, 10)
            norm_pe(pe, T)
            phase_end(pe, 11)

            norm_pe(pe, NT)
            phase_end(pe, 12)
            hboth = (hhi, hlo)
            linear("conv2", lambda s: (hboth, NT), free=lambda i, q: pe.wait_ge(evac["conv2"], i * 2 + (q % 2 - 1)))
            phase_end(pe, 13)
            linear("rkv", lambda s: (hboth, NT))
            phase_end(pe, 14)
            linear("lora", lambda s: (hboth, NT))
            pe.wait_ge(lora_landed, 32)
            pe.wait_ge(lora_ready, 2)
            for u in range(2):
                for j in range(KW):
                    if u == 0:
                        if j == 0:
                            pe.wait_ge(evac["lora"], 4)
                    else:
                        pe.wait_ge(loraup_evac, j + 1)
                    nc.tensor.matmul(bank[:, j, 0:NT], ring[0:LORA, 2, u * W + j * P:u * W + (j + 1) * P],
                                     wdad[0:LORA, u, :], start=True, stop=True).then_inc(loraup_tiles, 1)
            for j in range(KW):
                pe.wait_ge(kk_squared, 1)
                pe.wait_ge(loraup_evac, KW + j + 1)
                nc.tensor.matmul(bank[:, j, 0:NT], const("heads"), temp8[:, j, :], start=True, stop=True).then_inc(kk_summed, 1)
            phase_end(pe, 15)

            def chunk(x, c):
                return x[:, c * L:(c + 1) * L]

            def recur(i):
                rows = [slice(0, RN), slice(RN, P)]

                def task(n):
                    b = 6 + n % 2
                    if n in (2, 3, 4):
                        pe.wait_ge(tok_read, i * 3 + (n - 1))
                    if n > 4:
                        pe.wait_ge(mat_read, i * 7 + (n - 4))
                    if n < 3:
                        src = (kt, bt, vt)[n]
                        for c in range(NC):
                            last = nc.tensor.transpose(bank[0:L, b, c * P:(c + 1) * P], chunk(src, c), const("ident"))
                    elif n < 9:
                        kind, e = (n - 3) // 2, (n - 3) % 2
                        lhs, which = ((kt, 0), (kt, 1), (bt, 1))[kind]
                        for c in range(NC):
                            last = nc.tensor.matmul(bank[0:L, b, c * L:(c + 1) * L], chunk(lhs, c)[rows[e], :],
                                                    AR[rows[e], c, which, :], start=True, stop=True)
                    else:
                        last = nc.tensor.matmul(bank[:, b, 0:NT], const("heads"), rkr, start=True, stop=True)
                    last.then_inc(task_done, 1)

                pe.wait_ge(feat_done, i + 1)
                for e in range(2):
                    for c in range(NC):
                        last = nc.tensor.matmul(bank[0:L, e, c * L:(c + 1) * L], chunk(bt, c)[rows[e], :],
                                                AR[rows[e], c, 0, :], start=True, stop=True)
                    last.then_inc(n_raw, 1)
                for e in range(2):
                    pe.wait_ge(g0_done, i * 2 + (e + 1))
                    for c in range(NC):
                        last = nc.tensor.transpose(bank[0:L, 2 + e, c * L:(c + 1) * L], G[0:L, e, c * L:(c + 1) * L],
                                                   const("ident")[0:L, 0:L])
                    last.then_inc(t0_raw, 1)
                nl = len(LEVELS)
                for l in range(nl):
                    for e in range(2):
                        pe.wait_ge(nm_ready, i * 2 * nl + (2 * l + e + 1))
                        if l == 0:
                            pe.wait_ge(t0_ready, i * 2 + (e + 1))
                        else:
                            pe.wait_ge(tg_ready, i * 2 * nl + (2 * (l - 1) + e + 1))
                        for c in range(NC):
                            cc = slice(c * L, (c + 1) * L)
                            last = nc.tensor.matmul(bank[0:L, e, cc], NM[0:L, l % 2, e * NT + c * L:e * NT + (c + 1) * L],
                                                    TT[0:L, e, cc], start=True, stop=True)
                        last.then_inc(w1_raw, 1)
                        if 2 * l + e < 10:
                            task(2 * l + e)
                    for e in range(2):
                        pe.wait_ge(w1_ready, i * 2 * nl + (2 * l + e + 1))
                        for c in range(NC):
                            cc = slice(c * L, (c + 1) * L)
                            if l < nl - 1:
                                nc.tensor.matmul(bank[0:L, 2 + e, cc], G[0:L, e, cc], W1[0:L, e, cc], start=True, stop=True)
                        for c in range(NC):
                            cc = slice(c * L, (c + 1) * L)
                            last = nc.tensor.matmul(bank[0:L, 4 + e, cc], W1[0:L, e, cc], G[0:L, e, cc], start=True, stop=True)
                        last.then_inc(tg_raw, 1)
                pe.wait_ge(tg_ready, i * 2 * nl + 2 * nl)
                pe.wait_ge(mat_read, i * 7 + 7)
                for c in range(NC):
                    cc = slice(c * L, (c + 1) * L)
                    H = Hs[:, c % 2, :]
                    for e in range(2):
                        v = tokV[0:L, c, e * RN:(e + 1) * RN]
                        last = nc.tensor.matmul(bank[0:L, e, 0:RN], lak[0:L, e, cc], v, start=True, stop=c == 0)
                        if c:
                            if e == 0:
                                pe.wait_ge(h_ready, i * 3 + c)
                            last = nc.tensor.matmul(bank[0:L, e, 0:RN], AR[rows[e], c, 0, :], H[rows[e], :],
                                                    start=False, stop=True)
                    last.then_inc(x_raw, 1)
                    pe.wait_ge(x_ready, i * NC + (c + 1))
                    for e in range(2):
                        last = nc.tensor.matmul(bank[0:L, 2, e * RN:(e + 1) * RN], G[0:L, e, cc], Xs[0:L, e * RN:(e + 1) * RN],
                                                start=True, stop=True)
                    last.then_inc(u_raw, 1)
                    pe.wait_ge(u_ready, i * NC + (c + 1))
                    if c < NC - 1:
                        for e in range(2):
                            ee = slice(e * RN, (e + 1) * RN)
                            nc.tensor.matmul(bank[rows[e], 3, 0:RN], tokK[0:L, c, ee], tokV[0:L, c, ee], start=True, stop=False)
                            last = nc.tensor.matmul(bank[rows[e], 3, 0:RN], tokB[0:L, c, ee], Us[0:L, ee], start=False, stop=True)
                        last.then_inc(h_raw, 1)
                    for e in range(2):
                        ee = slice(e * RN, (e + 1) * RN)
                        nc.tensor.matmul(bank[rows[e], 4 + e, cc], tokV[0:L, c, ee], lrk[0:L, e, cc], start=True, stop=False)
                        if c:
                            nc.tensor.matmul(bank[rows[e], 4 + e, cc], H[rows[e], :], AR[rows[e], c, 1, :], start=False, stop=False)
                        last = nc.tensor.matmul(bank[rows[e], 4 + e, cc], Us[0:L, ee], lrb[0:L, e, cc], start=False, stop=True)
                last.then_inc(y_raw, 1)
            repeat(pe, KW, recur)
            phase_end(pe, 16)

            for j in range(KW):
                nc.tensor.matmul(bank[:, j, 0:NT], const("heads"), zr[:, j, :], start=True, stop=True).then_inc(mean_raw, 1)
            for j in range(KW):
                pe.wait_ge(y_squared, j + 1)
                nc.tensor.matmul(bank[:, j, 0:NT], const("heads"), kk[:, j, :], start=True, stop=True).then_inc(var_raw, 1)
            pe.wait_ge(gate_landed, 16)
            gup = ring[:, 3, 0:2 * W].rearrange("p (k n) -> p k n", k=2)
            for j in range(KW):
                pe.wait_ge(var_read, j + 1)
                products(bank[:, j, 0:NT], [(gup[:, k, j * P:(j + 1) * P], gd[:, k, :]) for k in range(2)]).then_inc(gate_tiles, 1)
            phase_end(pe, 17)

            def mix(i):
                for u in range(8):
                    is_split(pe, "mix2", u, i)
                    pe.wait_ge(x_lo, x_number("mix2", u, i) + 1)
                    w = parts(u, 2, W)
                    for m in range(KW):
                        if not first(i) and u == 0:
                            pe.wait_ge(evac["mix2"], i * KW + (m + 1 - KW))
                        for k in range(2):
                            last = threefold(bank[:, m, 0:NT], [x[:, k, m * P:(m + 1) * P] for x in w],
                                             [x[:, u % 2, k * NT:(k + 1) * NT] for x in (xhi, xlo)], u == 0 and k == 0,
                                             u == 7 and k == 1)
                    last.then_inc(used, 1)
            repeat(pe, 2, mix)
            phase_end(pe, 18)
            norm_pe(pe, NT)
            phase_end(pe, 19)
            norm_pe(pe, NT)
            phase_end(pe, 20)
            linear("up2", lambda s: ([h[:, :, META - HALO:NT] for h in hboth], T + HALO) if s % 2 == 0 else
                   ([h[:, :, META:NT] for h in hboth], T))
            phase_end(pe, 21)
            by_rows("down2")
            phase_end(pe, 22)
            norm_pe(pe, T)
            phase_end(pe, 23)

        @block.scalar
        def _(act):
            step = Steps(act, act_step)
            act.wait_ge(params_in, 16)
            nc.scalar.activation(cact[:], param("c"), ACT.Silu).then_inc(cact_ready, 1)
            phase_end(act, 1)
            act.wait_ge(ones_set, 1)
            act.wait_ge(x_loaded, 16)
            ahead(round_unit, "ada", 0, True)
            norm_act(act, x1, T, step)
            hand_act(T, mod[:, 0, :])
            for n in range(4):
                act.wait_ge(angle_done, n + 1)
                dst = (tabs128[:, n % 2, 0:T], tabs64[:, n % 2, :])[n // 2]
                nc.scalar.activation(dst, turns[:, n, :], ACT.Sin).then_inc(sines, 1)
            phase_end(act, 2)

            def overlapped(body, count, per):
                body(0, tail=False)
                with act.Fori(1, count - 1) as i:
                    step.begin(i - 1, per)
                    body(i)
                    step.end()
                step.begin(count - 2, per)
                body(count - 1, last=True)
                step.end()
                step.leave(count - 1)
                body(count, head=False)

            def attended(i, o_sem, yT):
                act.wait_ge(o_sem, i * 2)
                for e in range(2):
                    if e == 0:
                        nc.scalar.activation(tile(yT, i * 2 - 2), bank[:, 3, 0:T], ACT.Copy)
                    else:
                        nc.scalar.activation(tile(yT, i * 2 - 1), bank[:, 3, T:2 * T], ACT.Copy)

            def sb(i, head=True, tail=True, last=False):
                if head:
                    round_unit("sb", 2, i)
                    round_unit("sb", 3, i)
                if tail:
                    for e in range(2):
                        act.wait_ge(zm_done, i * 2 + (e - 1))
                        step(nc.scalar.activation(s_b[:, e, :], s_a[:, e, :], ACT.Abs))
                        step(nc.scalar.activation(s_c[:, e, :], s_b[:, e, :], ACT.Exp, scale=-1.0))
                        nc.scalar.activation(s_d[:, e, :], s_c[:, e, :], ACT.Ln, bias=ones[:, 0:1]).then_inc(l_done, 1)
                if head:
                    round_unit("sb", 4, i)
                    round_unit("sb", 5, i)
                if tail:
                    for e in range(2):
                        act.wait_ge(d_done, i * 2 + (e - 1))
                        nc.scalar.activation(s_f[:, e, :], s_b[:, e, :], ACT.Exp).then_inc(w_done, 1)
                if head:
                    ahead(round_unit, "sb", i, last)
                if tail:
                    attended(i, o_done, yaT)
            overlapped(sb, 4, 4)
            phase_end(act, 3)

            ahead(round_unit, "ki", 0, True)
            for u in range(2, 8):
                round_unit("qi", u, 0)
            ahead(round_unit, "qi", 0, True)
            for h in range(IDX_HEADS):
                act.wait_ge(dots_done, h + 1)
                if h >= 2:
                    act.wait_ge(relu_used, h - 1)
                nc.scalar.activation(relu[:, (h % 2) * 384:(h % 2 + 1) * 384], bank[:, h % 8, 0:384], ACT.Relu,
                                     scale=IDX_D ** -0.5 * IDX_HEADS ** -0.5).then_inc(relu_done, 1)
            phase_end(act, 4)

            def dsa(i, head=True, tail=True, last=False):
                if head:
                    round_unit("dsa", 2, i)
                    round_unit("dsa", 3, i)
                if tail:
                    for e in range(2):
                        act.wait_ge(max_done, i * 2 + (e - 1))
                        nc.scalar.activation(s_b[:, e, 0:P], s_a[:, e, 0:P], ACT.Exp, bias=small[:, 8 * e:8 * e + 1],
                                             accum_out=small[:, 8 * e + 2:8 * e + 3])
                        nc.scalar.activation(s_b[:, e, P:384], s_a[:, e, P:384], ACT.Exp, bias=small[:, 8 * e + 1:8 * e + 2],
                                             accum_out=small[:, 8 * e + 3:8 * e + 4]).then_inc(exp_done, 1)
                if head:
                    round_unit("dsa", 4, i)
                    round_unit("dsa", 5, i)
                if tail:
                    for e in range(2):
                        act.wait_ge(turned, i * 2 + (e - 1))
                        nc.scalar.activation(s_f[:, e, :], bank[:, 6 + e, 0:384], ACT.Copy).then_inc(turned_read, 1)
                if head:
                    ahead(round_unit, "dsa", i, last)
                if tail:
                    attended(i, o2_done, ybT)
            overlapped(dsa, 4, 0)
            phase_end(act, 5)

            nc.scalar.activation(yhi[:], work[:, 0:KD * T].rearrange("p (k t) -> p k t", k=KD), ACT.Copy).then_inc(y_hi, 1)

            def merge(i, last):
                for u in range(2, 6):
                    round_unit("merge", u, i)
                if not first(i):
                    act.wait_ge(merged, i * 2)
                for s in (2, 3):
                    if s == 3:
                        ahead(round_unit, "merge", i, last)
                    multiplied(act, "merge", 2 * s - 1, i)
                    for t in range(2):
                        nc.scalar.activation(gates[:, 2 * s + t - 4, :], bank[:, 2 * s + t, 0:T], ACT.Sigmoid)\
                            .then_inc(merge_read[s], 1)
            rotated(act, 8, merge)
            phase_end(act, 6)

            def by_rows_act(phase, src):
                _, count, per, _, _ = PLAN[phase]

                def body(i, last):
                    if first(i):
                        for u in range(2):
                            round_x(phase, u, i, src(u, i))
                    for u in range(2, per):
                        round_x(phase, u, i, src(u, i))
                        round_unit(phase, u, i)
                    for u in range(2):
                        if not last:
                            round_x(phase, u, i + 1, src(u, i + 1))
                            round_unit(phase, u, i + 1)
                    if last:
                        ahead(round_unit, phase, i, True)
                rotated(act, count, body)
            by_rows_act("wo", lambda u, i: [tile(mergedT, i * 4 + u)])
            phase_end(act, 7)
            norm_act(act, x1, T, step)
            hand_act(T, mod[:, 3, :])
            phase_end(act, 8)

            def linear_act(phase, read):
                _, count, per, _, _ = PLAN[phase]

                def body(i, last):
                    for s in range(per // 2):
                        if s < per // 2 - 1:
                            round_unit(phase, 2 * s + 2, i)
                            round_unit(phase, 2 * s + 3, i)
                        else:
                            ahead(round_unit, phase, i, last)
                        read(s, i)
                rotated(act, count, body)

            def up(s, i):
                if s == 0 and not first(i):
                    act.wait_ge(acted, i * 4)
                multiplied(act, "up", 2 * s + 1, i)
                for t in range(2):
                    q = 2 * s + t
                    f = 4 * i + (2 * (s // 2) + t + (KF if s % 2 else 0))
                    nc.scalar.activation(cv[:, q, 0:T], bank[:, q, 0:T], ACT.Identity, scale=pcol("conv_w", 4 * KF + f),
                                         bias=pcol("conv_b", f)).then_inc(tap_done, 1)
                if s % 2:
                    for t in range(2):
                        act.wait_ge(evac["up"], i * 8 + (2 * s - 2 + t + 1))
                        nc.scalar.activation(sa[:, s - 1 + t, :], cv[:, 2 * s - 2 + t, 0:T], ACT.Silu).then_inc(silu_done, 1)
            linear_act("up", up)
            phase_end(act, 9)
            by_rows_act("down", lambda u, i: [tile(actT, i * 4 + u)])
            phase_end(act, 10)
            norm_act(act, x1, T, step)
            phase_end(act, 11)

            act.dma_start(res[:, :, 0:META], A["metaT"]).then_inc(meta_loaded, 16)
            act.wait_ge(meta_loaded, 16)
            norm_act(act, res, NT, step)
            hand_act(NT)
            phase_end(act, 12)

            def conv2(s, i):
                if s == 1:
                    if not first(i):
                        act.wait_ge(evac["conv2"], i * 2)
                    multiplied(act, "conv2", 3, i)
                    for t in range(2):
                        nc.scalar.activation(cs[:, t, :], bank[:, 2 + t, 0:NT], ACT.Copy).then_inc(c_copied, 1)
            linear_act("conv2", conv2)
            phase_end(act, 13)

            def rkv(s, i):
                multiplied(act, "rkv", 2 * s + 1, i)
                for t in range(2):
                    q = 2 * s + t
                    f = i * 8 + q
                    m = omu[:, f:f + 1] if isinstance(f, int) else omu[:, bass.ds(f, 1)]
                    nc.scalar.activation(tile(zr, f), bank[:, q, 0:NT], ACT.Copy, scale=m).then_inc(own_done, 1)
            linear_act("rkv", rkv)
            phase_end(act, 14)
            lora_parts = [(gd[:, 0, :], bank[:, 0, 0:NT], omu[:, 24:25]), (gd[:, 1, :], bank[:, 1, 0:NT], omu[:, 25:26]),
                          (wdad[0:LORA, 0, :], bank[0:LORA, 2, 0:NT], omu[0:LORA, 26:27]),
                          (wdad[0:LORA, 1, :], bank[0:LORA, 3, 0:NT], omu[0:LORA, 27:28])]

            def lora(s, i):
                multiplied(act, "lora", 2 * s + 1, i)
                for dst, src, m in lora_parts[2 * s:2 * s + 2]:
                    nc.scalar.activation(dst, src, ACT.Copy, scale=m).then_inc(own_done, 1)
            linear_act("lora", lora)
            act.wait_ge(evac["lora"], 4)
            nc.scalar.activation(wdad[0:LORA, 0, :], wdad[0:LORA, 0, :], ACT.Tanh).then_inc(lora_ready, 2)
            for t in range(2):
                nc.scalar.activation(gd[:, t, :], gd[:, t, :], ACT.Sigmoid)
            for u, (dst, shift) in enumerate(((lw, "w0"), (aa, "a0"))):
                for j in range(KW):
                    act.wait_ge(loraup_tiles, u * KW + j + 1)
                    nc.scalar.activation(dst[:, j, :], bank[:, j, 0:NT], ACT.Sigmoid, bias=param(shift, j)).then_inc(loraup_evac, 1)
            act.wait_ge(kk_floored, 1)
            nc.scalar.activation(all8(temp8b), all8(temp8b), ACT.Sqrt).then_inc(kk_rooted, 1)
            phase_end(act, 15)

            def recur(i):
                nl = len(LEVELS)
                act.wait_ge(cum_done, i + 1)
                nc.scalar.activation(Ep, cumc, ACT.Exp)
                nc.scalar.activation(Em, cumc, ACT.Exp, scale=-1.0)
                nc.scalar.activation(Epm, cpm, ACT.Exp)
                nc.scalar.activation(ecm, mids, ACT.Exp)
                nc.scalar.activation(vt, tile(zr, i + 2 * KW), ACT.Copy).then_inc(exps_done, 1)
                for e in range(2):
                    act.wait_ge(t0_raw, i * 2 + (e + 1))
                    nc.scalar.activation(TT[0:L, e, :], bank[0:L, 2 + e, 0:NT], ACT.Copy).then_inc(t0_ready, 1)
                for l in range(nl):
                    for e in range(2):
                        n = 2 * l + e
                        act.wait_ge(w1_raw, i * 2 * nl + (n + 1))
                        nc.scalar.activation(W1[0:L, e, :], bank[0:L, e, 0:NT], ACT.Copy).then_inc(w1_ready, 1)
                        if n < 3:
                            act.wait_ge(task_done, i * 10 + (n + 1))
                            dst = (tokK, tokB, tokV)[n]
                            nc.scalar.activation(dst[0:L, :, :].rearrange("p a t -> p (a t)"), bank[0:L, 6 + n % 2, :], ACT.Copy)\
                                .then_inc(tok_read, 1)
                for c in range(NC):
                    act.wait_ge(x_raw, i * NC + (c + 1))
                    nc.scalar.activation(Xs[0:L, :].rearrange("p (a v) -> p a v", a=2), bank[0:L, 0:2, 0:RN], ACT.Copy).then_inc(x_ready, 1)
                act.wait_ge(y_raw, i + 1)
                y = tile(zr, i)
                nc.scalar.activation(y[0:RN, :], bank[0:RN, 4, 0:NT], ACT.Copy)
                nc.scalar.activation(y[RN:P, :], bank[RN:P, 5, 0:NT], ACT.Copy).then_inc(pair_done, 1)
            repeat(act, KW, recur)
            phase_end(act, 16)

            for j in range(KW):
                act.wait_ge(centred, j + 1)
                nc.scalar.activation(kk[:, j, :], zr[:, j, :], ACT.Square).then_inc(y_squared, 1)
            for j in range(KW):
                act.wait_ge(var_raw, j + 1)
                nc.scalar.activation(lw[:, j, :], bank[:, j, 0:NT], ACT.Sqrt, scale=1.0 / RN, bias=epsc[:, 1:2]).then_inc(var_read, 1)
            phase_end(act, 17)

            def mix(i, last):
                def src(u):
                    return [yconv[:, k, :] if k < KW else zr[:, k - KW, :] for k in (2 * u, 2 * u + 1)]
                if first(i):
                    for u in range(2):
                        round_x("mix2", u, i, src(u))
                for u in range(2, 8):
                    round_x("mix2", u, i, src(u))
                    round_unit("mix2", u, i)
                if not last:
                    for u in range(2):
                        round_x("mix2", u, i + 1, src(u))
                ahead(round_unit, "mix2", i, last)
                multiplied(act, "mix2", 7, i)
                for m in range(KW):
                    nc.scalar.activation(tile(fT, i * KW + m), bank[:, m, 0:NT], ACT.Copy).then_inc(evac["mix2"], 1)
            rotated(act, 2, mix)
            phase_end(act, 18)
            norm_act(act, fT, NT, step)
            phase_end(act, 19)
            norm_act(act, res, NT, step)
            hand_act(NT)
            phase_end(act, 20)

            def up2(s, i):
                if s == 0 and not first(i):
                    act.wait_ge(evac["up2"], i * 8)
                if s % 2 == 0:
                    multiplied(act, "up2", 2 * s + 1, i)
                    for t in range(2):
                        nc.scalar.activation(cv[:, 2 * s + t, 0:T], bank[:, 2 * s + t, HALO:T + HALO], ACT.Copy,
                                             scale=pcol("conv_ffn", 4 * i + (s + t + 2 * KF))).then_inc(tap2_done, 1)
                else:
                    for t in range(2):
                        act.wait_ge(evac["up2"], i * 8 + (2 * s - 2 + t + 1))
                        nc.scalar.activation(sa[:, s - 1 + t, :], cv[:, 2 * s - 2 + t, 0:T], ACT.Silu).then_inc(silu2_done, 1)
            linear_act("up2", up2)
            phase_end(act, 21)
            by_rows_act("down2", lambda u, i: [tile(actT, i * 4 + u)])
            multiplied(act, "down2", 3, 10)
            for f in range(KD):
                nc.scalar.activation(fT[:, f, 0:T], bank[:, f // 2, (f % 2) * T:(f % 2 + 1) * T], ACT.Copy)
            phase_end(act, 22)
            norm_act(act, fT[:, :, 0:T], T, step)
            phase_end(act, 23)

        @block.vector
        def _(dve):
            step = Steps(dve, dve_step)
            nc.vector.memset(epsc[:, 0:1], EPS)
            nc.vector.memset(epsc[:, 1:2], GN_EPS)
            nc.vector.memset(ones[:], 1.0).then_inc(ones_set, 1)
            dve.wait_ge(params_in, 16)
            dve.wait_ge(cact_ready, 1)

            def ada(i):
                for b in range(2):
                    for k in range(KD):
                        u = b * KD + k
                        arrived(dve, "ada", u, i)
                        if k == 0:
                            if not first(i):
                                dve.wait_ge(ada_summed, i * 2 + (b - 1))
                            ins = nc.vector.tensor_scalar(acc[:, b, :], ring[:, u % NSLOT, :], cact[:, k:k + 1], None, ALU.mult)
                        else:
                            dve.wait_ge(ada_used, i * 2 * KD + u)
                            ins = nc.vector.scalar_tensor_tensor(acc[:, b, :], ring[:, u % NSLOT, :], cact[:, k:k + 1],
                                                                 acc[:, b, :], ALU.mult, ALU.add)
                        ins.then_inc(ada_used, 1)
            repeat(dve, 3, ada)
            dve.wait_ge(ada_summed, 6)
            flat = mod[:].rearrange("p a k -> p (a k)")
            step(nc.vector.tensor_tensor(flat, bank[:, 0, 0:6 * KD], param("b_ada"), ALU.add))
            nc.vector.scalar_tensor_tensor(gain[:, 0, :], mod[:, 1, :], 1.0, param("g_mix"), ALU.add, ALU.mult)
            nc.vector.scalar_tensor_tensor(gain[:, 1, :], mod[:, 4, :], 1.0, param("g_ffn"), ALU.add, ALU.mult)
            nc.vector.tensor_scalar(mod[:, 2, :], mod[:, 2, :], 1.0, None, ALU.add)
            step(nc.vector.tensor_scalar(mod[:, 5, :], mod[:, 5, :], 1.0, None, ALU.add))
            phase_end(dve, 1)

            dve.wait_ge(pos_in, 16)
            dve.wait_ge(consts_in, 16)
            dve.wait_ge(x_loaded, 16)
            step(nc.vector.tensor_copy(posf, posi))
            C1, C2 = 6.28125, 0.0019350051879882812
            C3 = 2 * math.pi - C1 - C2
            ROUND = 1.5 * 2.0 ** 23
            EDGE = 3.1415925
            for n in range(4):
                f = n // 2
                cosine = n % 2 == 1
                if n:
                    dve.wait_ge(angle_done, n)
                step(nc.vector.tensor_scalar(angles[:, 0, :], posf, const("invf")[:, f:f + 1], None, ALU.mult))
                step(nc.vector.tensor_scalar(angles[:, 1, :], angles[:, 0, :], 1 / (2 * math.pi), 0.25 if cosine else 0.0,
                                             ALU.mult, ALU.add))
                step(nc.vector.tensor_scalar(angles[:, 1, :], angles[:, 1, :], ROUND, -ROUND, ALU.add, ALU.add))
                for c in (C1, C2, C3):
                    step(nc.vector.scalar_tensor_tensor(angles[:, 0, :], angles[:, 1, :], -c, angles[:, 0, :], ALU.mult, ALU.add))
                step(nc.vector.tensor_scalar(angles[:, 0, :], angles[:, 0, :], math.pi / 2 if cosine else 0.0, EDGE,
                                             ALU.add, ALU.min))
                nc.vector.tensor_scalar(turns[:, n, :], angles[:, 0, :], -EDGE, None, ALU.max).then_inc(angle_done, 1)
            ahead(rest_unit, "ada", 0, True)
            norm_dve_handing(dve, x1, gain[:, 0, :], T, step, mod[:, 0, :])
            dve.wait_ge(sines, 4)
            step(nc.vector.tensor_scalar(tabs128[:, 0, 0:T], tabs128[:, 0, 0:T], const("sign")[:, 0:1], None, ALU.mult))
            nc.vector.tensor_scalar(tabs64[:, 0, :], tabs64[:, 0, :], const("sign")[:, 1:2], None, ALU.mult)
            for n in range(2):
                nc.vector.tensor_copy(tabs128[:, n, T:2 * T], tabs128[:, n, 0:T])
            phase_end(dve, 2)

            def overlapped(body, count, per):
                body(0, tail=False)
                with dve.Fori(1, count - 1) as i:
                    step.begin(i - 1, per)
                    body(i)
                    step.end()
                step.begin(count - 2, per)
                body(count - 1, last=True)
                step.end()
                step.leave(count - 1)
                body(count, head=False)

            def sb(i, head=True, tail=True, last=False):
                if head:
                    rest_unit("sb", 2, i)
                    rest_unit("sb", 3, i)
                if tail:
                    for e in range(2):
                        dve.wait_ge(z_done, i * 2 + (e - 1))
                        nc.vector.scalar_tensor_tensor(s_a[:, e, :], bank[:, 4 + e, 0:384], SCALE, past, ALU.mult, ALU.add)\
                            .then_inc(zm_done, 1)
                if head:
                    multiplied(dve, "sb", 1, i)
                    nc.vector.tensor_copy(qT[:].rearrange("p a t -> p (a t)"), bank[:, 0, :]).then_inc(q_read, 1)
                if tail:
                    for e in range(2):
                        dve.wait_ge(l_done, i * 2 + (e - 1))
                        dve.wait_ge(zm_done, i * 2 + (e - 1))
                        nc.vector.scalar_tensor_tensor(s_e[:, e, :], s_a[:, e, :], 0.0, s_d[:, e, :], ALU.max, ALU.add)\
                            .then_inc(sp_done, 1)
                if head:
                    rest_unit("sb", 4, i)
                    rest_unit("sb", 5, i)
                    multiplied(dve, "sb", 3, i)
                    nc.vector.tensor_copy(kT[:].rearrange("p a t -> p (a t)"), bank[:, 1, :]).then_inc(k_read, 1)
                if tail:
                    for e in range(2):
                        dve.wait_ge(s_done, i * 2 + (e - 1))
                        nc.vector.tensor_tensor(s_b[:, e, :], s_a[:, e, :], bank[:, 6 + e, 0:384], ALU.subtract)\
                            .then_inc(d_done, 1)
                    dve.wait_ge(d_done, i * 2)
                if head:
                    ahead(rest_unit, "sb", i, last)
                    multiplied(dve, "sb", 5, i)
                    if tail:
                        dve.wait_ge(o_done, i * 2)
                    nc.vector.tensor_copy(vS[:].rearrange("p a t -> p (a t)"), bank[:, 2, :]).then_inc(v_read, 1)
            overlapped(sb, 4, 0)
            phase_end(dve, 3)

            def rope(dst, src, n, tabs, half, done, count):
                sin, cos = tabs[:, 0, 0:n], tabs[:, 1, 0:n]
                a, b = ropeA[:, 0:n], ropeB[:, 0:n]
                for lo in range(0, P, 2 * half):
                    mid, hi = lo + half, lo + 2 * half
                    nc.vector.tensor_tensor(a[lo:mid, :], src[mid:hi, :], sin[mid:hi, :], ALU.mult)
                    last = nc.vector.tensor_tensor(a[mid:hi, :], src[lo:mid, :], sin[lo:mid, :], ALU.mult)
                step.mark(last)
                step(nc.vector.tensor_tensor(b, src, cos, ALU.mult))
                nc.vector.tensor_tensor(dst, a, b, ALU.add).then_inc(done, 1)
                dve.wait_ge(done, count)

            ahead(rest_unit, "ki", 0, True)
            multiplied(dve, "ki", 1, 0)
            rope(kiT, bank[:, 6, 0:T], T, tabs64, 32, evac["ki"], 1)
            nc.vector.tensor_copy(small[:, 0:2 * IDX_HEADS], bank[:, 7, 0:2 * IDX_HEADS]).then_inc(evac["ki"], 1)
            for q in range(8):
                if q % 2 == 0 and q < 6:
                    rest_unit("qi", q + 2, 0)
                    rest_unit("qi", q + 3, 0)
                elif q == 6:
                    ahead(rest_unit, "qi", 0, True)
                multiplied(dve, "qi", q // 2 * 2 + 1, 0)
                rope(qiT[:, q, :], bank[:, q, 0:T], T, tabs64, 32, evac["qi"], q + 1)
            score, spare = s_a[:, 0, :], s_a[:, 1, :]
            dve.wait_ge(evac["ki"], 2)
            step(nc.vector.memset(score, 0.0))
            for h in range(IDX_HEADS):
                dve.wait_ge(relu_done, h + 1)
                r = relu[:, (h % 2) * 384:(h % 2 + 1) * 384]
                step.mark(nc.vector.scalar_tensor_tensor(score[:, 0:P], r[:, 0:P], small[:, h:h + 1], score[:, 0:P],
                                                         ALU.mult, ALU.add))
                nc.vector.scalar_tensor_tensor(score[:, P:384], r[:, P:384], small[:, IDX_HEADS + h:IDX_HEADS + h + 1],
                                               score[:, P:384], ALU.mult, ALU.add).then_inc(relu_used, 1)
                dve.wait_ge(relu_used, h + 1)
            step(nc.vector.scalar_tensor_tensor(score, seen, UNSEEN / NEG, score, ALU.mult, ALU.add))
            src, dst = score, spare
            for r in range(TOPK // 8):
                for lo, hi, m in ((0, P, 40), (P, 384, 48)):
                    step.mark(nc.vector.max(small[:, m:m + 8], src[:, lo:hi]))
                step.wait()
                for lo, hi, m in ((0, P, 40), (P, 384, 48)):
                    step.mark(nc.vector.match_replace(dst[:, lo:hi], small[:, m:m + 8], src[:, lo:hi], TAKEN))
                step.wait()
                src, dst = dst, src
            taken = biasM[:, 0, :]
            step(nc.vector.tensor_scalar(taken, src, TAKEN, None, ALU.is_equal))
            step(nc.vector.tensor_scalar(taken, taken, -NEG, NEG, ALU.mult, ALU.add))
            step(nc.vector.tensor_tensor(taken, taken, seen, ALU.add))
            phase_end(dve, 4)

            def dsa(i, head=True, tail=True, last=False):
                if head:
                    rest_unit("dsa", 2, i)
                    rest_unit("dsa", 3, i)
                if tail:
                    for e in range(2):
                        dve.wait_ge(logits_done, i * 2 + (e - 1))
                        step(nc.vector.scalar_tensor_tensor(s_a[:, e, :], bank[:, 4 + e, 0:384], SCALE, taken, ALU.mult, ALU.add))
                        nc.vector.tensor_reduce(small[:, 8 * e:8 * e + 1], s_a[:, e, 0:P], AX, ALU.max, negate=True)
                        nc.vector.tensor_reduce(small[:, 8 * e + 1:8 * e + 2], s_a[:, e, P:384], AX, ALU.max, negate=True)\
                            .then_inc(max_done, 1)
                if head:
                    multiplied(dve, "dsa", 1, i)
                    rope(qT[:].rearrange("p a t -> p (a t)"), bank[:, 0, :], 2 * T, tabs128, 64, q2_read, i + 1)
                if tail:
                    for e in range(2):
                        dve.wait_ge(exp_done, i * 2 + (e - 1))
                        step(nc.vector.reciprocal(small[:, 8 * e + 4:8 * e + 6], small[:, 8 * e + 2:8 * e + 4]))
                        step.mark(nc.vector.tensor_scalar(s_c[:, e, 0:P], s_b[:, e, 0:P], small[:, 8 * e + 4:8 * e + 5], None, ALU.mult))
                        nc.vector.tensor_scalar(s_c[:, e, P:384], s_b[:, e, P:384], small[:, 8 * e + 5:8 * e + 6], None, ALU.mult)\
                            .then_inc(probs_done, 1)
                if head:
                    rest_unit("dsa", 4, i)
                    rest_unit("dsa", 5, i)
                    multiplied(dve, "dsa", 3, i)
                    rope(kT[:].rearrange("p a t -> p (a t)"), bank[:, 1, :], 2 * T, tabs128, 64, k2_read, i + 1)
                    ahead(rest_unit, "dsa", i, last)
                    multiplied(dve, "dsa", 5, i)
                    if tail:
                        dve.wait_ge(o2_done, i * 2)
                    nc.vector.tensor_copy(vS[:].rearrange("p a t -> p (a t)"), bank[:, 2, :]).then_inc(v2_read, 1)
            overlapped(dsa, 4, 10)
            phase_end(dve, 5)

            dve.wait_ge(y_hi, 1)
            nc.vector.tensor_tensor(ylo[:], work[:, 0:KD * T].rearrange("p (k t) -> p k t", k=KD), yhi[:].bitcast(F32),
                                    ALU.subtract).then_inc(y_lo, 1)

            def merge(i, last):
                for u in range(2, 6):
                    rest_unit("merge", u, i)
                for s in range(2):
                    if s == 1:
                        ahead(rest_unit, "merge", i, last)
                    for t in range(2):
                        dve.wait_ge(merge_read[2 + s], i * 2 + (t + 1))
                        nc.vector.tensor_tensor(gated[:, 2 * s + t, :], gates[:, 2 * s + t, :],
                                                bank[:, 2 * s + t, 0:T], ALU.mult).then_inc(merge_read[s], 1)
                for t in range(2):
                    dve.wait_ge(merge_read[1], i * 2 + (t + 1))
                    nc.vector.tensor_tensor(tile(mergedT, i * 2 + t), gated[:, t, :], gated[:, 2 + t, :],
                                            ALU.add).then_inc(merged, 1)
            rotated(dve, 8, merge)
            phase_end(dve, 6)

            def by_rows_dve(phase, src):
                _, count, per, _, _ = PLAN[phase]

                def body(i, last):
                    if first(i):
                        for u in range(2):
                            rest_x(phase, u, i, src(u, i))
                    for u in range(2, per):
                        rest_x(phase, u, i, src(u, i))
                        rest_unit(phase, u, i)
                    for u in range(2):
                        if not last:
                            rest_x(phase, u, i + 1, src(u, i + 1))
                            rest_unit(phase, u, i + 1)
                    if last:
                        ahead(rest_unit, phase, i, True)
                rotated(dve, count, body)

            def add_gated(phase, gate):
                multiplied(dve, phase, PLAN[phase][2] - 1, PLAN[phase][1] - 1)
                for f in range(KD):
                    nc.vector.scalar_tensor_tensor(x1[:, f, :], bank[:, f // 2, (f % 2) * T:(f % 2 + 1) * T], gate[:, f:f + 1],
                                                   x1[:, f, :], ALU.mult, ALU.add)
            by_rows_dve("wo", lambda u, i: [tile(mergedT, i * 4 + u)])
            add_gated("wo", mod[:, 2, :])
            phase_end(dve, 7)
            norm_dve_handing(dve, x1, gain[:, 1, :], T, step, mod[:, 3, :])
            phase_end(dve, 8)

            def linear_dve(phase, read, per_steps=None):
                _, count, per, _, _ = PLAN[phase]

                def body(i, last):
                    step.begin(i)
                    for s in range(per // 2):
                        if s < per // 2 - 1:
                            rest_unit(phase, 2 * s + 2, i)
                            rest_unit(phase, 2 * s + 3, i)
                        else:
                            ahead(rest_unit, phase, i, last)
                        read(s, i)
                    step.end()
                rotated(dve, count, body)
                step.leave(count)

            def up(s, i):
                for t in range(2):
                    q = 2 * s + t
                    f = 4 * i + (2 * (s // 2) + t + (KF if s % 2 else 0))
                    dve.wait_ge(tap_done, i * 8 + (q + 1))
                    c, b = cv[:, q, 0:T], bank[:, q, 0:T]
                    step(nc.vector.scalar_tensor_tensor(c[:, 1:T], b[:, 0:T - 1], pcol("conv_w", 2 * KF + f), c[:, 1:T],
                                                        ALU.mult, ALU.add))
                    nc.vector.scalar_tensor_tensor(c[:, 2:T], b[:, 0:T - 2], pcol("conv_w", f), c[:, 2:T],
                                                   ALU.mult, ALU.add).then_inc(evac["up"], 1)
                if s % 2:
                    for t in range(2):
                        dve.wait_ge(silu_done, i * 4 + (s - 1 + t + 1))
                        dve.wait_ge(evac["up"], i * 8 + (2 * s + t + 1))
                        nc.vector.tensor_tensor(tile(actT, i * 4 + (s - 1 + t)), sa[:, s - 1 + t, :],
                                                cv[:, 2 * s + t, 0:T], ALU.mult).then_inc(acted, 1)
            linear_dve("up", up)
            phase_end(dve, 9)
            by_rows_dve("down", lambda u, i: [tile(actT, i * 4 + u)])
            add_gated("down", mod[:, 5, :])
            phase_end(dve, 10)
            norm_dve(dve, T, step, scaled(x1, x1, param("g_final"), T))
            phase_end(dve, 11)

            norm_dve_handing(dve, res, param("g_pre_mix"), NT, step)
            lo = pw["mu_rkv"][0]
            nc.vector.tensor_scalar(omu[:], params[:, lo:lo + 28], -1.0, 1.0, ALU.mult, ALU.add)
            nc.vector.tensor_scalar(omka[:], param("k_a"), -1.0, 1.0, ALU.mult, ALU.add)
            nc.vector.memset(chs[:, :, 0:HALO], 0.0)
            phase_end(dve, 12)

            def conv2(s, i):
                if s < 2:
                    return
                multiplied(dve, "conv2", 5, i)
                for t in range(2):
                    f = i * 2 + t
                    dve.wait_ge(c_copied, i * 2 + (t + 1))
                    step(nc.vector.tensor_tensor(chs[:, t, HALO:HALO + NT], cs[:, t, :], bank[:, 4 + t, 0:NT], ALU.mult))
                    step(nc.vector.tensor_scalar(ycs[:, t, :], chs[:, t, 0:NT], pcol("conv_w2", f), None, ALU.mult))
                    for tap in (1, 2):
                        step(nc.vector.scalar_tensor_tensor(ycs[:, t, :], chs[:, t, tap:tap + NT], pcol("conv_w2", f + tap * KW),
                                                            ycs[:, t, :], ALU.mult, ALU.add))
                    nc.vector.tensor_tensor(tile(yconv, f), ycs[:, t, :], bank[:, t, 0:NT], ALU.mult).then_inc(evac["conv2"], 1)
            linear_dve("conv2", conv2)
            phase_end(dve, 13)

            def shift(dst, src, mu, f, done):
                dve.wait_ge(own_done, f + 1)
                nc.vector.scalar_tensor_tensor(dst[:, 1:NT], src[:, 0:NT - 1], mu, dst[:, 1:NT], ALU.mult, ALU.add).then_inc(done, 1)

            def rkv(s, i):
                for q in (2 * s, 2 * s + 1):
                    f = i * 8 + q
                    shift(tile(zr, f), bank[:, q, 0:NT], pcol("mu_rkv", f), f, evac["rkv"])
            linear_dve("rkv", rkv)
            phase_end(dve, 14)

            def lora(s, i):
                for t in range(2):
                    if s == 0:
                        shift(gd[:, t, :], bank[:, t, 0:NT], param("mu_gd", t), 24 + t, evac["lora"])
                    else:
                        shift(wdad[0:LORA, t, :], bank[0:LORA, 2 + t, 0:NT], param(("mu_wd", "mu_ad")[t], 0)[0:LORA, :],
                              26 + t, evac["lora"])
            linear_dve("lora", lora)
            for j in range(KW):
                last = nc.vector.tensor_scalar(kk[:, j, :], zr[:, KW + j, :], param("k_k", j), None, ALU.mult)
            step(last)
            nc.vector.tensor_tensor(all8(temp8), all8(kk), all8(kk), ALU.mult).then_inc(kk_squared, 1)
            dve.wait_ge(loraup_evac, KW)
            nc.vector.tensor_scalar(all8(lw), all8(lw), -DECAY_SCALE, None, ALU.mult)
            for j in range(KW):
                dve.wait_ge(kk_summed, j + 1)
                last = nc.vector.tensor_scalar(temp8b[:, j, :], bank[:, j, 0:NT], 1e-24, None, ALU.max)
            last.then_inc(kk_floored, 1)
            dve.wait_ge(kk_rooted, 1)
            step(nc.vector.reciprocal(all8(temp8b), all8(temp8b)))
            nc.vector.tensor_tensor(all8(kk), all8(kk), all8(temp8b), ALU.mult)
            phase_end(dve, 15)

            def by_chunk(x):
                return x.rearrange("p (c t) -> p c t", c=NC)

            def mask(name):
                return const(name)[0:L, :].unsqueeze(1).to_broadcast([L, NC, L])

            def recur(i):
                nl = len(LEVELS)
                step.begin(i)
                if not first(i):
                    dve.wait_ge(pair_done, i)
                lwi = tile(lw, i)
                for c in range(NC):
                    last = nc.vector.tensor_tensor_scan(cum[:, c * L:(c + 1) * L], onesrow, lwi[:, c * L:(c + 1) * L], 0.0,
                                                        ALU.mult, ALU.add)
                step(last)
                for c in range(NC):
                    m = cum[:, c * L + MID:c * L + MID + 1]
                    step.mark(nc.vector.tensor_scalar(cumc[:, c * L:(c + 1) * L], cum[:, c * L:(c + 1) * L], m, None, ALU.subtract))
                step(nc.vector.tensor_copy(mids, by_chunk(cum)[:, :, MID]))
                nc.vector.tensor_tensor(cpm, cumc, lwi, ALU.subtract).then_inc(cum_done, 1)
                ki = tile(zr, i + KW)
                step(nc.vector.tensor_scalar(k2, tile(aa, i), pcol("k_a", i), omka[:, i:i + 1] if isinstance(i, int)
                                             else omka[:, bass.ds(i, 1)], ALU.mult, ALU.add))
                step(nc.vector.tensor_tensor(k2, k2, ki, ALU.mult))
                step(nc.vector.tensor_tensor(bb, tile(kk, i), tile(aa, i), ALU.mult))
                step.mark(nc.vector.scalar_tensor_tensor(rkr, tile(zr, i), pcol("r_k", i), k2, ALU.mult, ALU.mult))
                dve.wait_ge(exps_done, i + 1)
                nc.vector.scalar_tensor_tensor(AR[:, :, 0, :], by_chunk(Epm), -1.0, by_chunk(tile(kk, i)), ALU.mult, ALU.mult)
                nc.vector.tensor_tensor(AR[:, :, 1, :], by_chunk(Ep), by_chunk(tile(zr, i)), ALU.mult)
                nc.vector.tensor_tensor(kt, k2, Em, ALU.mult)
                nc.vector.tensor_tensor(bt, bb, Em, ALU.mult).then_inc(feat_done, 1)
                for e in range(2):
                    dve.wait_ge(n_raw, i * 2 + (e + 1))
                    step(nc.vector.scalar_tensor_tensor(by_chunk(N[0:L, e, :]), by_chunk(bank[0:L, e, 0:NT]), BIG, mask("strict"),
                                                        ALU.min, ALU.mult))
                    step(nc.vector.tensor_tensor(by_chunk(G[0:L, e, :]), by_chunk(N[0:L, e, :]), mask("first"), ALU.mult))
                    nc.vector.tensor_tensor(by_chunk(G[0:L, e, :]), by_chunk(G[0:L, e, :]),
                                            const("ident")[0:L, 0:L].unsqueeze(1).to_broadcast([L, NC, L]), ALU.add)\
                        .then_inc(g0_done, 1)
                for l in range(nl):
                    for e in range(2):
                        n = 2 * l + e
                        if 3 <= n < 10:
                            dve.wait_ge(task_done, i * 10 + (n + 1))
                            b = bank[:, 6 + n % 2, 0:NT]
                            if n < 9:
                                kind, h = (n - 3) // 2, (n - 3) % 2
                                dst = (lak, lrk, lrb)[kind]
                                ins = nc.vector.scalar_tensor_tensor(by_chunk(dst[0:L, h, :]), by_chunk(b[0:L, :]), BIG,
                                                                     mask("strict" if kind == 0 else "incl"), ALU.min, ALU.mult)
                            else:
                                ins = nc.vector.tensor_tensor(ki, tile(zr, i + 2 * KW), b, ALU.mult)
                            ins.then_inc(mat_read, 1)
                    for e in range(2):
                        dve.wait_ge(tg_raw, i * 2 * nl + (2 * l + e + 1))
                        if l < nl - 1:
                            nc.vector.tensor_tensor(TT[0:L, e, :], TT[0:L, e, :], bank[0:L, 2 + e, 0:NT], ALU.add)
                        nc.vector.tensor_tensor(G[0:L, e, :], G[0:L, e, :], bank[0:L, 4 + e, 0:NT], ALU.add).then_inc(tg_ready, 1)
                for c in range(NC):
                    dve.wait_ge(u_raw, i * NC + (c + 1))
                    nc.vector.tensor_copy(Us[0:L, :], bank[0:L, 2, 0:P]).then_inc(u_ready, 1)
                    if c < NC - 1:
                        dve.wait_ge(h_raw, i * 3 + (c + 1))
                        src = bank[:, 3, 0:RN]
                        if c:
                            step(nc.vector.tensor_tensor(Hsum, bank[:, 3, 0:RN], Hs[:, c % 2, :], ALU.add))
                            src = Hsum
                        nc.vector.tensor_scalar(Hs[:, (c + 1) % 2, :], src, Ep[:, (c + 1) * L - 1:(c + 1) * L],
                                                ecm[:, c + 1:c + 2], ALU.mult, ALU.mult).then_inc(h_ready, 1)
                        dve.wait_ge(h_ready, i * 3 + (c + 1))
                step.end()
            repeat(dve, KW, recur)
            step.leave(KW)
            phase_end(dve, 16)

            for j in range(KW):
                dve.wait_ge(mean_raw, j + 1)
                nc.vector.scalar_tensor_tensor(zr[:, j, :], bank[:, j, 0:NT], -1.0 / RN, zr[:, j, :], ALU.mult, ALU.add)\
                    .then_inc(centred, 1)
            dve.wait_ge(var_read, KW)
            dve.wait_ge(centred, KW)
            step(nc.vector.reciprocal(all8(lw), all8(lw)))
            for j in range(KW):
                step(nc.vector.scalar_tensor_tensor(zr[:, j, :], zr[:, j, :], param("ln_w", j), lw[:, j, :], ALU.mult, ALU.mult))
                step(nc.vector.scalar_tensor_tensor(zr[:, j, :], zr[:, j, :], param("ln_b", j), zr[:, KW + j, :], ALU.add, ALU.add))
                dve.wait_ge(gate_tiles, j + 1)
                nc.vector.tensor_tensor(zr[:, j, :], zr[:, j, :], bank[:, j, 0:NT], ALU.mult)
            phase_end(dve, 17)

            def mix(i, last):
                def src(u):
                    return [yconv[:, k, :] if k < KW else zr[:, k - KW, :] for k in (2 * u, 2 * u + 1)]
                if first(i):
                    for u in range(2):
                        rest_x("mix2", u, i, src(u))
                for u in range(2, 8):
                    rest_x("mix2", u, i, src(u))
                    rest_unit("mix2", u, i)
                if not last:
                    for u in range(2):
                        rest_x("mix2", u, i + 1, src(u))
                ahead(rest_unit, "mix2", i, last)
            rotated(dve, 2, mix)
            phase_end(dve, 18)

            def add_normed(g, n, dst):
                def apply(k):
                    step(nc.vector.scalar_tensor_tensor(fT[:, k, 0:n], fT[:, k, 0:n], param(g, k), rms[:, 0:n], ALU.mult, ALU.mult))
                    return nc.vector.tensor_tensor(dst[:, k, :], dst[:, k, :], fT[:, k, 0:n], ALU.add)
                return apply
            norm_dve(dve, NT, step, add_normed("g_post_mix", NT, res))
            phase_end(dve, 19)
            norm_dve_handing(dve, res, param("g_pre_ffn"), NT, step)
            phase_end(dve, 20)

            def up2(s, i):
                for t in range(2):
                    if s % 2 == 0:
                        q = 2 * s + t
                        f = 4 * i + (s + t)
                        dve.wait_ge(tap2_done, i * 4 + (s + t + 1))
                        step(nc.vector.scalar_tensor_tensor(cv[:, q, 0:T], bank[:, q, 1:T + 1], pcol("conv_ffn", f + KF),
                                                            cv[:, q, 0:T], ALU.mult, ALU.add))
                        nc.vector.scalar_tensor_tensor(cv[:, q, 0:T], bank[:, q, 0:T], pcol("conv_ffn", f),
                                                       cv[:, q, 0:T], ALU.mult, ALU.add).then_inc(evac["up2"], 1)
                    else:
                        q = 2 * s + t
                        if t == 0:
                            multiplied(dve, "up2", 2 * s + 1, i)
                        dve.wait_ge(silu2_done, i * 4 + (s - 1 + t + 1))
                        nc.vector.tensor_tensor(tile(actT, i * 4 + (s - 1 + t)), sa[:, s - 1 + t, :],
                                                bank[:, q, 0:T], ALU.mult).then_inc(evac["up2"], 1)
            linear_dve("up2", up2)
            phase_end(dve, 21)
            by_rows_dve("down2", lambda u, i: [tile(actT, i * 4 + u)])
            phase_end(dve, 22)
            norm_dve(dve, T, step, add_normed("g_post_ffn", T, x1))
            dve.sem_inc(result_ready, 1)
            phase_end(dve, 23)

        @block.gpsimd
        def _(pool):
            pool.wait_ge(consts_in, 16)

            def recur(i):
                nl = len(LEVELS)
                for l, b in enumerate(LEVELS):
                    for e in range(2):
                        if l == 0:
                            pool.wait_ge(g0_done, i * 2 + (e + 1))
                        if l >= 2:
                            pool.wait_ge(w1_raw, i * 2 * nl + (2 * (l - 2) + e + 1))
                        nc.gpsimd.tensor_tensor(
                            NM[0:L, l % 2, e * NT:(e + 1) * NT].rearrange("p (c t) -> p c t", c=NC),
                            N[0:L, e, :].rearrange("p (c t) -> p c t", c=NC),
                            const(f"level{b}")[0:L, :].unsqueeze(1).to_broadcast([L, NC, L]), ALU.mult).then_inc(nm_ready, 1)
            repeat(pool, KW, recur)


def constant_block():
    where, width = offsets(CONSTS)
    c = np.zeros((P, width), np.float32)

    def put(name, a):
        lo = where[name][0]
        c[:a.shape[0], lo:lo + a.shape[1]] = a
    p = np.arange(P)[:, None]
    j = np.arange(P)[None, :]
    put("ident", (p == j).astype(np.float32))
    put("tri", (p >= j).astype(np.float32))
    put("heads", (p // RN == j // RN).astype(np.float32))
    past = np.where(p < j, 0.0, NEG).astype(np.float32)
    put("past", np.concatenate([past, np.zeros((P, P), np.float32), past], 1))
    seen = np.where(j <= p, 0.0, NEG).astype(np.float32)
    put("seen", np.concatenate([seen, np.zeros((P, P), np.float32), seen], 1))
    invf, sign = np.zeros((P, 2), np.float32), np.zeros((P, 2), np.float32)
    for n, d in enumerate((HD, IDX_D)):
        f = (np.float32(1.0) / (np.float32(10000.0) ** (np.arange(0, d, 2, dtype=np.float32) / np.float32(d)))).astype(np.float32)
        at = np.arange(P) % d
        invf[:, n] = f[at % (d // 2)]
        sign[:, n] = np.where(at < d // 2, 1.0, -1.0)
    put("invf", invf)
    put("sign", sign)
    s, t = np.arange(L)[:, None], np.arange(L)[None, :]
    put("strict", (s < t).astype(np.float32))
    put("incl", (s <= t).astype(np.float32))

    def level(b):
        return ((s // (2 * b) == t // (2 * b)) & (s % (2 * b) < b) & (t % (2 * b) >= b)).astype(np.float32)
    put("first", level(1))
    for b in LEVELS:
        put(f"level{b}", level(b))
    return c


def by_feature(a):
    return np.ascontiguousarray(a.reshape(-1, P).T)


def tokens_by_feature(a):
    return np.ascontiguousarray(a.T.reshape(-1, P, a.shape[0]).transpose(1, 0, 2))


def kernel(**inputs):
    import concourse.bacc as bacc
    from concourse.bass_utils import run_bass_kernel_spmd

    x = {k: np.asarray(v) for k, v in inputs.items()}
    mu = x["mu_rwkv_2"]

    def lora_column(a):
        return np.concatenate([a, np.zeros(P - LORA, a.dtype)]).reshape(P, 1)
    pieces = {
        "c": by_feature(x["c"]), "b_ada": by_feature(x["b_ada"]), "g_mix": by_feature(x["g_mix"]),
        "g_ffn": by_feature(x["g_ffn"]), "g_final": by_feature(x["g_final"]), "conv_w": by_feature(x["conv_w"]),
        "conv_b": by_feature(x["conv_b"]), "g_pre_mix": by_feature(x["g_pre_mix_2"]), "g_post_mix": by_feature(x["g_post_mix_2"]),
        "g_pre_ffn": by_feature(x["g_pre_ffn_2"]), "g_post_ffn": by_feature(x["g_post_ffn_2"]),
        "conv_w2": by_feature(x["conv_w_2"]), "mu_rkv": by_feature(mu[:3 * W]), "mu_gd": by_feature(mu[3 * W + 2 * LORA:]),
        "mu_wd": lora_column(mu[3 * W:3 * W + LORA]), "mu_ad": lora_column(mu[3 * W + LORA:3 * W + 2 * LORA]),
        "w0": by_feature(x["w0_2"]), "a0": by_feature(x["a0_2"]), "k_k": by_feature(x["k_k_2"]), "k_a": by_feature(x["k_a_2"]),
        "r_k": by_feature(x["r_k_2"]), "ln_w": by_feature(x["ln_x_w_2"]), "ln_b": by_feature(x["ln_x_b_2"]),
        "conv_ffn": by_feature(x["conv_ffn_2"]),
    }
    arrays = {
        "params": np.ascontiguousarray(np.concatenate([pieces[n] for n, _ in PARAMS], axis=1)),
        "consts": constant_block(),
        "pos": np.ascontiguousarray(np.broadcast_to(x["positions"].reshape(1, T), (P, T))),
        "xT": tokens_by_feature(x["x"][0]), "metaT": tokens_by_feature(x["meta_tokens_2"]),
    }
    for name in ("w_in", "w_a", "w_b", "w_o", "w_ada", "w_up", "w_down"):
        arrays[name] = np.ascontiguousarray(x[name][0])
    for name in ("w_in_2", "w_decay_up_2", "a_up_2", "g_up_2", "w_out_2", "w_gate_up_2", "w_down_2"):
        arrays[name] = np.ascontiguousarray(x[name])
    nc = bacc.Bacc("TRN2", target_bir_lowering=False, num_devices=1)
    aps = {n: nc.dram_tensor(f"{n}_dram", a.shape, mybir.dt.from_np(a.dtype), kind="ExternalInput").ap() for n, a in arrays.items()}
    out = nc.dram_tensor("out_dram", (P, KD, T), F32, kind="ExternalOutput").ap()
    build(nc, aps, out)
    got = run_bass_kernel_spmd(nc, [{f"{n}_dram": a for n, a in arrays.items()}], core_ids=[0]).results[0]["out_dram"]
    return np.ascontiguousarray(got.transpose(2, 1, 0)).reshape(1, T, D)
```

```python
import math
from contextlib import ExitStack

import numpy as np

import concourse.bass as bass
from concourse import mybir

F32 = mybir.dt.float32
F32R = mybir.dt.float32r
I32 = mybir.dt.int32
ACT = mybir.ActivationFunctionType
ALU = mybir.AluOpType
AX = mybir.AxisListType.X

P = 128
D = 2048
WORK = 18432
KD = D // P
T = 256
META = 16
NT = META + T
F = 5632
KF = F // P
HD = 128
IDX_HEADS = 16
IDX_D = 64
TOPK = 64
UNIT = 256
KH = KD // 2
SLOT = KH * UNIT
NSLOT = 4
LATE = 512
NLATE = 4 * D // LATE
LATE_AT = 448
SBUF_START = 16512
HALO = 2
EPS = 1e-6
GN_EPS = 64e-5
DECAY_SCALE = math.exp(-0.5)
NEG = -1e30
UNSEEN = -1e38
TAKEN = -3e38
BIG = 1e30

L = 68
NC = NT // L
MID = L // 2
RH = 16
RN = 64
W = 1024
KW = W // P
LORA = 96
SB_OFF = 0
DSA_OFF = 3 * W
QI_OFF = 6 * W
KI_OFF = 7 * W
WI_OFF = KI_OFF + IDX_D
GATE_OFF = WI_OFF + IDX_HEADS
RW_OFF = 3 * W
LORA_OFF = RW_OFF + 3 * W
GD_OFF = LORA_OFF + 2 * LORA

PARAMS = [("c", KD), ("b_ada", 6 * KD), ("g_mix", KD), ("g_ffn", KD), ("g_final", KD),
          ("conv_w", 3 * 2 * KF), ("conv_b", 2 * KF),
          ("g_pre_mix", KD), ("g_post_mix", KD), ("g_pre_ffn", KD), ("g_post_ffn", KD),
          ("conv_w2", 3 * KW), ("mu_rkv", 3 * KW), ("mu_gd", 2), ("mu_wd", 1), ("mu_ad", 1),
          ("w0", KW), ("a0", KW), ("k_k", KW), ("k_a", KW), ("r_k", KW), ("ln_w", KW), ("ln_b", KW),
          ("conv_ffn", 3 * KF)]
LEVELS = [2, 4, 8, 16, 32, 64]
CONSTS = [("ident", P), ("tri", P), ("heads", P), ("past", 384), ("seen", 384), ("invf", 2), ("sign", 2),
          ("strict", L), ("incl", L), ("first", L)] + [(f"level{b}", L) for b in LEVELS]

STREAM = [("ada", 1, 32, 4, 1), ("sb", 4, 6, 3, 1), ("ki", 1, 2, 2, 3), ("qi", 1, 8, 4, 1), ("dsa", 4, 6, 3, 1),
          ("merge", 8, 6, 3, 1), ("wo", 4, 4, 4, 1), ("up", 11, 8, 4, 1), ("down", 11, 4, 4, 1),
          ("conv2", 4, 6, 3, 1), ("rkv", 3, 8, 4, 1), ("lora", 1, 4, 4, 2),
          ("mix2", 2, 8, 4, 1), ("up2", 11, 8, 4, 1), ("down2", 11, 4, 4, 1)]
PLAN = {p[0]: p for p in STREAM}
AFTER = {a[0]: b[0] for a, b in zip(STREAM, STREAM[1:])}


def offsets(table):
    at, where = 0, {}
    for name, width in table:
        where[name] = (at, at + width)
        at += width
    return where, at


def landed_before():
    count, before = [0] * NSLOT, {}
    for name, iters, units, slots, dmas in STREAM:
        before[name] = list(count)
        for s in range(slots):
            count[s] += 16 * dmas * iters * (units // slots)
    return before


def units_before():
    count, before = 0, {}
    for name, iters, units, _, _ in STREAM:
        if name != "ada":
            before[name] = count
            count += iters * units
    return before


def feature_major(w):
    return w.rearrange("(k p) n -> p k n", p=P)


def first(i):
    return isinstance(i, int) and i == 0


class Steps:

    def __init__(self, eng, sem):
        self.eng, self.sem, self.base, self.i, self.per, self.n = eng, sem, 0, 0, 0, 0

    def begin(self, i, per=None):
        if first(i) or (per is not None and self.per == 0):
            self.base, self.n = self.base + self.n, 0
        if first(i) and per is None:
            self.i, self.per = 0, 0
        else:
            self.i, self.per = i, self.n if per is None else per
        self.n = 0

    def end(self):
        assert self.per == 0 or self.n == self.per, (self.n, self.per)

    def leave(self, count):
        self.base, self.i, self.per, self.n = self.base + count * self.per, 0, 0, 0

    def mark(self, ins):
        self.n += 1
        ins.then_inc(self.sem, 1)

    def wait(self):
        self.eng.wait_ge(self.sem, self.base + self.i * self.per + self.n)

    def __call__(self, ins):
        self.mark(ins)
        self.wait()


def repeat(eng, count, body):
    body(0)
    if count > 1:
        with eng.Fori(1, count) as i:
            body(i)


def rotated(eng, count, body):
    body(0, count == 1)
    if count > 2:
        with eng.Fori(1, count - 1) as i:
            body(i, False)
    if count > 1:
        body(count - 1, True)


def build(nc, A, out):
    before, unit0 = landed_before(), units_before()
    with ExitStack() as ctx:
        cursor = [SBUF_START]

        def sb(name, shape, dt=F32, at=None):
            where = cursor[0] if at is None else at
            t = nc.alloc_sbuf_tensor_at(name, shape, dt, offset=where, align_bytes=32)
            if at is None:
                cursor[0] += -(-4 * int(np.prod(shape[1:])) // 32) * 32
            return t

        def sem(name):
            return ctx.enter_context(nc.semaphore(name))

        bank = ctx.enter_context(nc.psum_tensor("bank", [P, 8, 512], F32))
        ring = sb("ring", [P, NSLOT, SLOT])
        whi_at = cursor[0]
        whi = sb("whi", [P, 2, SLOT], F32R)
        wlo = sb("wlo", [P, 2, SLOT], F32R)
        res = sb("res", [P, KD, NT])
        hhi_at = cursor[0]
        hhi = sb("hhi", [P, KD, NT], F32R)
        hlo_at = cursor[0]
        hlo = sb("hlo", [P, KD, NT], F32R)
        hT = sb("hraw", [P, KD, NT], at=hlo_at)
        other = sb("other", [P, KD, NT], at=whi_at)
        fT = sb("fT", [P, KD, NT], at=hhi_at)
        pw, pwidth = offsets(PARAMS)
        cw, cwidth = offsets(CONSTS)
        params = sb("params", [P, pwidth])
        consts = sb("consts", [P, cwidth])
        ones = sb("ones", [P, P])
        cact = sb("cact", [P, KD])
        mod = sb("mod", [P, 6, KD])
        gain = sb("gain", [P, 2, KD])
        xhi_at = cursor[0]
        xhi = sb("xhi", [P, 2, 2 * NT], F32R)
        xlo_at = cursor[0]
        xlo = sb("xlo", [P, 2, 2 * NT], F32R)
        sq = sb("sq", [P, 2, NT], at=xhi_at)
        rms = sb("rms", [P, NT], at=xlo_at)
        late_ring = sb("late_ring", [P, NSLOT, LATE], at=xhi_at)
        epsc = sb("epsc", [P, 2])
        omu = sb("omu", [P, 28])
        omka = sb("omka", [P, KW])
        work_at = cursor[0]
        work = sb("work", [P, WORK])
        yhi_at = work_at + 4 * (2 * 8 + KD) * T
        yhi = sb("yhi", [P, KD, T], F32R, at=yhi_at)
        ylo = sb("ylo", [P, KD, T], F32R, at=yhi_at + 4 * KD * T)
        assert cursor[0] <= 229344, cursor

        def param(name, a=None, b=None):
            lo, hi = pw[name]
            return params[:, lo:hi] if a is None else params[:, lo + a:lo + (a + 1 if b is None else b)]

        def pcol(name, i):
            lo, _ = pw[name]
            return params[:, bass.ds(i + lo, 1)] if not isinstance(i, int) else params[:, lo + i:lo + i + 1]

        def const(name):
            lo, hi = cw[name]
            return consts[:, lo:hi]

        def carve(*shapes):
            at, views = 0, []
            for shape in shapes:
                n = int(np.prod(shape))
                v = work[:, at:at + n]
                if len(shape) == 2:
                    v = v.rearrange("p (a b) -> p a b", a=shape[0])
                if len(shape) == 3:
                    v = v.rearrange("p (a b c) -> p a b c", a=shape[0], b=shape[1])
                views.append(v)
                at += n
            assert at <= WORK, at
            return views

        def tile(t, i):
            return t[:, i, :] if isinstance(i, int) else t[:, bass.ds(i, 1), :].rearrange("p a n -> p (a n)")

        def weights(slot, k, n):
            return ring[:, slot, 0:k * n].rearrange("p (k n) -> p k n", k=k)

        def parts(u, k, n):
            return tuple(w[:, u % 2, 0:k * n].rearrange("p (k n) -> p k n", k=k) for w in (whi, wlo))

        params_in, consts_in, pos_in = sem("params_in"), sem("consts_in"), sem("pos_in")
        x_loaded = sem("x_loaded")
        landed = [sem(f"landed{s}") for s in range(NSLOT)]
        hi_done, lo_done, used = sem("hi_done"), sem("lo_done"), sem("used")
        x_hi, x_lo = sem("x_hi"), sem("x_lo")
        tile_done = sem("tile_done")
        h_scaled, h_hi, h_lo = sem("h_scaled"), sem("h_hi"), sem("h_lo")
        y_hi, y_lo = sem("y_hi"), sem("y_lo")
        ada_used, ada_summed = sem("ada_used"), sem("ada_summed")
        late_landed = [sem(f"late_landed{n}") for n in range(NSLOT)]
        late_used, late_summed = sem("late_used"), sem("late_summed")
        lora_landed, gate_landed = sem("lora_landed"), sem("gate_landed")
        phase_done = sem("phase_done")
        act_step, dve_step, pool_step = sem("act_step"), sem("dve_step"), sem("pool_step")
        ones_set = sem("ones_set")
        stored = sem("stored")
        squared, summed, rooted, normed, shifted = (sem(n) for n in ("squared", "summed", "rooted", "normed", "shifted"))
        z_done, s_done, o_done, zm_done, sp_done, l_done, d_done, w_done = (
            sem(n) for n in ("z_done", "s_done", "o_done", "zm_done", "sp_done", "l_done", "d_done", "w_done"))
        q_read, k_read, v_read, q2_read, k2_read, v2_read = (
            sem(n) for n in ("q_read", "k_read", "v_read", "q2_read", "k2_read", "v2_read"))
        angle_done, sines, dots_done, relu_done, relu_used = (
            sem(n) for n in ("angle_done", "sines", "dots_done", "relu_done", "relu_used"))
        logits_done, max_done, exp_done, probs_done, turned, turned_read, o2_done = (
            sem(n) for n in ("logits_done", "max_done", "exp_done", "probs_done", "turned", "turned_read", "o2_done"))
        merge_read = [sem(f"merge_read{s}") for s in range(4)]
        merged, tap_done, silu_done, acted = sem("merged"), sem("tap_done"), sem("silu_done"), sem("acted")
        cact_ready = sem("cact_ready")
        meta_loaded = sem("meta_loaded")
        b_copied, x_read = sem("b_copied"), sem("x_read")
        c_copied, own_done, lora_ready, tap2_done, silu2_done = (
            sem(n) for n in ("c_copied", "own_done", "lora_ready", "tap2_done", "silu2_done"))
        kk_squared, kk_summed, kk_floored, kk_rooted = (sem(n) for n in ("kk_squared", "kk_summed", "kk_floored", "kk_rooted"))
        cum_done, exps_done, feat_done, n_raw, g0_done, t0_raw, t0_ready, nm_ready, w1_raw, w1_ready, tg_raw, tg_ready = (
            sem(n) for n in ("cum_done", "exps_done", "feat_done", "n_raw", "g0_done", "t0_raw", "t0_ready", "nm_ready",
                             "w1_raw", "w1_ready", "tg_raw", "tg_ready"))
        task_done, tok_read, mat_read, x_raw, x_ready, u_raw, u_ready, h_raw, h_ready, y_raw, pair_done = (
            sem(n) for n in ("task_done", "tok_read", "mat_read", "x_raw", "x_ready", "u_raw", "u_ready", "h_raw", "h_ready",
                             "y_raw", "pair_done"))
        mean_raw, centred, y_squared, var_raw, var_read, gate_tiles = (
            sem(n) for n in ("mean_raw", "centred", "y_squared", "var_raw", "var_read", "gate_tiles"))
        loraup_tiles, loraup_evac = sem("loraup_tiles"), sem("loraup_evac")
        evac = {n: sem(f"{n}_evac") for n, *_ in STREAM}

        def arrived(eng, phase, u, i):
            _, _, units, slots, dmas = PLAN[phase]
            n = 16 * dmas
            eng.wait_ge(landed[u % slots], before[phase][u % slots] + n * (u // slots + 1) + i * (n * (units // slots)))

        def multiplied(eng, phase, u, i):
            eng.wait_ge(used, twice(phase, u, i) + 2)

        def twice(phase, u, i):
            return i * (2 * PLAN[phase][2]) + 2 * (unit0[phase] + u)

        def half_of(t, u, h, n):
            return t[:, u % 2, h * SLOT // 2:(h * SLOT + n) // 2]

        def round_unit(phase, u, i, n=SLOT):
            arrived(nc.scalar, phase, u, i)
            for h in range(2):
                if unit0[phase] or u >= 2 or not isinstance(i, int) or i:
                    nc.scalar.wait_ge(used, twice(phase, u, i) + (h - 3))
                nc.scalar.activation(half_of(whi, u, h, n), ring[:, u % PLAN[phase][3], h * n // 2:(h + 1) * n // 2], ACT.Copy)\
                    .then_inc(hi_done, 1)

        def rest_unit(phase, u, i, n=SLOT):
            for h in range(2):
                nc.vector.wait_ge(hi_done, twice(phase, u, i) + (h + 1))
                nc.vector.tensor_tensor(half_of(wlo, u, h, n), ring[:, u % PLAN[phase][3], h * n // 2:(h + 1) * n // 2],
                                        half_of(whi, u, h, n).bitcast(F32), ALU.subtract).then_inc(lo_done, 1)

        def is_split(pe, phase, u, h, i):
            pe.wait_ge(lo_done, twice(phase, u, i) + (h + 1))

        KI_N = KH * 144

        def ahead(split, phase, i, last):
            for u in range(2):
                if last:
                    if phase in AFTER:
                        split(AFTER[phase], u, 0, *((KI_N,) if AFTER[phase] == "ki" else ()))
                else:
                    split(phase, u, i + 1)

        X_PHASES = ("wo", "down", "mix2", "down2")
        xunit0, n_x = {}, 0
        for name in X_PHASES:
            xunit0[name] = n_x
            n_x += PLAN[name][1] * PLAN[name][2]

        def x_number(phase, u, i):
            return i * PLAN[phase][2] + (xunit0[phase] + u)

        def x_buf(t, u, n):
            return t[:, u % 2, 0:n]

        def round_x(phase, u, i, srcs):
            if isinstance(i, int) and i == 0 and u < 2:
                pass
            else:
                nc.scalar.wait_ge(used, twice(phase, u, i) - 2)
            at = 0
            for src in srcs:
                n = src.shape[-1]
                last = nc.scalar.activation(xhi[:, u % 2, at:at + n], src, ACT.Copy)
                at += n
            last.then_inc(x_hi, 1)

        def rest_x(phase, u, i, srcs):
            nc.vector.wait_ge(x_hi, x_number(phase, u, i) + 1)
            at = 0
            for src in srcs:
                n = src.shape[-1]
                last = nc.vector.tensor_tensor(xlo[:, u % 2, at:at + n], src, xhi[:, u % 2, at:at + n].bitcast(F32), ALU.subtract)
                at += n
            last.then_inc(x_lo, 1)

        def threefold(out_ap, a, b, start, stop):
            kw = dict(skip_group_check=True)
            nc.tensor.matmul(out_ap, a[0], b[0], start=start, stop=False, **kw)
            nc.tensor.matmul(out_ap, a[0], b[1], start=False, stop=False, **kw)
            return nc.tensor.matmul(out_ap, a[1], b[0], start=False, stop=stop, **kw)

        def products(out_ap, pairs, **kw):
            last = None
            for n, (a, b) in enumerate(pairs):
                last = nc.tensor.matmul(out_ap, a, b, start=n == 0, stop=n == len(pairs) - 1, **kw)
            return last

        ends = [0]

        (yaT, ybT, mergedT, qT, kT, vS, s_a, s_b, s_c, s_d, s_e, s_f, small, biasM, tabs128, tabs64) = carve(
            (8, T), (8, T), (KD, T), (2, T), (2, T), (2, T),
            (2, 384), (2, 384), (2, 384), (2, 384), (2, 384), (2, 384), (1, 64), (1, 384), (2, 2 * T), (2, T))
        ropeA = mergedT[:, 0:2, :].rearrange("p a t -> p (a t)")
        ropeB = mergedT[:, 2:4, :].rearrange("p a t -> p (a t)")
        angles = mergedT[:, 4:8, :]
        turns = mergedT[:, 8:12, :]
        qiT = mergedT[:, 4:12, :]
        kiT = mergedT[:, 12, :]
        relu = mergedT[:, 13:16, :].rearrange("p a t -> p (a t)")
        posf = mergedT[:, 12, :]
        posi = mergedT[:, 13, :].bitcast(I32)
        small = small[:, 0, :]
        late_acc = work[:, WORK - LATE:WORK]
        acc = work[:, 0:2 * D].rearrange("p (b n) -> p b n", b=2)
        past, seen = const("past"), const("seen")
        gates_at = 2 * 8 * T + KD * T + 2 * KD * T
        gates = work[:, gates_at:gates_at + 4 * T].rearrange("p (a t) -> p a t", a=4)
        assert gates_at + 4 * T <= WORK - LATE
        actT, cv, sa = carve((KF, T), (8, NT), (4, T))
        yconv, zr, lw, aa, kk, gd, NM, tokK, tokB, tokV = carve(
            (KW, NT), (3 * KW, NT), (KW, NT), (KW, NT), (KW, NT), (2, NT), (2, 2 * NT), (NC, P), (NC, P), (NC, P))
        low = hT[:].rearrange("p k t -> p (k t)")
        TT, G, N, W1, lak, lrk, lrb = (low[:, n * 2 * NT:(n + 1) * 2 * NT].rearrange("p (a t) -> p a t", a=2) for n in range(7))
        XU = low[:, 14 * NT:14 * NT + 2 * P].rearrange("p (a t) -> p a t", a=2)
        Xs, Us = XU[:, 0, :], XU[:, 1, :]
        bs, cs, chs, ycs = carve((KW, NT), (3 * KW, NT), (2, NT), (2, NT), (2, NT + HALO), (2, NT))[2:]
        wdad = carve((KW, NT), (3 * KW, NT), (KW, NT), (KW, NT), (KW, NT), (2, NT), (2, NT))[6]
        temp8, temp8b = fT[:, 0:KW, :], fT[:, KW:KD, :]

        def pair_tiles(par):
            t = (fT, other)[par]
            flat_ = t[:].rearrange("p k t -> p (k t)")
            return (*(t[:, k, :] for k in range(12)),
                    flat_[:, 12 * NT:14 * NT].rearrange("p (c a t) -> p c a t", c=NC, a=2),
                    flat_[:, 14 * NT + 3 * RN:14 * NT + 3 * RN + NC], flat_[:, 14 * NT + 3 * RN + 8:14 * NT + 3 * RN + 8 + NC])
        hflat = fT[:].rearrange("p k t -> p (k t)")
        Hs = hflat[:, 14 * NT:14 * NT + 2 * RN].rearrange("p (a v) -> p a v", a=2)
        Hsum = hflat[:, 14 * NT + 2 * RN:14 * NT + 3 * RN]
        onesrow = ones[:, 0:L]

        def all8(x):
            return x.rearrange("p a t -> p (a t)")
        SCALE = HD ** -0.5

        TOLD = {name: n * KD for n, name in enumerate(("wo", "down", "g_final", "mixed", "down2", "result"))}

        block = ctx.enter_context(nc.Block())

        def phase_end(eng, n, meet=True):
            eng.drain().then_inc(phase_done, 1)
            if meet:
                eng.wait_ge(phase_done, 3 * n)

        @block.sync
        def _(sp):
            sp.dma_start(params[:], A["params"]).then_inc(params_in, 16)
            sp.dma_start(consts[:], A["consts"]).then_inc(consts_in, 16)
            sp.dma_start(res[:, :, META:NT], A["xT"]).then_inc(x_loaded, 16)
            sp.dma_start(posi, A["pos"]).then_inc(pos_in, 16)
            free = [None] * NSLOT

            def phase(name, units):
                _, count, per, slots, _ = PLAN[name]

                def read(u, i):
                    return (ada_used, i * per + (u + 1)) if name == "ada" else (lo_done, twice(name, u, i) + 2)

                def body(i):
                    for u in range(per):
                        if first(i) and u < slots:
                            if free[u] is not None:
                                sp.wait_ge(*free[u])
                        else:
                            sp.wait_ge(*read(u - slots, i))
                        for dst, src in units(u, i):
                            sp.dma_start(dst, src).then_inc(landed[u % slots], 16)
                repeat(sp, count, body)
                for s in range(slots):
                    free[s] = read(per - slots + s, count - 1)

            def half_unit(w, slot, u, col):
                lo = (u % 2) * KH if w.shape[0] > W else 0
                v = feature_major(w)[:, lo:lo + KH, :]
                v = v[:, :, col:col + UNIT] if isinstance(col, int) else v[:, :, bass.ds(col, UNIT)]
                return [(weights(slot, KH, UNIT), v)]

            def halves_of(name, w, col0, step):
                slots = PLAN[name][3]
                return lambda u, i: half_unit(w, u % slots, u, col0(u // 2) + i * step)

            def row_units(w):
                def units(u, i):
                    row = i * 4 + u
                    v = feature_major(w)
                    v = v[:, row:row + 1, :] if isinstance(row, int) else v[:, bass.ds(row, 1), :]
                    return [(weights(u, 1, D), v)]
                return units

            def ada_units(u, i):
                v = feature_major(A["w_ada"])[:, u % KD:u % KD + 1, :]
                return [(weights(u % NSLOT, 1, D), v[:, :, (u // KD) * D:(u // KD + 1) * D])]
            phase("ada", ada_units)
            phase("sb", halves_of("sb", A["w_in"], lambda s: SB_OFF + s * W, UNIT))
            wv = feature_major(A["w_in"])

            def ki_units(u, i):
                w144, k = weights(u, KH, 144), slice(u * KH, (u + 1) * KH)
                return [(w144[:, :, 0:64], wv[:, k, KI_OFF:KI_OFF + IDX_D]),
                        (w144[:, :, 64:128], wv[:, k, KI_OFF:KI_OFF + IDX_D]),
                        (w144[:, :, 128:144], wv[:, k, WI_OFF:WI_OFF + IDX_HEADS])]
            phase("ki", ki_units)
            phase("qi", halves_of("qi", A["w_in"], lambda s: QI_OFF + s * UNIT, 0))
            phase("dsa", halves_of("dsa", A["w_in"], lambda s: DSA_OFF + s * W, UNIT))

            def merge_units(u, i):
                if u < 2:
                    return half_unit(A["w_a"] if u == 0 else A["w_b"], u, u, i * UNIT)
                return half_unit(A["w_in"], u % 3, u, i * UNIT + (GATE_OFF + (u // 2 - 1) * D))
            phase("merge", merge_units)
            phase("wo", row_units(A["w_o"]))

            def up_units(name, w):
                return halves_of(name, w, lambda s: (s % 2) * F + (s // 2) * UNIT, 2 * UNIT)
            phase("up", up_units("up", A["w_up"]))
            phase("down", row_units(A["w_down"]))
            w2 = A["w_in_2"]
            phase("conv2", halves_of("conv2", w2, lambda s: s * W, UNIT))
            phase("rkv", halves_of("rkv", w2, lambda s: RW_OFF + s * UNIT, W))

            def lora_units(u, i):
                k = slice((u % 2) * KH, (u % 2 + 1) * KH)
                cols = (GD_OFF, GD_OFF + P) if u < 2 else (LORA_OFF, LORA_OFF + LORA)
                return [(weights(u, KH, UNIT)[:, :, t * P:(t + 1) * P], feature_major(w2)[:, k, c:c + P])
                        for t, c in enumerate(cols)]
            phase("lora", lora_units)
            sp.wait_ge(*free[2])
            sp.dma_start(ring[0:LORA, 2, 0:W], A["w_decay_up_2"]).then_inc(lora_landed, 16)
            sp.dma_start(ring[0:LORA, 2, W:2 * W], A["a_up_2"]).then_inc(lora_landed, 16)
            sp.wait_ge(*free[3])
            sp.dma_start(weights(3, 2, W), feature_major(A["g_up_2"])).then_inc(gate_landed, 16)
            free[2], free[3] = (loraup_tiles, 2 * KW), (gate_tiles, KW)

            def mix_units(u, i):
                v = feature_major(A["w_out_2"])[:, 2 * u:2 * u + 2, :]
                return [(weights(u % NSLOT, 2, W), v[:, :, i * W:(i + 1) * W])]
            phase("mix2", mix_units)
            phase("up2", up_units("up2", A["w_gate_up_2"]))
            phase("down2", row_units(A["w_down_2"]))
            for q in range(4):
                k = slice(q * KD // 4, (q + 1) * KD // 4)
                sp.wait_ge(tile_done, TOLD["result"] + k.stop)
                sp.dma_start(out[:, k, :], res[:, k, META:NT]).then_inc(stored, 16)
            sp.wait_ge(stored, 4 * 16)

        norms = {"act": 0, "pe": 0, "dve": 0}
        def norm_act(act, src, n, step, ready=None):
            m = norms["act"]
            norms["act"] += 1
            for k in range(KD):
                if ready:
                    act.wait_ge(ready[0], ready[1] + k + 1)
                if k >= 2 or m:
                    act.wait_ge(summed, KD * m + k - 1)
                nc.scalar.activation(sq[:, k % 2, 0:n], src[:, k, :], ACT.Square).then_inc(squared, 1)
            act.wait_ge(summed, KD * (m + 1))
            nc.scalar.activation(rms[:, 0:n], bank[:, 0, 0:n], ACT.Sqrt, scale=1.0 / D, bias=epsc[:, 0:1]).then_inc(rooted, 1)

        def norm_pe(pe, n, free=None):
            m = norms["pe"]
            norms["pe"] += 1
            if free:
                pe.wait_ge(*free)
            for k in range(KD):
                pe.wait_ge(squared, KD * m + k + 1)
                nc.tensor.matmul(bank[:, 0, 0:n], ones[:], sq[:, k % 2, 0:n], start=k == 0, stop=k == KD - 1)\
                    .then_inc(summed, 1)

        def norm_dve(dve, n, step, apply):
            m = norms["dve"]
            norms["dve"] += 1
            dve.wait_ge(rooted, m + 1)
            step(nc.vector.reciprocal(rms[:, 0:n], rms[:, 0:n]))
            for k in range(KD):
                last = apply(k)
            if last is not None:
                step(last)

        def scaled(dst, src, g, n):
            def apply(k):
                nc.vector.scalar_tensor_tensor(dst[:, k, :], src[:, k, :], g[:, k:k + 1], rms[:, 0:n], ALU.mult, ALU.mult)\
                    .then_inc(tile_done, 1)
            return apply

        handed = {"act": 0, "dve": 0}

        def hand_act(n, shift=None):
            m = handed["act"]
            handed["act"] += 1
            for k in range(KD):
                nc.scalar.wait_ge(h_scaled, KD * m + k + 1)
                if shift is None:
                    ins = nc.scalar.activation(hhi[:, k, 0:n], hT[:, k, 0:n], ACT.Copy)
                else:
                    ins = nc.scalar.activation(hhi[:, k, 0:n], hT[:, k, 0:n], ACT.Identity, bias=shift[:, k:k + 1])
                ins.then_inc(h_hi, 1)

        def hand_dve(src, g, n, shift=None):
            m = handed["dve"]
            handed["dve"] += 1
            lag = 3
            for at in range(KD + lag):
                if at < KD:
                    nc.vector.scalar_tensor_tensor(hT[:, at, 0:n], src[:, at, :], g[:, at:at + 1], rms[:, 0:n], ALU.mult, ALU.mult)\
                        .then_inc(h_scaled, 1)
                k = at - lag
                if k < 0:
                    continue
                nc.vector.wait_ge(h_hi, KD * m + k + 1)
                nc.vector.scalar_tensor_tensor(hlo[:, k, 0:n], hT[:, k, 0:n], 0.0 if shift is None else shift[:, k:k + 1],
                                               hhi[:, k, 0:n].bitcast(F32), ALU.add, ALU.subtract).then_inc(h_lo, 1)

        def norm_dve_handing(dve, src, g, n, step, shift=None):
            m = norms["dve"]
            norms["dve"] += 1
            dve.wait_ge(rooted, m + 1)
            step(nc.vector.reciprocal(rms[:, 0:n], rms[:, 0:n]))
            hand_dve(src, g, n, shift)

        x1 = res[:, :, META:NT]
        h1 = (hhi[:, :, 0:T], hlo[:, :, 0:T])

        @block.tensor
        def _(pe):
            pe.wait_ge(ones_set, 1)
            pe.wait_ge(consts_in, 16)
            norm_pe(pe, T)
            handed_on = [0]

            def hand_over(quarter):
                pe.wait_ge(h_lo, KD * (handed_on[0] - 1) + (quarter + 1) * (KD // 4))

            for b in range(2):
                pe.wait_ge(ada_used, (b + 1) * KD)
                for m in range(KD):
                    last = nc.tensor.matmul(bank[:, 1, b * KD + m:b * KD + m + 1], acc[:, b, m * P:(m + 1) * P],
                                            ones[:, 0:1], start=True, stop=True)
                last.then_inc(ada_summed, 1)

            def late_sum(b):
                pe.wait_ge(late_used, b * KD + KD)
                for m in range(LATE // P):
                    col = b * (LATE // P) + (LATE_AT + m)
                    dst = bank[:, 7, col:col + 1] if isinstance(b, int) else bank[:, 7, bass.ds(col, 1)]
                    last = nc.tensor.matmul(dst, late_acc[:, m * P:(m + 1) * P], ones[:, 0:1], start=True, stop=True)
                last.then_inc(late_summed, 1)
            phase_end(pe, 1)
            phase_end(pe, 2, meet=False)
            handed_on[0] += 1

            def halves(quarter, k=KH):
                return range(quarter % 2 * (k // 2), (quarter % 2 + 1) * (k // 2))

            def project(phase, n, i, token_major, dst):
                for quarter in range(4):
                    half = quarter // 2
                    if first(i) and n == 0 and phase == "sb":
                        hand_over(quarter)
                    is_split(pe, phase, 2 * n + half, quarter % 2, i)
                    w = parts(half, KH, UNIT)
                    for t in range(2):
                        tt = slice(t * P, (t + 1) * P)
                        for k in halves(quarter):
                            kk_ = half * KH + k
                            if token_major:
                                a, b = [x[:, kk_, tt] for x in h1], [x[:, k, :] for x in w]
                            else:
                                a, b = [x[:, k, tt] for x in w], [x[:, kk_, :] for x in h1]
                            last = threefold(bank[:, dst, t * T:(t + 1) * T], a, b, kk_ == 0 and t == 0,
                                             half == 1 and k == KH - 1)
                    last.then_inc(used, 1)

            def attend_values(e, probs):
                o = bank[:, 3, e * T:(e + 1) * T]
                nc.tensor.matmul(o, vS[:, 0, e * HD:(e + 1) * HD], probs[:, e, 0:T], start=True, stop=False)
                return nc.tensor.matmul(o[:, P:T], vS[:, 1, e * HD:(e + 1) * HD], probs[:, e, T:384], start=False, stop=True)

            def sb(i, head=True, tail=True):
                if head:
                    if not first(i):
                        pe.wait_ge(q_read, i)
                    project("sb", 0, i, False, 0)
                if tail:
                    pe.wait_ge(q_read, i)
                    pe.wait_ge(k_read, i)
                    for e in range(2):
                        z = bank[:, 4 + e, :]
                        nc.tensor.matmul(z[:, 0:T], kT[:, e, 0:P], qT[:, e, :], start=True, stop=True)
                        nc.tensor.matmul(z[:, T:384], kT[:, e, P:T], qT[:, e, P:T], start=True, stop=True)\
                            .then_inc(z_done, 1)
                if not first(i):
                    late_sum(i + -1)
                if head:
                    project("sb", 1, i, False, 1)
                if tail:
                    for e in range(2):
                        pe.wait_ge(sp_done, i * 2 + (e - 1))
                        sp_ = s_e[:, e, :]
                        nc.tensor.matmul(bank[:, 6 + e, 0:T], const("tri"), sp_[:, 0:T], start=True, stop=False)
                        nc.tensor.matmul(bank[:, 6 + e, P:T], ones[:], sp_[:, T:384], start=False, stop=True)
                        nc.tensor.matmul(bank[:, 6 + e, T:384], const("tri"), sp_[:, T:384], start=True, stop=True)\
                            .then_inc(s_done, 1)
                if head:
                    if not first(i):
                        pe.wait_ge(v_read, i)
                    project("sb", 2, i, True, 2)
                if tail:
                    pe.wait_ge(v_read, i)
                    for e in range(2):
                        pe.wait_ge(w_done, i * 2 + (e - 1))
                        attend_values(e, s_f).then_inc(o_done, 1)

            def overlapped(body, count):
                body(0, tail=False)
                with pe.Fori(1, count) as i:
                    body(i)
                body(count, head=False)
            overlapped(sb, 4)
            phase_end(pe, 3)

            for quarter in range(4):
                half = quarter // 2
                is_split(pe, "ki", half, quarter % 2, 0)
                w = [half_of(x, half, quarter % 2, KI_N).rearrange("p (k n) -> p k n", k=KH // 2) for x in (whi, wlo)]
                tiles_in = [(k, quarter * (KH // 2) + k) for k in range(KH // 2)]
                for k, kk_ in tiles_in:
                    threefold(bank[:, 6, 0:T], [x[:, k, 0:P] for x in w], [x[:, kk_, :] for x in h1], kk_ == 0, kk_ == KD - 1)
                for t in range(2):
                    for k, kk_ in tiles_in:
                        last = threefold(bank[:, 7, t * IDX_HEADS:(t + 1) * IDX_HEADS],
                                         [x[:, kk_, t * P:(t + 1) * P] for x in h1], [x[:, k, P:144] for x in w],
                                         kk_ == 0 and t == 0, kk_ == KD - 1)
                last.then_inc(used, 1)

            def pair_of_tiles(phase, s, i, rhs, width, free):
                for quarter in range(4):
                    half = quarter // 2
                    if first(i) and s == 0 and phase in ("up", "conv2", "up2"):
                        hand_over(quarter)
                    is_split(pe, phase, 2 * s + half, quarter % 2, i)
                    w = parts(half, KH, UNIT)
                    for t in range(2):
                        q = 2 * s + t
                        if quarter == 0:
                            free(q)
                        for k in halves(quarter):
                            last = threefold(bank[:, q, 0:width], [x[:, k, t * P:(t + 1) * P] for x in w],
                                             [x[:, half * KH + k, :] for x in rhs], half == 0 and k == 0,
                                             half == 1 and k == KH - 1)
                    last.then_inc(used, 1)

            for s in range(4):
                pair_of_tiles("qi", s, 0, h1, T, lambda q: pe.wait_ge(evac["ki"], 2) if q == 6 else None)
            for h in range(IDX_HEADS):
                j, e = h // 2, 64 * (h % 2)
                if h < 8:
                    pe.wait_ge(evac["qi"], 8)
                    pe.wait_ge(evac["ki"], 2)
                else:
                    pe.wait_ge(relu_done, h - 7)
                d = bank[:, h % 8, :]
                nc.tensor.matmul(d[:, 0:P], qiT[e:e + 64, j, 0:P], kiT[e:e + 64, 0:P], start=True, stop=True)
                nc.tensor.matmul(d[:, P:384], qiT[e:e + 64, j, P:T], kiT[e:e + 64, :], start=True, stop=True)\
                    .then_inc(dots_done, 1)
            phase_end(pe, 4)

            def dsa(i, head=True, tail=True):
                if head:
                    if not first(i):
                        pe.wait_ge(q2_read, i)
                    project("dsa", 0, i, False, 0)
                if tail:
                    pe.wait_ge(q2_read, i)
                    pe.wait_ge(k2_read, i)
                    for e in range(2):
                        z = bank[:, 4 + e, :]
                        nc.tensor.matmul(z[:, 0:P], qT[:, e, 0:P], kT[:, e, 0:P], start=True, stop=True)
                        nc.tensor.matmul(z[:, P:384], qT[:, e, P:T], kT[:, e, :], start=True, stop=True)\
                            .then_inc(logits_done, 1)
                if not first(i):
                    late_sum(i + 3)
                if head:
                    project("dsa", 1, i, False, 1)
                if tail:
                    for e in range(2):
                        pe.wait_ge(probs_done, i * 2 + (e - 1))
                        for n in range(3):
                            last = nc.tensor.transpose(bank[:, 6 + e, n * P:(n + 1) * P], s_c[:, e, n * P:(n + 1) * P],
                                                       const("ident"))
                        last.then_inc(turned, 1)
                if head:
                    if not first(i):
                        pe.wait_ge(v2_read, i)
                    project("dsa", 2, i, True, 2)
                if tail:
                    pe.wait_ge(v2_read, i)
                    for e in range(2):
                        pe.wait_ge(turned_read, i * 2 + (e - 1))
                        attend_values(e, s_f).then_inc(o2_done, 1)
            overlapped(dsa, 4)
            phase_end(pe, 5)

            pe.wait_ge(y_lo, 1)

            def merge(i):
                def free(q):
                    if not first(i):
                        pe.wait_ge(merge_read[q // 2], i * 2 + (q % 2 - 1))
                for s in range(2):
                    for h in range(2):
                        is_split(pe, "merge", s, h, i)
                        w = parts(s, KW, UNIT)
                        for t in range(2):
                            if h == 0:
                                free(2 * s + t)
                            for k in halves(h):
                                last = threefold(bank[:, 2 * s + t, 0:T], [x[:, k, t * P:(t + 1) * P] for x in w],
                                                 [x[:, s * KW + k, :] for x in (yhi, ylo)], k == 0, k == KW - 1)
                        last.then_inc(used, 1)
                if not first(i):
                    pe.wait_ge(merge_read[3], i * 2)
                    late_sum(i + 7)
                for s in (2, 3):
                    for quarter in range(4):
                        half = quarter // 2
                        is_split(pe, "merge", 2 * s - 2 + half, quarter % 2, i)
                        w = parts(half, KH, UNIT)
                        for t in range(2):
                            if quarter == 0:
                                free(2 * s + t)
                            for k in halves(quarter):
                                last = threefold(bank[:, 2 * s + t, 0:T], [x[:, k, t * P:(t + 1) * P] for x in w],
                                                 [x[:, half * KH + k, :] for x in h1], half == 0 and k == 0,
                                                 half == 1 and k == KH - 1)
                        last.then_inc(used, 1)
            repeat(pe, 8, merge)
            pe.wait_ge(merge_read[3], 16)
            late_sum(NLATE - 1)
            phase_end(pe, 6)

            def linear(phase, src, free=None):
                _, count, per, _, _ = PLAN[phase]

                def body(i):
                    def bank_free(q):
                        if not first(i):
                            if free:
                                free(i, q)
                            else:
                                pe.wait_ge(evac[phase], i * per + (q + 1 - per))
                    for s in range(per // 2):
                        pair_of_tiles(phase, s, i, *src(s), bank_free)
                repeat(pe, count, body)

            def by_rows(phase):
                _, count, per, _, _ = PLAN[phase]

                def body(i):
                    for u in range(per):
                        pe.wait_ge(x_lo, x_number(phase, u, i) + 1)
                        b = [x_buf(x, u, T) for x in (xhi, xlo)]
                        for h in range(2):
                            is_split(pe, phase, u, h, i)
                            for m in range(h * KW, (h + 1) * KW):
                                last = threefold(bank[:, m // 2, (m % 2) * T:(m % 2 + 1) * T],
                                                 [x[:, u % 2, m * P:(m + 1) * P] for x in (whi, wlo)], b,
                                                 first(i) and u == 0 and m % 2 == 0, False)
                            last.then_inc(used, 1)
                repeat(pe, count, body)

            by_rows("wo")
            phase_end(pe, 7, meet=False)
            norm_pe(pe, T, free=(tile_done, TOLD["wo"] + 2))
            phase_end(pe, 8, meet=False)
            handed_on[0] += 1
            linear("up", lambda s: (h1, T))
            phase_end(pe, 9)
            by_rows("down")
            phase_end(pe, 10, meet=False)
            norm_pe(pe, T, free=(tile_done, TOLD["down"] + 2))
            phase_end(pe, 11, meet=False)

            norm_pe(pe, NT)
            phase_end(pe, 12, meet=False)
            handed_on[0] += 1
            hboth = (hhi, hlo)
            linear("conv2", lambda s: (hboth, NT), free=lambda i, q: pe.wait_ge((b_copied, c_copied, x_read)[q // 2], i * 2 + (q % 2 - 1)))
            phase_end(pe, 13)
            linear("rkv", lambda s: (hboth, NT))
            phase_end(pe, 14)
            linear("lora", lambda s: (hboth, NT))
            pe.wait_ge(lora_landed, 32)
            pe.wait_ge(lora_ready, 2)
            for u in range(2):
                for j in range(KW):
                    if u == 0:
                        if j == 0:
                            pe.wait_ge(evac["lora"], 4)
                    else:
                        pe.wait_ge(loraup_evac, j + 1)
                    nc.tensor.matmul(bank[:, j, 0:NT], ring[0:LORA, 2, u * W + j * P:u * W + (j + 1) * P],
                                     wdad[0:LORA, u, :], start=True, stop=True).then_inc(loraup_tiles, 1)
            for j in range(KW):
                pe.wait_ge(kk_squared, 1)
                pe.wait_ge(loraup_evac, KW + j + 1)
                nc.tensor.matmul(bank[:, j, 0:NT], const("heads"), temp8[:, j, :], start=True, stop=True).then_inc(kk_summed, 1)
            phase_end(pe, 15)

            def keep_warm(b, count):
                for _ in range(count):
                    nc.tensor.matmul(bank[:, b, 0:T], ones[:], consts[:, 0:T], start=True, stop=True)

            def chunk(x, c):
                return x[:, c * L:(c + 1) * L]

            def recur(i, par):
                cum, cumc, cpm, Ep, Em, Epm, k2, bb, kt, bt, rkr, vt, AR, ecm, mids = pair_tiles(par)
                rows = [slice(0, RN), slice(RN, P)]

                def task(n):
                    b = 6 + n % 2
                    if n in (2, 3, 4):
                        pe.wait_ge(tok_read, i * 3 + (n - 1))
                    if n > 4:
                        pe.wait_ge(mat_read, i * 7 + (n - 4))
                    if n < 3:
                        src = (kt, bt, vt)[n]
                        for c in range(NC):
                            last = nc.tensor.transpose(bank[0:L, b, c * P:(c + 1) * P], chunk(src, c), const("ident"))
                    elif n < 9:
                        kind, e = (n - 3) // 2, (n - 3) % 2
                        lhs, which = ((kt, 0), (kt, 1), (bt, 1))[kind]
                        for c in range(NC):
                            last = nc.tensor.matmul(bank[0:L, b, c * L:(c + 1) * L], chunk(lhs, c)[rows[e], :],
                                                    AR[rows[e], c, which, :], start=True, stop=True)
                    else:
                        last = nc.tensor.matmul(bank[:, b, 0:NT], const("heads"), rkr, start=True, stop=True)
                    last.then_inc(task_done, 1)

                pe.wait_ge(feat_done, i + 1)
                for e in range(2):
                    for c in range(NC):
                        last = nc.tensor.matmul(bank[0:L, e, c * L:(c + 1) * L], chunk(bt, c)[rows[e], :],
                                                AR[rows[e], c, 0, :], start=True, stop=True)
                    last.then_inc(n_raw, 1)
                keep_warm(3, 8)
                for e in range(2):
                    pe.wait_ge(g0_done, i * 2 + (e + 1))
                    for c in range(NC):
                        last = nc.tensor.transpose(bank[0:L, 2 + e, c * L:(c + 1) * L], G[0:L, e, c * L:(c + 1) * L],
                                                   const("ident")[0:L, 0:L])
                    last.then_inc(t0_raw, 1)
                nl = len(LEVELS)
                for l in range(nl):
                    for e in range(2):
                        pe.wait_ge(nm_ready, i * 2 * nl + (2 * l + e + 1))
                        if l == 0:
                            pe.wait_ge(t0_ready, i * 2 + (e + 1))
                        else:
                            pe.wait_ge(tg_ready, i * 2 * nl + (2 * (l - 1) + e + 1))
                        for c in range(NC):
                            cc = slice(c * L, (c + 1) * L)
                            last = nc.tensor.matmul(bank[0:L, e, cc], NM[0:L, l % 2, e * NT + c * L:e * NT + (c + 1) * L],
                                                    TT[0:L, e, cc], start=True, stop=True)
                        last.then_inc(w1_raw, 1)
                        if 2 * l + e < 10:
                            task(2 * l + e)
                    for e in range(2):
                        pe.wait_ge(w1_ready, i * 2 * nl + (2 * l + e + 1))
                        for c in range(NC):
                            cc = slice(c * L, (c + 1) * L)
                            if l < nl - 1:
                                nc.tensor.matmul(bank[0:L, 2 + e, cc], G[0:L, e, cc], W1[0:L, e, cc], start=True, stop=True)
                        for c in range(NC):
                            cc = slice(c * L, (c + 1) * L)
                            last = nc.tensor.matmul(bank[0:L, 4 + e, cc], W1[0:L, e, cc], G[0:L, e, cc], start=True, stop=True)
                        last.then_inc(tg_raw, 1)
                pe.wait_ge(tg_ready, i * 2 * nl + 2 * nl)
                pe.wait_ge(mat_read, i * 7 + 7)
                for c in range(NC):
                    cc = slice(c * L, (c + 1) * L)
                    H = Hs[:, c % 2, :]
                    for e in range(2):
                        v = tokV[0:L, c, e * RN:(e + 1) * RN]
                        last = nc.tensor.matmul(bank[0:L, e, 0:RN], lak[0:L, e, cc], v, start=True, stop=c == 0)
                        if c:
                            if e == 0:
                                pe.wait_ge(h_ready, i * 3 + c)
                            last = nc.tensor.matmul(bank[0:L, e, 0:RN], AR[rows[e], c, 0, :], H[rows[e], :],
                                                    start=False, stop=True)
                    last.then_inc(x_raw, 1)
                    keep_warm(2, 2)
                    pe.wait_ge(x_ready, i * NC + (c + 1))
                    for e in range(2):
                        last = nc.tensor.matmul(bank[0:L, 2, e * RN:(e + 1) * RN], G[0:L, e, cc], Xs[0:L, e * RN:(e + 1) * RN],
                                                start=True, stop=True)
                    last.then_inc(u_raw, 1)
                    keep_warm(3, 2)
                    pe.wait_ge(u_ready, i * NC + (c + 1))
                    if c < NC - 1:
                        for e in range(2):
                            ee = slice(e * RN, (e + 1) * RN)
                            nc.tensor.matmul(bank[rows[e], 3, 0:RN], tokK[0:L, c, ee], tokV[0:L, c, ee], start=True, stop=False)
                            last = nc.tensor.matmul(bank[rows[e], 3, 0:RN], tokB[0:L, c, ee], Us[0:L, ee], start=False, stop=True)
                        last.then_inc(h_raw, 1)
                    for e in range(2):
                        ee = slice(e * RN, (e + 1) * RN)
                        nc.tensor.matmul(bank[rows[e], 4 + e, cc], tokV[0:L, c, ee], lrk[0:L, e, cc], start=True, stop=False)
                        if c:
                            nc.tensor.matmul(bank[rows[e], 4 + e, cc], H[rows[e], :], AR[rows[e], c, 1, :], start=False, stop=False)
                        last = nc.tensor.matmul(bank[rows[e], 4 + e, cc], Us[0:L, ee], lrb[0:L, e, cc], start=False, stop=True)
                last.then_inc(y_raw, 1)

            def two_pairs(i):
                for par in range(2):
                    recur(i * 2 + par, par)
            repeat(pe, KW // 2, two_pairs)
            phase_end(pe, 16)

            for j in range(KW):
                nc.tensor.matmul(bank[:, j, 0:NT], const("heads"), zr[:, j, :], start=True, stop=True).then_inc(mean_raw, 1)
            for j in range(KW):
                pe.wait_ge(y_squared, j + 1)
                nc.tensor.matmul(bank[:, j, 0:NT], const("heads"), kk[:, j, :], start=True, stop=True).then_inc(var_raw, 1)
            pe.wait_ge(gate_landed, 16)
            gup = ring[:, 3, 0:2 * W].rearrange("p (k n) -> p k n", k=2)
            for j in range(KW):
                pe.wait_ge(var_read, j + 1)
                products(bank[:, j, 0:NT], [(gup[:, k, j * P:(j + 1) * P], gd[:, k, :]) for k in range(2)]).then_inc(gate_tiles, 1)
            phase_end(pe, 17)

            def mix(i):
                for u in range(8):
                    pe.wait_ge(x_lo, x_number("mix2", u, i) + 1)
                    w = parts(u, 2, W)
                    for k in range(2):
                        is_split(pe, "mix2", u, k, i)
                        for m in range(KW):
                            if not first(i) and u == 0 and k == 0:
                                pe.wait_ge(evac["mix2"], i * KW + (m + 1 - KW))
                            last = threefold(bank[:, m, 0:NT], [x[:, k, m * P:(m + 1) * P] for x in w],
                                             [x[:, u % 2, k * NT:(k + 1) * NT] for x in (xhi, xlo)], u == 0 and k == 0,
                                             u == 7 and k == 1)
                        last.then_inc(used, 1)
            repeat(pe, 2, mix)
            phase_end(pe, 18, meet=False)
            norm_pe(pe, NT, free=(evac["mix2"], KW + 1))
            phase_end(pe, 19, meet=False)
            norm_pe(pe, NT)
            phase_end(pe, 20, meet=False)
            handed_on[0] += 1
            linear("up2", lambda s: ([h[:, :, META - HALO:NT] for h in hboth], T + HALO) if s % 2 == 0 else
                   ([h[:, :, META:NT] for h in hboth], T))
            phase_end(pe, 21)
            by_rows("down2")
            phase_end(pe, 22, meet=False)
            norm_pe(pe, T, free=(tile_done, TOLD["down2"] + 2))
            phase_end(pe, 23)

        @block.scalar
        def _(act):
            step = Steps(act, act_step)
            act.wait_ge(params_in, 16)
            nc.scalar.activation(cact[:], param("c"), ACT.Silu).then_inc(cact_ready, 1)
            act.wait_ge(ones_set, 1)
            act.wait_ge(x_loaded, 16)
            norm_act(act, x1, T, step)
            ahead(round_unit, "ada", 0, True)
            phase_end(act, 1)
            hand_act(T, mod[:, 0, :])
            for n in range(4):
                act.wait_ge(angle_done, n + 1)
                dst = (tabs128[:, n % 2, 0:T], tabs64[:, n % 2, :])[n // 2]
                nc.scalar.activation(dst, turns[:, n, :], ACT.Sin).then_inc(sines, 1)
            phase_end(act, 2)

            def overlapped(body, count, per):
                body(0, tail=False)
                with act.Fori(1, count - 1) as i:
                    step.begin(i - 1, per)
                    body(i)
                    step.end()
                step.begin(count - 2, per)
                body(count - 1, last=True)
                step.end()
                step.leave(count - 1)
                body(count, head=False)

            def attended(i, o_sem, yT):
                act.wait_ge(o_sem, i * 2)
                for e in range(2):
                    if e == 0:
                        nc.scalar.activation(tile(yT, i * 2 - 2), bank[:, 3, 0:T], ACT.Copy)
                    else:
                        nc.scalar.activation(tile(yT, i * 2 - 1), bank[:, 3, T:2 * T], ACT.Copy)

            def sb(i, head=True, tail=True, last=False):
                if head:
                    round_unit("sb", 2, i)
                    round_unit("sb", 3, i)
                if tail:
                    for e in range(2):
                        act.wait_ge(zm_done, i * 2 + (e - 1))
                        step(nc.scalar.activation(s_b[:, e, :], s_a[:, e, :], ACT.Abs))
                        step(nc.scalar.activation(s_c[:, e, :], s_b[:, e, :], ACT.Exp, scale=-1.0))
                        nc.scalar.activation(s_d[:, e, :], s_c[:, e, :], ACT.Ln, bias=ones[:, 0:1]).then_inc(l_done, 1)
                if head:
                    round_unit("sb", 4, i)
                    round_unit("sb", 5, i)
                if tail:
                    for e in range(2):
                        act.wait_ge(d_done, i * 2 + (e - 1))
                        nc.scalar.activation(s_f[:, e, :], s_b[:, e, :], ACT.Exp).then_inc(w_done, 1)
                if head:
                    ahead(round_unit, "sb", i, last)
                if tail:
                    attended(i, o_done, yaT)
            overlapped(sb, 4, 4)
            phase_end(act, 3)

            ahead(round_unit, "ki", 0, True)
            for u in range(2, 8):
                round_unit("qi", u, 0)
            ahead(round_unit, "qi", 0, True)
            for h in range(IDX_HEADS):
                act.wait_ge(dots_done, h + 1)
                if h >= 2:
                    act.wait_ge(relu_used, h - 1)
                nc.scalar.activation(relu[:, (h % 2) * 384:(h % 2 + 1) * 384], bank[:, h % 8, 0:384], ACT.Relu,
                                     scale=IDX_D ** -0.5 * IDX_HEADS ** -0.5).then_inc(relu_done, 1)
            phase_end(act, 4)

            def dsa(i, head=True, tail=True, last=False):
                if head:
                    round_unit("dsa", 2, i)
                    round_unit("dsa", 3, i)
                if tail:
                    for e in range(2):
                        act.wait_ge(max_done, i * 2 + (e - 1))
                        nc.scalar.activation(s_b[:, e, 0:P], s_a[:, e, 0:P], ACT.Exp, bias=small[:, 8 * e:8 * e + 1],
                                             accum_out=small[:, 8 * e + 2:8 * e + 3])
                        nc.scalar.activation(s_b[:, e, P:384], s_a[:, e, P:384], ACT.Exp, bias=small[:, 8 * e + 1:8 * e + 2],
                                             accum_out=small[:, 8 * e + 3:8 * e + 4]).then_inc(exp_done, 1)
                if head:
                    round_unit("dsa", 4, i)
                    round_unit("dsa", 5, i)
                if tail:
                    for e in range(2):
                        act.wait_ge(turned, i * 2 + (e - 1))
                        nc.scalar.activation(s_f[:, e, :], bank[:, 6 + e, 0:384], ACT.Copy).then_inc(turned_read, 1)
                if head:
                    ahead(round_unit, "dsa", i, last)
                if tail:
                    attended(i, o2_done, ybT)
            overlapped(dsa, 4, 0)
            phase_end(act, 5)

            nc.scalar.activation(yhi[:], work[:, 0:KD * T].rearrange("p (k t) -> p k t", k=KD), ACT.Copy).then_inc(y_hi, 1)

            def merge(i, last):
                for u in range(2, 6):
                    round_unit("merge", u, i)
                if not first(i):
                    act.wait_ge(merged, i * 2)
                for s in (2, 3):
                    if s == 3:
                        ahead(round_unit, "merge", i, last)
                    multiplied(act, "merge", 2 * s - 1, i)
                    for t in range(2):
                        nc.scalar.activation(gates[:, 2 * s + t - 4, :], bank[:, 2 * s + t, 0:T], ACT.Sigmoid)\
                            .then_inc(merge_read[s], 1)
            rotated(act, 8, merge)
            phase_end(act, 6)

            def by_rows_act(phase, src):
                _, count, per, _, _ = PLAN[phase]

                def body(i, last):
                    if first(i):
                        for u in range(2):
                            round_x(phase, u, i, src(u, i))
                    for u in range(2, per):
                        round_x(phase, u, i, src(u, i))
                        round_unit(phase, u, i)
                    for u in range(2):
                        if not last:
                            round_x(phase, u, i + 1, src(u, i + 1))
                            round_unit(phase, u, i + 1)
                    if last:
                        ahead(round_unit, phase, i, True)
                rotated(act, count, body)
            by_rows_act("wo", lambda u, i: [tile(mergedT, i * 4 + u)])
            phase_end(act, 7, meet=False)
            norm_act(act, x1, T, step, ready=(tile_done, TOLD["wo"]))
            hand_act(T, mod[:, 3, :])
            phase_end(act, 8)

            def linear_act(phase, read):
                _, count, per, _, _ = PLAN[phase]

                def body(i, last):
                    for s in range(per // 2):
                        if s < per // 2 - 1:
                            round_unit(phase, 2 * s + 2, i)
                            round_unit(phase, 2 * s + 3, i)
                        elif phase != "lora":
                            ahead(round_unit, phase, i, last)
                        read(s, i)
                rotated(act, count, body)

            def up(s, i):
                if s == 0 and not first(i):
                    act.wait_ge(acted, i * 4)
                multiplied(act, "up", 2 * s + 1, i)
                for t in range(2):
                    q = 2 * s + t
                    f = 4 * i + (2 * (s // 2) + t + (KF if s % 2 else 0))
                    nc.scalar.activation(cv[:, q, 0:T], bank[:, q, 0:T], ACT.Identity, scale=pcol("conv_w", 4 * KF + f),
                                         bias=pcol("conv_b", f)).then_inc(tap_done, 1)
                if s % 2:
                    for t in range(2):
                        act.wait_ge(evac["up"], i * 8 + (2 * s - 2 + t + 1))
                        nc.scalar.activation(sa[:, s - 1 + t, :], cv[:, 2 * s - 2 + t, 0:T], ACT.Silu).then_inc(silu_done, 1)
            linear_act("up", up)
            phase_end(act, 9)
            by_rows_act("down", lambda u, i: [tile(actT, i * 4 + u)])
            phase_end(act, 10, meet=False)
            norm_act(act, x1, T, step, ready=(tile_done, TOLD["down"]))
            phase_end(act, 11, meet=False)

            act.dma_start(res[:, :, 0:META], A["metaT"]).then_inc(meta_loaded, 16)
            act.wait_ge(meta_loaded, 16)
            norm_act(act, res, NT, step, ready=(tile_done, TOLD["g_final"]))
            hand_act(NT)
            phase_end(act, 12)

            def conv2(s, i):
                if s < 2:
                    if s == 0 and not first(i):
                        act.wait_ge(evac["conv2"], i * 2)
                    multiplied(act, "conv2", 2 * s + 1, i)
                    for t in range(2):
                        nc.scalar.activation((bs, cs)[s][:, t, :], bank[:, 2 * s + t, 0:NT], ACT.Copy)\
                            .then_inc((b_copied, c_copied)[s], 1)
            linear_act("conv2", conv2)
            phase_end(act, 13)

            def rkv(s, i):
                multiplied(act, "rkv", 2 * s + 1, i)
                for t in range(2):
                    q = 2 * s + t
                    f = i * 8 + q
                    m = omu[:, f:f + 1] if isinstance(f, int) else omu[:, bass.ds(f, 1)]
                    nc.scalar.activation(tile(zr, f), bank[:, q, 0:NT], ACT.Copy, scale=m).then_inc(own_done, 1)
            linear_act("rkv", rkv)
            phase_end(act, 14)
            lora_parts = [(gd[:, 0, :], bank[:, 0, 0:NT], omu[:, 24:25]), (gd[:, 1, :], bank[:, 1, 0:NT], omu[:, 25:26]),
                          (wdad[0:LORA, 0, :], bank[0:LORA, 2, 0:NT], omu[0:LORA, 26:27]),
                          (wdad[0:LORA, 1, :], bank[0:LORA, 3, 0:NT], omu[0:LORA, 27:28])]

            def lora(s, i):
                multiplied(act, "lora", 2 * s + 1, i)
                for dst, src, m in lora_parts[2 * s:2 * s + 2]:
                    nc.scalar.activation(dst, src, ACT.Copy, scale=m).then_inc(own_done, 1)
            linear_act("lora", lora)
            act.wait_ge(evac["lora"], 4)
            nc.scalar.activation(wdad[0:LORA, 0, :], wdad[0:LORA, 0, :], ACT.Tanh).then_inc(lora_ready, 2)
            for t in range(2):
                nc.scalar.activation(gd[:, t, :], gd[:, t, :], ACT.Sigmoid)
            for u, (dst, shift) in enumerate(((lw, "w0"), (aa, "a0"))):
                for j in range(KW):
                    act.wait_ge(loraup_tiles, u * KW + j + 1)
                    nc.scalar.activation(dst[:, j, :], bank[:, j, 0:NT], ACT.Sigmoid, bias=param(shift, j)).then_inc(loraup_evac, 1)
            act.wait_ge(kk_floored, 1)
            nc.scalar.activation(all8(temp8b), all8(temp8b), ACT.Sqrt).then_inc(kk_rooted, 1)
            phase_end(act, 15)

            def decays(i, par):
                cum, cumc, cpm, Ep, Em, Epm, k2, bb, kt, bt, rkr, vt, AR, ecm, mids = pair_tiles(par)
                act.wait_ge(cum_done, i + 1)
                nc.scalar.activation(Ep, cumc, ACT.Exp)
                nc.scalar.activation(Em, cumc, ACT.Exp, scale=-1.0)
                nc.scalar.activation(Epm, cpm, ACT.Exp)
                nc.scalar.activation(ecm, mids, ACT.Exp)
                nc.scalar.activation(vt, tile(zr, i + 2 * KW), ACT.Copy).then_inc(exps_done, 1)

            def recur(i, par, last):
                nl = len(LEVELS)
                for e in range(2):
                    act.wait_ge(t0_raw, i * 2 + (e + 1))
                    nc.scalar.activation(TT[0:L, e, :], bank[0:L, 2 + e, 0:NT], ACT.Copy).then_inc(t0_ready, 1)
                for l in range(nl):
                    for e in range(2):
                        n = 2 * l + e
                        act.wait_ge(w1_raw, i * 2 * nl + (n + 1))
                        nc.scalar.activation(W1[0:L, e, :], bank[0:L, e, 0:NT], ACT.Copy).then_inc(w1_ready, 1)
                        if n < 3:
                            act.wait_ge(task_done, i * 10 + (n + 1))
                            dst = (tokK, tokB, tokV)[n]
                            nc.scalar.activation(dst[0:L, :, :].rearrange("p a t -> p (a t)"), bank[0:L, 6 + n % 2, :], ACT.Copy)\
                                .then_inc(tok_read, 1)
                    if l == 2 and not last:
                        decays(i + 1, 1 - par)
                for c in range(NC):
                    act.wait_ge(x_raw, i * NC + (c + 1))
                    nc.scalar.activation(Xs[0:L, :].rearrange("p (a v) -> p a v", a=2), bank[0:L, 0:2, 0:RN], ACT.Copy).then_inc(x_ready, 1)
                act.wait_ge(y_raw, i + 1)
                y = tile(zr, i)
                nc.scalar.activation(y[0:RN, :], bank[0:RN, 4, 0:NT], ACT.Copy)
                nc.scalar.activation(y[RN:P, :], bank[RN:P, 5, 0:NT], ACT.Copy).then_inc(pair_done, 1)

            def two_pairs(i, last):
                for par in range(2):
                    recur(i * 2 + par, par, last and par == 1)
            decays(0, 0)
            rotated(act, KW // 2, two_pairs)
            phase_end(act, 16)
            ahead(round_unit, "lora", 0, True)

            for j in range(KW):
                act.wait_ge(centred, j + 1)
                nc.scalar.activation(kk[:, j, :], zr[:, j, :], ACT.Square).then_inc(y_squared, 1)
            for j in range(KW):
                act.wait_ge(var_raw, j + 1)
                nc.scalar.activation(lw[:, j, :], bank[:, j, 0:NT], ACT.Sqrt, scale=1.0 / RN, bias=epsc[:, 1:2]).then_inc(var_read, 1)
            phase_end(act, 17)

            def mix(i, last):
                def src(u):
                    return [yconv[:, k, :] if k < KW else zr[:, k - KW, :] for k in (2 * u, 2 * u + 1)]
                if first(i):
                    for u in range(2):
                        round_x("mix2", u, i, src(u))
                for u in range(2, 8):
                    round_x("mix2", u, i, src(u))
                    round_unit("mix2", u, i)
                if last:
                    ahead(round_unit, "mix2", i, last)
                else:
                    for u in range(2):
                        round_x("mix2", u, i + 1, src(u))
                        round_unit("mix2", u, i + 1)
            rotated(act, 2, mix)
            phase_end(act, 18, meet=False)
            norm_act(act, fT, NT, step, ready=(evac["mix2"], 0))
            phase_end(act, 19, meet=False)
            norm_act(act, res, NT, step, ready=(tile_done, TOLD["mixed"]))
            hand_act(NT)
            phase_end(act, 20)

            def up2(s, i):
                if s == 0 and not first(i):
                    act.wait_ge(evac["up2"], i * 8)
                if s % 2 == 0:
                    multiplied(act, "up2", 2 * s + 1, i)
                    for t in range(2):
                        nc.scalar.activation(cv[:, 2 * s + t, 0:T], bank[:, 2 * s + t, HALO:T + HALO], ACT.Copy,
                                             scale=pcol("conv_ffn", 4 * i + (s + t + 2 * KF))).then_inc(tap2_done, 1)
                else:
                    for t in range(2):
                        act.wait_ge(evac["up2"], i * 8 + (2 * s - 2 + t + 1))
                        nc.scalar.activation(sa[:, s - 1 + t, :], cv[:, 2 * s - 2 + t, 0:T], ACT.Silu).then_inc(silu2_done, 1)
            linear_act("up2", up2)
            phase_end(act, 21)
            by_rows_act("down2", lambda u, i: [tile(actT, i * 4 + u)])
            phase_end(act, 22, meet=False)
            norm_act(act, fT[:, :, 0:T], T, step, ready=(tile_done, TOLD["down2"]))
            phase_end(act, 23)

        @block.vector
        def _(dve):
            step = Steps(dve, dve_step)
            nc.vector.memset(epsc[:, 0:1], EPS)
            nc.vector.memset(epsc[:, 1:2], GN_EPS)
            nc.vector.memset(ones[:], 1.0).then_inc(ones_set, 1)
            dve.wait_ge(params_in, 16)
            dve.wait_ge(pos_in, 16)
            dve.wait_ge(consts_in, 16)
            dve.wait_ge(x_loaded, 16)
            step(nc.vector.tensor_copy(posf, posi))
            C1, C2 = 6.28125, 0.0019350051879882812
            C3 = 2 * math.pi - C1 - C2
            ROUND = 1.5 * 2.0 ** 23
            EDGE = 3.1415925
            for n in range(4):
                f = n // 2
                cosine = n % 2 == 1
                if n:
                    dve.wait_ge(angle_done, n)
                step(nc.vector.tensor_scalar(angles[:, 0, :], posf, const("invf")[:, f:f + 1], None, ALU.mult))
                step(nc.vector.tensor_scalar(angles[:, 1, :], angles[:, 0, :], 1 / (2 * math.pi), 0.25 if cosine else 0.0,
                                             ALU.mult, ALU.add))
                step(nc.vector.tensor_scalar(angles[:, 1, :], angles[:, 1, :], ROUND, -ROUND, ALU.add, ALU.add))
                for c in (C1, C2, C3):
                    step(nc.vector.scalar_tensor_tensor(angles[:, 0, :], angles[:, 1, :], -c, angles[:, 0, :], ALU.mult, ALU.add))
                step(nc.vector.tensor_scalar(angles[:, 0, :], angles[:, 0, :], math.pi / 2 if cosine else 0.0, EDGE,
                                             ALU.add, ALU.min))
                nc.vector.tensor_scalar(turns[:, n, :], angles[:, 0, :], -EDGE, None, ALU.max).then_inc(angle_done, 1)
            dve.wait_ge(cact_ready, 1)
            for b in range(2):
                for k in range(KD):
                    u = b * KD + k
                    arrived(dve, "ada", u, 0)
                    if k == 0:
                        ins = nc.vector.tensor_scalar(acc[:, b, :], ring[:, u % NSLOT, :], cact[:, k:k + 1], None, ALU.mult)
                    else:
                        dve.wait_ge(ada_used, u)
                        ins = nc.vector.scalar_tensor_tensor(acc[:, b, :], ring[:, u % NSLOT, :], cact[:, k:k + 1],
                                                             acc[:, b, :], ALU.mult, ALU.add)
                    ins.then_inc(ada_used, 1)
            ahead(rest_unit, "ada", 0, True)
            dve.wait_ge(ada_summed, 2)
            flat = mod[:].rearrange("p a k -> p (a k)")
            step(nc.vector.tensor_tensor(flat[:, 0:2 * KD], bank[:, 1, 0:2 * KD], param("b_ada", 0, 2 * KD), ALU.add))
            step(nc.vector.scalar_tensor_tensor(gain[:, 0, :], mod[:, 1, :], 1.0, param("g_mix"), ALU.add, ALU.mult))
            phase_end(dve, 1)

            norm_dve_handing(dve, x1, gain[:, 0, :], T, step, mod[:, 0, :])
            dve.wait_ge(sines, 4)
            step(nc.vector.tensor_scalar(tabs128[:, 0, 0:T], tabs128[:, 0, 0:T], const("sign")[:, 0:1], None, ALU.mult))
            nc.vector.tensor_scalar(tabs64[:, 0, :], tabs64[:, 0, :], const("sign")[:, 1:2], None, ALU.mult)
            for n in range(2):
                nc.vector.tensor_copy(tabs128[:, n, T:2 * T], tabs128[:, n, 0:T])
            phase_end(dve, 2)

            def late(b, j0, j1):
                for j in range(j0, j1):
                    n = j % NSLOT
                    dve.wait_ge(late_landed[n], b * (16 * KD // NSLOT) + 16 * (j // NSLOT + 1))
                    src = late_ring[:, n, :]
                    if j == 0:
                        if not first(b):
                            dve.wait_ge(late_summed, b)
                        ins = nc.vector.tensor_scalar(late_acc, src, cact[:, j:j + 1], None, ALU.mult)
                    else:
                        dve.wait_ge(late_used, b * KD + j)
                        ins = nc.vector.scalar_tensor_tensor(late_acc, src, cact[:, j:j + 1], late_acc, ALU.mult, ALU.add)
                    ins.then_inc(late_used, 1)

            def overlapped(body, count, per):
                body(0, tail=False)
                with dve.Fori(1, count - 1) as i:
                    step.begin(i - 1, per)
                    body(i)
                    step.end()
                step.begin(count - 2, per)
                body(count - 1, last=True)
                step.end()
                step.leave(count - 1)
                body(count, head=False)

            def sb(i, head=True, tail=True, last=False):
                if head:
                    rest_unit("sb", 2, i)
                    rest_unit("sb", 3, i)
                if tail:
                    for e in range(2):
                        dve.wait_ge(z_done, i * 2 + (e - 1))
                        nc.vector.scalar_tensor_tensor(s_a[:, e, :], bank[:, 4 + e, 0:384], SCALE, past, ALU.mult, ALU.add)\
                            .then_inc(zm_done, 1)
                if head:
                    multiplied(dve, "sb", 1, i)
                    nc.vector.tensor_copy(qT[:].rearrange("p a t -> p (a t)"), bank[:, 0, :]).then_inc(q_read, 1)
                    late(i, 0, 3)
                    rest_unit("sb", 4, i)
                if tail:
                    for e in range(2):
                        dve.wait_ge(l_done, i * 2 + (e - 1))
                        dve.wait_ge(zm_done, i * 2 + (e - 1))
                        nc.vector.scalar_tensor_tensor(s_e[:, e, :], s_a[:, e, :], 0.0, s_d[:, e, :], ALU.max, ALU.add)\
                            .then_inc(sp_done, 1)
                if head:
                    late(i, 3, 6)
                    rest_unit("sb", 5, i)
                    multiplied(dve, "sb", 3, i)
                    nc.vector.tensor_copy(kT[:].rearrange("p a t -> p (a t)"), bank[:, 1, :]).then_inc(k_read, 1)
                if tail:
                    for e in range(2):
                        dve.wait_ge(s_done, i * 2 + (e - 1))
                        nc.vector.tensor_tensor(s_b[:, e, :], s_a[:, e, :], bank[:, 6 + e, 0:384], ALU.subtract)\
                            .then_inc(d_done, 1)
                    dve.wait_ge(d_done, i * 2)
                if head:
                    late(i, 6, KD if last else 11)
                    ahead(rest_unit, "sb", i, last)
                    multiplied(dve, "sb", 5, i)
                    if tail:
                        dve.wait_ge(o_done, i * 2)
                    nc.vector.tensor_copy(vS[:].rearrange("p a t -> p (a t)"), bank[:, 2, :]).then_inc(v_read, 1)
                    if not last:
                        late(i, 11, KD)
            overlapped(sb, 4, 0)
            phase_end(dve, 3)

            def rope(dst, src, n, tabs, half, done, count):
                sin, cos = tabs[:, 0, 0:n], tabs[:, 1, 0:n]
                a, b = ropeA[:, 0:n], ropeB[:, 0:n]
                for lo in range(0, P, 2 * half):
                    mid, hi = lo + half, lo + 2 * half
                    nc.vector.tensor_tensor(a[lo:mid, :], src[mid:hi, :], sin[mid:hi, :], ALU.mult)
                    last = nc.vector.tensor_tensor(a[mid:hi, :], src[lo:mid, :], sin[lo:mid, :], ALU.mult)
                step.mark(last)
                step(nc.vector.tensor_tensor(b, src, cos, ALU.mult))
                nc.vector.tensor_tensor(dst, a, b, ALU.add).then_inc(done, 1)
                dve.wait_ge(done, count)

            ahead(rest_unit, "ki", 0, True)
            multiplied(dve, "ki", 1, 0)
            rope(kiT, bank[:, 6, 0:T], T, tabs64, 32, evac["ki"], 1)
            nc.vector.tensor_copy(small[:, 0:2 * IDX_HEADS], bank[:, 7, 0:2 * IDX_HEADS]).then_inc(evac["ki"], 1)
            for q in range(8):
                if q % 2 == 0 and q < 6:
                    rest_unit("qi", q + 2, 0)
                    rest_unit("qi", q + 3, 0)
                elif q == 6:
                    ahead(rest_unit, "qi", 0, True)
                multiplied(dve, "qi", q // 2 * 2 + 1, 0)
                rope(qiT[:, q, :], bank[:, q, 0:T], T, tabs64, 32, evac["qi"], q + 1)
            score, spare = s_a[:, 0, :], s_a[:, 1, :]
            dve.wait_ge(evac["ki"], 2)
            step(nc.vector.memset(score, 0.0))
            for h in range(IDX_HEADS):
                dve.wait_ge(relu_done, h + 1)
                r = relu[:, (h % 2) * 384:(h % 2 + 1) * 384]
                step.mark(nc.vector.scalar_tensor_tensor(score[:, 0:P], r[:, 0:P], small[:, h:h + 1], score[:, 0:P],
                                                         ALU.mult, ALU.add))
                nc.vector.scalar_tensor_tensor(score[:, P:384], r[:, P:384], small[:, IDX_HEADS + h:IDX_HEADS + h + 1],
                                               score[:, P:384], ALU.mult, ALU.add).then_inc(relu_used, 1)
                dve.wait_ge(relu_used, h + 1)
            step(nc.vector.scalar_tensor_tensor(score, seen, UNSEEN / NEG, score, ALU.mult, ALU.add))
            src, dst = score, spare
            for r in range(TOPK // 8):
                for lo, hi, m in ((0, P, 40), (P, 384, 48)):
                    step.mark(nc.vector.max(small[:, m:m + 8], src[:, lo:hi]))
                step.wait()
                for lo, hi, m in ((0, P, 40), (P, 384, 48)):
                    step.mark(nc.vector.match_replace(dst[:, lo:hi], small[:, m:m + 8], src[:, lo:hi], TAKEN))
                step.wait()
                src, dst = dst, src
            taken = biasM[:, 0, :]
            step(nc.vector.tensor_scalar(taken, src, TAKEN, None, ALU.is_equal))
            step(nc.vector.tensor_scalar(taken, taken, -NEG, NEG, ALU.mult, ALU.add))
            step(nc.vector.tensor_tensor(taken, taken, seen, ALU.add))
            phase_end(dve, 4)

            def dsa(i, head=True, tail=True, last=False):
                if head:
                    rest_unit("dsa", 2, i)
                    rest_unit("dsa", 3, i)
                if tail:
                    for e in range(2):
                        dve.wait_ge(logits_done, i * 2 + (e - 1))
                        step(nc.vector.scalar_tensor_tensor(s_a[:, e, :], bank[:, 4 + e, 0:384], SCALE, taken, ALU.mult, ALU.add))
                        nc.vector.tensor_reduce(small[:, 8 * e:8 * e + 1], s_a[:, e, 0:P], AX, ALU.max, negate=True)
                        nc.vector.tensor_reduce(small[:, 8 * e + 1:8 * e + 2], s_a[:, e, P:384], AX, ALU.max, negate=True)\
                            .then_inc(max_done, 1)
                if head:
                    multiplied(dve, "dsa", 1, i)
                    rope(qT[:].rearrange("p a t -> p (a t)"), bank[:, 0, :], 2 * T, tabs128, 64, q2_read, i + 1)
                    rest_unit("dsa", 4, i)
                if tail:
                    for e in range(2):
                        dve.wait_ge(exp_done, i * 2 + (e - 1))
                        step(nc.vector.reciprocal(small[:, 8 * e + 4:8 * e + 6], small[:, 8 * e + 2:8 * e + 4]))
                        step.mark(nc.vector.tensor_scalar(s_c[:, e, 0:P], s_b[:, e, 0:P], small[:, 8 * e + 4:8 * e + 5], None, ALU.mult))
                        nc.vector.tensor_scalar(s_c[:, e, P:384], s_b[:, e, P:384], small[:, 8 * e + 5:8 * e + 6], None, ALU.mult)\
                            .then_inc(probs_done, 1)
                if head:
                    late(i + 4, 0, 6)
                    rest_unit("dsa", 5, i)
                    multiplied(dve, "dsa", 3, i)
                    rope(kT[:].rearrange("p a t -> p (a t)"), bank[:, 1, :], 2 * T, tabs128, 64, k2_read, i + 1)
                    late(i + 4, 6, KD if last else 11)
                    ahead(rest_unit, "dsa", i, last)
                    multiplied(dve, "dsa", 5, i)
                    if tail:
                        dve.wait_ge(o2_done, i * 2)
                    nc.vector.tensor_copy(vS[:].rearrange("p a t -> p (a t)"), bank[:, 2, :]).then_inc(v2_read, 1)
                    if not last:
                        late(i + 4, 11, KD)
            overlapped(dsa, 4, 10)
            phase_end(dve, 5)

            dve.wait_ge(y_hi, 1)
            nc.vector.tensor_tensor(ylo[:], work[:, 0:KD * T].rearrange("p (k t) -> p k t", k=KD), yhi[:].bitcast(F32),
                                    ALU.subtract).then_inc(y_lo, 1)

            def merge(i, last):
                for u in range(2, 6):
                    rest_unit("merge", u, i)
                    late(i + 8, 4 * (u - 2), 4 * (u - 1))
                for s in range(2):
                    if s == 1:
                        ahead(rest_unit, "merge", i, last)
                    for t in range(2):
                        dve.wait_ge(merge_read[2 + s], i * 2 + (t + 1))
                        nc.vector.tensor_tensor(gates[:, 2 * s + t, :], gates[:, 2 * s + t, :],
                                                bank[:, 2 * s + t, 0:T], ALU.mult).then_inc(merge_read[s], 1)
                for t in range(2):
                    dve.wait_ge(merge_read[1], i * 2 + (t + 1))
                    nc.vector.tensor_tensor(tile(mergedT, i * 2 + t), gates[:, t, :], gates[:, 2 + t, :],
                                            ALU.add).then_inc(merged, 1)
            rotated(dve, 8, merge)
            dve.wait_ge(late_summed, NLATE)
            step(nc.vector.tensor_tensor(flat[:, 2 * KD:6 * KD], bank[:, 7, LATE_AT:LATE_AT + 4 * KD],
                                         param("b_ada", 2 * KD, 6 * KD), ALU.add))
            nc.vector.scalar_tensor_tensor(gain[:, 1, :], mod[:, 4, :], 1.0, param("g_ffn"), ALU.add, ALU.mult)
            nc.vector.tensor_scalar(mod[:, 2, :], mod[:, 2, :], 1.0, None, ALU.add)
            step(nc.vector.tensor_scalar(mod[:, 5, :], mod[:, 5, :], 1.0, None, ALU.add))
            phase_end(dve, 6)

            def by_rows_dve(phase, src):
                _, count, per, _, _ = PLAN[phase]

                def body(i, last):
                    if first(i):
                        for u in range(2):
                            rest_x(phase, u, i, src(u, i))
                    for u in range(2, per):
                        rest_x(phase, u, i, src(u, i))
                        rest_unit(phase, u, i)
                    for u in range(2):
                        if not last:
                            rest_x(phase, u, i + 1, src(u, i + 1))
                            rest_unit(phase, u, i + 1)
                    if last:
                        ahead(rest_unit, phase, i, True)
                rotated(dve, count, body)

            def add_gated(phase, gate):
                multiplied(dve, phase, PLAN[phase][2] - 1, PLAN[phase][1] - 1)
                for f in range(KD):
                    nc.vector.scalar_tensor_tensor(x1[:, f, :], bank[:, f // 2, (f % 2) * T:(f % 2 + 1) * T], gate[:, f:f + 1],
                                                   x1[:, f, :], ALU.mult, ALU.add).then_inc(tile_done, 1)
            by_rows_dve("wo", lambda u, i: [tile(mergedT, i * 4 + u)])
            add_gated("wo", mod[:, 2, :])
            phase_end(dve, 7)
            norm_dve_handing(dve, x1, gain[:, 1, :], T, step, mod[:, 3, :])
            phase_end(dve, 8)

            def linear_dve(phase, read, per_steps=None):
                _, count, per, _, _ = PLAN[phase]

                def body(i, last):
                    step.begin(i)
                    for s in range(per // 2):
                        if s < per // 2 - 1:
                            rest_unit(phase, 2 * s + 2, i)
                            rest_unit(phase, 2 * s + 3, i)
                        elif phase != "lora":
                            ahead(rest_unit, phase, i, last)
                        read(s, i)
                    step.end()
                rotated(dve, count, body)
                step.leave(count)

            def up(s, i):
                for t in range(2):
                    q = 2 * s + t
                    f = 4 * i + (2 * (s // 2) + t + (KF if s % 2 else 0))
                    dve.wait_ge(tap_done, i * 8 + (q + 1))
                    c, b = cv[:, q, 0:T], bank[:, q, 0:T]
                    step(nc.vector.scalar_tensor_tensor(c[:, 1:T], b[:, 0:T - 1], pcol("conv_w", 2 * KF + f), c[:, 1:T],
                                                        ALU.mult, ALU.add))
                    nc.vector.scalar_tensor_tensor(c[:, 2:T], b[:, 0:T - 2], pcol("conv_w", f), c[:, 2:T],
                                                   ALU.mult, ALU.add).then_inc(evac["up"], 1)
                if s % 2:
                    for t in range(2):
                        dve.wait_ge(silu_done, i * 4 + (s - 1 + t + 1))
                        dve.wait_ge(evac["up"], i * 8 + (2 * s + t + 1))
                        nc.vector.tensor_tensor(tile(actT, i * 4 + (s - 1 + t)), sa[:, s - 1 + t, :],
                                                cv[:, 2 * s + t, 0:T], ALU.mult).then_inc(acted, 1)
            linear_dve("up", up)
            phase_end(dve, 9)
            by_rows_dve("down", lambda u, i: [tile(actT, i * 4 + u)])
            add_gated("down", mod[:, 5, :])
            phase_end(dve, 10)
            norm_dve(dve, T, step, scaled(x1, x1, param("g_final"), T))
            phase_end(dve, 11)

            norm_dve_handing(dve, res, param("g_pre_mix"), NT, step)
            lo = pw["mu_rkv"][0]
            nc.vector.tensor_scalar(omu[:], params[:, lo:lo + 28], -1.0, 1.0, ALU.mult, ALU.add)
            nc.vector.tensor_scalar(omka[:], param("k_a"), -1.0, 1.0, ALU.mult, ALU.add)
            nc.vector.memset(chs[:, :, 0:HALO], 0.0)
            phase_end(dve, 12)

            def conv2(s, i):
                if s < 2:
                    return
                multiplied(dve, "conv2", 5, i)
                for t in range(2):
                    f = i * 2 + t
                    dve.wait_ge(c_copied, i * 2 + (t + 1))
                    nc.vector.tensor_tensor(chs[:, t, HALO:HALO + NT], cs[:, t, :], bank[:, 4 + t, 0:NT], ALU.mult)\
                        .then_inc(x_read, 1)
                    dve.wait_ge(x_read, i * 2 + (t + 1))
                    step(nc.vector.tensor_scalar(ycs[:, t, :], chs[:, t, 0:NT], pcol("conv_w2", f), None, ALU.mult))
                    for tap in (1, 2):
                        step(nc.vector.scalar_tensor_tensor(ycs[:, t, :], chs[:, t, tap:tap + NT], pcol("conv_w2", f + tap * KW),
                                                            ycs[:, t, :], ALU.mult, ALU.add))
                    nc.vector.tensor_tensor(tile(yconv, f), ycs[:, t, :], bs[:, t, :], ALU.mult).then_inc(evac["conv2"], 1)
            linear_dve("conv2", conv2)
            phase_end(dve, 13)

            def shift(dst, src, mu, f, done):
                dve.wait_ge(own_done, f + 1)
                nc.vector.scalar_tensor_tensor(dst[:, 1:NT], src[:, 0:NT - 1], mu, dst[:, 1:NT], ALU.mult, ALU.add).then_inc(done, 1)

            def rkv(s, i):
                for q in (2 * s, 2 * s + 1):
                    f = i * 8 + q
                    shift(tile(zr, f), bank[:, q, 0:NT], pcol("mu_rkv", f), f, evac["rkv"])
            linear_dve("rkv", rkv)
            phase_end(dve, 14)

            def lora(s, i):
                for t in range(2):
                    if s == 0:
                        shift(gd[:, t, :], bank[:, t, 0:NT], param("mu_gd", t), 24 + t, evac["lora"])
                    else:
                        shift(wdad[0:LORA, t, :], bank[0:LORA, 2 + t, 0:NT], param(("mu_wd", "mu_ad")[t], 0)[0:LORA, :],
                              26 + t, evac["lora"])
            linear_dve("lora", lora)
            for j in range(KW):
                last = nc.vector.tensor_scalar(kk[:, j, :], zr[:, KW + j, :], param("k_k", j), None, ALU.mult)
            step(last)
            nc.vector.tensor_tensor(all8(temp8), all8(kk), all8(kk), ALU.mult).then_inc(kk_squared, 1)
            dve.wait_ge(loraup_evac, KW)
            nc.vector.tensor_scalar(all8(lw), all8(lw), -DECAY_SCALE, None, ALU.mult)
            for j in range(KW):
                dve.wait_ge(kk_summed, j + 1)
                last = nc.vector.tensor_scalar(temp8b[:, j, :], bank[:, j, 0:NT], 1e-24, None, ALU.max)
            last.then_inc(kk_floored, 1)
            dve.wait_ge(kk_rooted, 1)
            step(nc.vector.reciprocal(all8(temp8b), all8(temp8b)))
            nc.vector.tensor_tensor(all8(kk), all8(kk), all8(temp8b), ALU.mult)
            phase_end(dve, 15)

            def by_chunk(x):
                return x.rearrange("p (c t) -> p c t", c=NC)

            def mask(name):
                return const(name)[0:L, :].unsqueeze(1).to_broadcast([L, NC, L])

            def prepare(i, par, part):
                cum, cumc, cpm, Ep, Em, Epm, k2, bb, kt, bt, rkr, vt, AR, ecm, mids = pair_tiles(par)
                lwi, ki = tile(lw, i), tile(zr, i + KW)
                if part == 0:
                    for c in range(NC):
                        last = nc.vector.tensor_tensor_scan(cum[:, c * L:(c + 1) * L], onesrow, lwi[:, c * L:(c + 1) * L], 0.0,
                                                            ALU.mult, ALU.add)
                    step(last)
                if part == 1:
                    for c in range(NC):
                        m = cum[:, c * L + MID:c * L + MID + 1]
                        step.mark(nc.vector.tensor_scalar(cumc[:, c * L:(c + 1) * L], cum[:, c * L:(c + 1) * L], m, None, ALU.subtract))
                    step(nc.vector.tensor_copy(mids, by_chunk(cum)[:, :, MID]))
                    nc.vector.tensor_tensor(cpm, cumc, lwi, ALU.subtract).then_inc(cum_done, 1)
                if part == 2:
                    step(nc.vector.tensor_scalar(k2, tile(aa, i), pcol("k_a", i), omka[:, i:i + 1] if isinstance(i, int)
                                                 else omka[:, bass.ds(i, 1)], ALU.mult, ALU.add))
                    step(nc.vector.tensor_tensor(k2, k2, ki, ALU.mult))
                    step(nc.vector.tensor_tensor(bb, tile(kk, i), tile(aa, i), ALU.mult))
                    step.mark(nc.vector.scalar_tensor_tensor(rkr, tile(zr, i), pcol("r_k", i), k2, ALU.mult, ALU.mult))
                if part == 3:
                    dve.wait_ge(exps_done, i + 1)
                    nc.vector.scalar_tensor_tensor(AR[:, :, 0, :], by_chunk(Epm), -1.0, by_chunk(tile(kk, i)), ALU.mult, ALU.mult)
                    nc.vector.tensor_tensor(AR[:, :, 1, :], by_chunk(Ep), by_chunk(tile(zr, i)), ALU.mult)
                    nc.vector.tensor_tensor(kt, k2, Em, ALU.mult)
                    nc.vector.tensor_tensor(bt, bb, Em, ALU.mult).then_inc(feat_done, 1)

            def recur(i, par, last_pair):
                cum, cumc, cpm, Ep, Em, Epm, k2, bb, kt, bt, rkr, vt, AR, ecm, mids = pair_tiles(par)
                nl = len(LEVELS)
                ki = tile(zr, i + KW)
                if not first(i):
                    dve.wait_ge(pair_done, i)
                for e in range(2):
                    dve.wait_ge(n_raw, i * 2 + (e + 1))
                    step(nc.vector.scalar_tensor_tensor(by_chunk(N[0:L, e, :]), by_chunk(bank[0:L, e, 0:NT]), BIG, mask("strict"),
                                                        ALU.min, ALU.mult))
                    step(nc.vector.tensor_tensor(by_chunk(G[0:L, e, :]), by_chunk(N[0:L, e, :]), mask("first"), ALU.mult))
                    nc.vector.tensor_tensor(by_chunk(G[0:L, e, :]), by_chunk(G[0:L, e, :]),
                                            const("ident")[0:L, 0:L].unsqueeze(1).to_broadcast([L, NC, L]), ALU.add)\
                        .then_inc(g0_done, 1)
                for l in range(nl):
                    for e in range(2):
                        n = 2 * l + e
                        if 3 <= n < 10:
                            dve.wait_ge(task_done, i * 10 + (n + 1))
                            b = bank[:, 6 + n % 2, 0:NT]
                            if n < 9:
                                kind, h = (n - 3) // 2, (n - 3) % 2
                                dst = (lak, lrk, lrb)[kind]
                                ins = nc.vector.scalar_tensor_tensor(by_chunk(dst[0:L, h, :]), by_chunk(b[0:L, :]), BIG,
                                                                     mask("strict" if kind == 0 else "incl"), ALU.min, ALU.mult)
                            else:
                                ins = nc.vector.tensor_tensor(ki, tile(zr, i + 2 * KW), b, ALU.mult)
                            ins.then_inc(mat_read, 1)
                    for e in range(2):
                        dve.wait_ge(tg_raw, i * 2 * nl + (2 * l + e + 1))
                        if l < nl - 1:
                            nc.vector.tensor_tensor(TT[0:L, e, :], TT[0:L, e, :], bank[0:L, 2 + e, 0:NT], ALU.add)
                        nc.vector.tensor_tensor(G[0:L, e, :], G[0:L, e, :], bank[0:L, 4 + e, 0:NT], ALU.add).then_inc(tg_ready, 1)
                    if not last_pair and l in (0, 1, 3, 4):
                        prepare(i + 1, 1 - par, (0, 1, None, 2, 3)[l])
                for c in range(NC):
                    dve.wait_ge(u_raw, i * NC + (c + 1))
                    nc.vector.tensor_copy(Us[0:L, :], bank[0:L, 2, 0:P]).then_inc(u_ready, 1)
                    if c < NC - 1:
                        dve.wait_ge(h_raw, i * 3 + (c + 1))
                        src = bank[:, 3, 0:RN]
                        if c:
                            step(nc.vector.tensor_tensor(Hsum, bank[:, 3, 0:RN], Hs[:, c % 2, :], ALU.add))
                            src = Hsum
                        nc.vector.tensor_scalar(Hs[:, (c + 1) % 2, :], src, Ep[:, (c + 1) * L - 1:(c + 1) * L],
                                                ecm[:, c + 1:c + 2], ALU.mult, ALU.mult).then_inc(h_ready, 1)
                        dve.wait_ge(h_ready, i * 3 + (c + 1))

            def two_pairs(i, last=False):
                for par in range(2):
                    recur(i * 2 + par, par, last and par == 1)
            for part in range(4):
                prepare(0, 0, part)
            step.begin(0)
            two_pairs(0)
            step.end()
            with dve.Fori(1, KW // 2 - 1) as i:
                step.begin(i)
                two_pairs(i)
                step.end()
            step.leave(KW // 2 - 1)
            two_pairs(KW // 2 - 1, last=True)
            phase_end(dve, 16)
            ahead(rest_unit, "lora", 0, True)

            for j in range(KW):
                dve.wait_ge(mean_raw, j + 1)
                nc.vector.scalar_tensor_tensor(zr[:, j, :], bank[:, j, 0:NT], -1.0 / RN, zr[:, j, :], ALU.mult, ALU.add)\
                    .then_inc(centred, 1)
            dve.wait_ge(centred, KW)
            for at in range(KW + 3):
                step.wait()
                if at < KW:
                    dve.wait_ge(var_read, at + 1)
                    last = nc.vector.reciprocal(lw[:, at, :], lw[:, at, :])
                j = at - 1
                if 0 <= j < KW:
                    last = nc.vector.scalar_tensor_tensor(zr[:, j, :], zr[:, j, :], param("ln_w", j), lw[:, j, :], ALU.mult, ALU.mult)
                j = at - 2
                if 0 <= j < KW:
                    last = nc.vector.scalar_tensor_tensor(zr[:, j, :], zr[:, j, :], param("ln_b", j), zr[:, KW + j, :], ALU.add, ALU.add)
                j = at - 3
                if 0 <= j < KW:
                    dve.wait_ge(gate_tiles, j + 1)
                    last = nc.vector.tensor_tensor(zr[:, j, :], zr[:, j, :], bank[:, j, 0:NT], ALU.mult)
                step.mark(last)
            phase_end(dve, 17)

            def mix(i, last):
                def src(u):
                    return [yconv[:, k, :] if k < KW else zr[:, k - KW, :] for k in (2 * u, 2 * u + 1)]
                if first(i):
                    for u in range(2):
                        rest_x("mix2", u, i, src(u))
                for u in range(2, 8):
                    rest_x("mix2", u, i, src(u))
                    rest_unit("mix2", u, i)
                if last:
                    ahead(rest_unit, "mix2", i, last)
                else:
                    rest_x("mix2", 0, i + 1, src(0))
                    rest_unit("mix2", 0, i + 1)
                multiplied(dve, "mix2", 7, i)
                for m in range(KW):
                    nc.vector.tensor_copy(tile(fT, i * KW + m), bank[:, m, 0:NT]).then_inc(evac["mix2"], 1)
                if not last:
                    rest_x("mix2", 1, i + 1, src(1))
                    rest_unit("mix2", 1, i + 1)
            rotated(dve, 2, mix)
            phase_end(dve, 18)

            def add_normed(g, n, dst):
                def apply(k):
                    step(nc.vector.scalar_tensor_tensor(fT[:, k, 0:n], fT[:, k, 0:n], param(g, k), rms[:, 0:n], ALU.mult, ALU.mult))
                    nc.vector.tensor_tensor(dst[:, k, :], dst[:, k, :], fT[:, k, 0:n], ALU.add).then_inc(tile_done, 1)
                return apply
            norm_dve(dve, NT, step, add_normed("g_post_mix", NT, res))
            phase_end(dve, 19)
            norm_dve_handing(dve, res, param("g_pre_ffn"), NT, step)
            phase_end(dve, 20)

            def up2(s, i):
                for t in range(2):
                    if s % 2 == 0:
                        q = 2 * s + t
                        f = 4 * i + (s + t)
                        dve.wait_ge(tap2_done, i * 4 + (s + t + 1))
                        step(nc.vector.scalar_tensor_tensor(cv[:, q, 0:T], bank[:, q, 1:T + 1], pcol("conv_ffn", f + KF),
                                                            cv[:, q, 0:T], ALU.mult, ALU.add))
                        nc.vector.scalar_tensor_tensor(cv[:, q, 0:T], bank[:, q, 0:T], pcol("conv_ffn", f),
                                                       cv[:, q, 0:T], ALU.mult, ALU.add).then_inc(evac["up2"], 1)
                    else:
                        q = 2 * s + t
                        if t == 0:
                            multiplied(dve, "up2", 2 * s + 1, i)
                        dve.wait_ge(silu2_done, i * 4 + (s - 1 + t + 1))
                        nc.vector.tensor_tensor(tile(actT, i * 4 + (s - 1 + t)), sa[:, s - 1 + t, :],
                                                bank[:, q, 0:T], ALU.mult).then_inc(evac["up2"], 1)
            linear_dve("up2", up2)
            phase_end(dve, 21)
            by_rows_dve("down2", lambda u, i: [tile(actT, i * 4 + u)])
            multiplied(dve, "down2", 3, PLAN["down2"][1] - 1)
            for f in range(KD):
                nc.vector.tensor_copy(fT[:, f, 0:T], bank[:, f // 2, (f % 2) * T:(f % 2 + 1) * T]).then_inc(tile_done, 1)
            phase_end(dve, 22)
            norm_dve(dve, T, step, add_normed("g_post_ffn", T, x1))
            phase_end(dve, 23)

        @block.gpsimd
        def _(pool):
            pool.wait_ge(phase_done, 3 * 2)

            def late_loads(b):
                for j in range(KD):
                    if not first(b) or j >= NSLOT:
                        pool.wait_ge(late_used, b * KD + (j + 1 - NSLOT))
                    v = feature_major(A["w_ada"])[:, j:j + 1, :]
                    v = v[:, :, 2 * D:2 * D + LATE] if isinstance(b, int) else v[:, :, bass.ds(b * LATE + 2 * D, LATE)]
                    nc.gpsimd.dma_start(late_ring[:, j % NSLOT:j % NSLOT + 1, :], v).then_inc(late_landed[j % NSLOT], 16)
            repeat(pool, NLATE, late_loads)
            pool.wait_ge(consts_in, 16)

            def recur(i):
                nl = len(LEVELS)
                for l, b in enumerate(LEVELS):
                    for e in range(2):
                        if l == 0:
                            pool.wait_ge(g0_done, i * 2 + (e + 1))
                        if l >= 2:
                            pool.wait_ge(w1_raw, i * 2 * nl + (2 * (l - 2) + e + 1))
                        nc.gpsimd.tensor_tensor(
                            NM[0:L, l % 2, e * NT:(e + 1) * NT].rearrange("p (c t) -> p c t", c=NC),
                            N[0:L, e, :].rearrange("p (c t) -> p c t", c=NC),
                            const(f"level{b}")[0:L, :].unsqueeze(1).to_broadcast([L, NC, L]), ALU.mult).then_inc(nm_ready, 1)
            repeat(pool, KW, recur)


def constant_block():
    where, width = offsets(CONSTS)
    c = np.zeros((P, width), np.float32)

    def put(name, a):
        lo = where[name][0]
        c[:a.shape[0], lo:lo + a.shape[1]] = a
    p = np.arange(P)[:, None]
    j = np.arange(P)[None, :]
    put("ident", (p == j).astype(np.float32))
    put("tri", (p >= j).astype(np.float32))
    put("heads", (p // RN == j // RN).astype(np.float32))
    past = np.where(p < j, 0.0, NEG).astype(np.float32)
    put("past", np.concatenate([past, np.zeros((P, P), np.float32), past], 1))
    seen = np.where(j <= p, 0.0, NEG).astype(np.float32)
    put("seen", np.concatenate([seen, np.zeros((P, P), np.float32), seen], 1))
    invf, sign = np.zeros((P, 2), np.float32), np.zeros((P, 2), np.float32)
    for n, d in enumerate((HD, IDX_D)):
        f = (np.float32(1.0) / (np.float32(10000.0) ** (np.arange(0, d, 2, dtype=np.float32) / np.float32(d)))).astype(np.float32)
        at = np.arange(P) % d
        invf[:, n] = f[at % (d // 2)]
        sign[:, n] = np.where(at < d // 2, 1.0, -1.0)
    put("invf", invf)
    put("sign", sign)
    s, t = np.arange(L)[:, None], np.arange(L)[None, :]
    put("strict", (s < t).astype(np.float32))
    put("incl", (s <= t).astype(np.float32))

    def level(b):
        return ((s // (2 * b) == t // (2 * b)) & (s % (2 * b) < b) & (t % (2 * b) >= b)).astype(np.float32)
    put("first", level(1))
    for b in LEVELS:
        put(f"level{b}", level(b))
    return c


def by_feature(a):
    return np.ascontiguousarray(a.reshape(-1, P).T)


def tokens_by_feature(a):
    return np.ascontiguousarray(a.T.reshape(-1, P, a.shape[0]).transpose(1, 0, 2))


def kernel(**inputs):
    import concourse.bacc as bacc
    from concourse.bass_utils import run_bass_kernel_spmd

    x = {k: np.asarray(v) for k, v in inputs.items()}
    mu = x["mu_rwkv_2"]

    def lora_column(a):
        return np.concatenate([a, np.zeros(P - LORA, a.dtype)]).reshape(P, 1)
    pieces = {
        "c": by_feature(x["c"]), "b_ada": by_feature(x["b_ada"]), "g_mix": by_feature(x["g_mix"]),
        "g_ffn": by_feature(x["g_ffn"]), "g_final": by_feature(x["g_final"]), "conv_w": by_feature(x["conv_w"]),
        "conv_b": by_feature(x["conv_b"]), "g_pre_mix": by_feature(x["g_pre_mix_2"]), "g_post_mix": by_feature(x["g_post_mix_2"]),
        "g_pre_ffn": by_feature(x["g_pre_ffn_2"]), "g_post_ffn": by_feature(x["g_post_ffn_2"]),
        "conv_w2": by_feature(x["conv_w_2"]), "mu_rkv": by_feature(mu[:3 * W]), "mu_gd": by_feature(mu[3 * W + 2 * LORA:]),
        "mu_wd": lora_column(mu[3 * W:3 * W + LORA]), "mu_ad": lora_column(mu[3 * W + LORA:3 * W + 2 * LORA]),
        "w0": by_feature(x["w0_2"]), "a0": by_feature(x["a0_2"]), "k_k": by_feature(x["k_k_2"]), "k_a": by_feature(x["k_a_2"]),
        "r_k": by_feature(x["r_k_2"]), "ln_w": by_feature(x["ln_x_w_2"]), "ln_b": by_feature(x["ln_x_b_2"]),
        "conv_ffn": by_feature(x["conv_ffn_2"]),
    }
    arrays = {
        "params": np.ascontiguousarray(np.concatenate([pieces[n] for n, _ in PARAMS], axis=1)),
        "consts": constant_block(),
        "pos": np.ascontiguousarray(np.broadcast_to(x["positions"].reshape(1, T), (P, T))),
        "xT": tokens_by_feature(x["x"][0]), "metaT": tokens_by_feature(x["meta_tokens_2"]),
    }
    for name in ("w_in", "w_a", "w_b", "w_o", "w_ada", "w_up", "w_down"):
        arrays[name] = np.ascontiguousarray(x[name][0])
    for name in ("w_in_2", "w_decay_up_2", "a_up_2", "g_up_2", "w_out_2", "w_gate_up_2", "w_down_2"):
        arrays[name] = np.ascontiguousarray(x[name])
    nc = bacc.Bacc("TRN2", target_bir_lowering=False, num_devices=1)
    aps = {n: nc.dram_tensor(f"{n}_dram", a.shape, mybir.dt.from_np(a.dtype), kind="ExternalInput").ap() for n, a in arrays.items()}
    out = nc.dram_tensor("out_dram", (P, KD, T), F32, kind="ExternalOutput").ap()
    build(nc, aps, out)
    got = run_bass_kernel_spmd(nc, [{f"{n}_dram": a for n, a in arrays.items()}], core_ids=[0]).results[0]["out_dram"]
    return np.ascontiguousarray(got.transpose(2, 1, 0)).reshape(1, T, D)
```
